# Optimizing a Trainium2 kernel written in Bass

```python
import jax
import jax.numpy as jnp
from jax import lax
import numpy as np

D_MODEL = 1024
BATCH = 1
SEQ = 512
DEPTH = 1
DEC_BATCH = 8
DEC_SEQ = 4
PAST_LEN = 2048
PAGE_SIZE = 128

HEAD_DIM = 64
ATTN_WIDTH = D_MODEL // 2
N_HEADS = ATTN_WIDTH // HEAD_DIM
CONV_WIDTH = D_MODEL - ATTN_WIDTH
CONV_K = 3
MIX_WIDTH = ATTN_WIDTH + CONV_WIDTH
IN_COLS = 3 * ATTN_WIDTH + 3 * CONV_WIDTH
BRANCHES = ((128, 1), (512, 4), (2048, 16))
W_MAX = 2048
Q_BLOCK = 128
ROPE_THETA = 10000.0
N_EXPERTS = 64
TOP_K = 8
N_GROUPS = 8
TOPK_GROUPS = 4
D_EXPERT = D_MODEL // 4
D_SHARED = D_EXPERT
ROUTED_SCALE = 2.5
MOE_BLOCK = 128
EPS = 1e-6

kernel_name = 'hymba_dilated_conv_moe_step'

def rms_norm(x, gain=None):
    xf = x.astype(jnp.float32)
    y = xf * lax.rsqrt(jnp.mean(xf * xf, axis=-1, keepdims=True) + EPS)
    if gain is not None:
        y = y * gain.astype(jnp.float32)
    return y.astype(x.dtype)

def rotary(x, pos):
    half = HEAD_DIM // 2
    inv_freq = ROPE_THETA ** (-jnp.arange(half, dtype=jnp.float32) / half)
    ang = pos.astype(jnp.float32)[:, None] * inv_freq[None, :]
    cos = jnp.cos(ang)[None, :, None, :]
    sin = jnp.sin(ang)[None, :, None, :]
    xf = x.astype(jnp.float32)
    x1, x2 = xf[..., :half], xf[..., half:]
    return jnp.concatenate([x1 * cos - x2 * sin, x2 * cos + x1 * sin], axis=-1).astype(x.dtype)

def _dilated_attention_seq(q, k_ext, v_ext, pos0):
    t = q.shape[0]
    qb = Q_BLOCK if t % Q_BLOCK == 0 else t
    n_blocks = t // qb
    scale = HEAD_DIM ** -0.5
    offsets = [jnp.arange(qb)[:, None] - d * jnp.arange(w // d + 1)[None, :] for (w, d) in BRANCHES]

    def one_block(blk):
        start = blk * qb
        q_blk = lax.dynamic_slice_in_dim(q, start, qb, axis=0)
        outs, lses = [], []
        for off in offsets:
            rows = W_MAX + start + off
            k_g = k_ext[rows]
            v_g = v_ext[rows]
            s = jnp.einsum('qhd,qjhd->hqj', q_blk, k_g, preferred_element_type=jnp.float32) * scale
            s = jnp.where((pos0 + rows >= 0)[None], s, -jnp.inf)
            m = jnp.max(s, axis=-1, keepdims=True)
            p = jnp.exp(s - m)
            den = jnp.sum(p, axis=-1)
            o = jnp.einsum('hqj,qjhd->qhd', p, v_g.astype(jnp.float32)) / jnp.transpose(den)[..., None]
            outs.append(o)
            lses.append(m[..., 0] + jnp.log(den))
        alpha = jax.nn.softmax(jnp.stack(lses), axis=0)
        alpha = jnp.transpose(alpha, (0, 2, 1))[..., None]
        out = alpha[0] * outs[0]
        for i in range(1, len(outs)):
            out = out + alpha[i] * outs[i]
        return out.astype(q.dtype)

    out = lax.map(one_block, jnp.arange(n_blocks))
    return out.reshape(t, N_HEADS, HEAD_DIM)

def dilated_attention(q, k_ext, v_ext, pos0):
    return lax.map(lambda a: _dilated_attention_seq(a[0], a[1], a[2], pos0), (q, k_ext, v_ext))

def moe_ffn(h, w_router, router_bias, w_exp_gate, w_exp_up, w_exp_down, w_sh_gate, w_sh_up, w_sh_down):
    n, d = h.shape
    scores = jax.nn.sigmoid(jnp.einsum('nd,de->ne', h, w_router, preferred_element_type=jnp.float32))
    sel = scores + router_bias.astype(jnp.float32)
    grp = jnp.sum(lax.top_k(sel.reshape(n, N_GROUPS, N_EXPERTS // N_GROUPS), 2)[0], axis=-1)
    _, gidx = lax.top_k(grp, TOPK_GROUPS)
    gmask = jnp.any(gidx[:, :, None] == jnp.arange(N_GROUPS)[None, None, :], axis=1)
    sel = jnp.where(jnp.repeat(gmask, N_EXPERTS // N_GROUPS, axis=1), sel, -jnp.inf)
    _, eidx = lax.top_k(sel, TOP_K)
    gate = jnp.take_along_axis(scores, eidx, axis=1)
    gate = gate / jnp.sum(gate, axis=-1, keepdims=True) * ROUTED_SCALE

    a = n * TOP_K
    e_flat = eidx.reshape(a)
    t_flat = jnp.repeat(jnp.arange(n, dtype=jnp.int32), TOP_K)
    g_flat = gate.reshape(a)
    order = jnp.argsort(e_flat)
    e_s, t_s, g_s = e_flat[order], t_flat[order], g_flat[order]
    sizes = jnp.bincount(e_flat, length=N_EXPERTS)
    padded = (sizes + MOE_BLOCK - 1) // MOE_BLOCK * MOE_BLOCK
    pad_end = jnp.cumsum(padded)
    pad_start = pad_end - padded
    grp_start = jnp.cumsum(sizes) - sizes
    dest = pad_start[e_s] + jnp.arange(a) - grp_start[e_s]
    n_blk = -(-(a + N_EXPERTS * (MOE_BLOCK - 1)) // MOE_BLOCK)
    m_rows = n_blk * MOE_BLOCK
    tok = jnp.zeros((m_rows,), jnp.int32).at[dest].set(t_s)
    gw = jnp.zeros((m_rows,), jnp.float32).at[dest].set(g_s)
    blk_e = jnp.minimum(jnp.searchsorted(pad_end, jnp.arange(n_blk) * MOE_BLOCK, side='right'), N_EXPERTS - 1)

    def expert_block(args):
        tb, gb, e = args
        xb = h[tb]
        hid = jax.nn.silu(xb @ w_exp_gate[e]) * (xb @ w_exp_up[e])
        return (hid @ w_exp_down[e]) * gb[:, None].astype(h.dtype)

    outs = lax.map(expert_block, (tok.reshape(n_blk, MOE_BLOCK), gw.reshape(n_blk, MOE_BLOCK), blk_e))
    routed = jnp.zeros_like(h).at[tok].add(outs.reshape(m_rows, d))
    shared = (jax.nn.silu(h @ w_sh_gate) * (h @ w_sh_up)) @ w_sh_down
    return routed + shared

def hybrid_layer(x, c, k_past, v_past, conv_past, start_pos, w_ada, b_ada, w_in, conv_w,
                 g_attn_out, g_conv_out, w_out, w_router, router_bias, w_exp_gate, w_exp_up,
                 w_exp_down, w_sh_gate, w_sh_up, w_sh_down):
    b, t, d = x.shape
    mod = (jax.nn.silu(c) @ w_ada + b_ada).reshape(b, 6, d)
    sh1, sc1, g1 = mod[:, 0, None, :], mod[:, 1, None, :], mod[:, 2, None, :]
    sh2, sc2, g2 = mod[:, 3, None, :], mod[:, 4, None, :], mod[:, 5, None, :]

    hmix = rms_norm(x) * (1.0 + sc1) + sh1
    proj = hmix @ w_in
    cuts = np.cumsum([ATTN_WIDTH] * 3 + [CONV_WIDTH] * 2).tolist()
    q, k, v, hc, gb, gc = jnp.split(proj, cuts, axis=-1)

    pos = start_pos + jnp.arange(t)
    q = rotary(q.reshape(b, t, N_HEADS, HEAD_DIM), pos)
    k = rotary(k.reshape(b, t, N_HEADS, HEAD_DIM), pos)
    v = v.reshape(b, t, N_HEADS, HEAD_DIM)
    pad = jnp.zeros((b, W_MAX - k_past.shape[1], N_HEADS, HEAD_DIM), x.dtype)
    k_ext = jnp.concatenate([pad, k_past.astype(x.dtype), k], axis=1)
    v_ext = jnp.concatenate([pad, v_past.astype(x.dtype), v], axis=1)
    attn = dilated_attention(q, k_ext, v_ext, start_pos - W_MAX).reshape(b, t, ATTN_WIDTH)

    u = gc * hc
    u_ext = jnp.concatenate([conv_past.astype(x.dtype), u], axis=1)
    conv = u_ext[:, 0:t] * conv_w[0]
    for i in range(1, CONV_K):
        conv = conv + u_ext[:, i:i + t] * conv_w[i]
    yconv = gb * conv

    mix = jnp.concatenate([rms_norm(attn, g_attn_out), rms_norm(yconv, g_conv_out)], axis=-1) @ w_out
    x = x + g1 * mix

    hff = rms_norm(x) * (1.0 + sc2) + sh2
    ff = moe_ffn(hff.reshape(b * t, d), w_router, router_bias, w_exp_gate, w_exp_up, w_exp_down,
                 w_sh_gate, w_sh_up, w_sh_down).reshape(b, t, d)
    x = x + g2 * ff
    return x, k, v, u_ext[:, -(CONV_K - 1):]

def setup_inputs(seed: int = 0) -> dict:
    key = jax.random.key(seed)
    ks = jax.random.split(key, 24)

    def nrm(k, shape, scale):
        return jax.random.normal(k, shape, jnp.float32) * scale

    d = D_MODEL
    buf = min(W_MAX, PAST_LEN)
    return {
        'x_prompt': nrm(ks[0], (BATCH, SEQ, d), 1.0),
        'x_sample': nrm(ks[1], (DEC_BATCH, DEC_SEQ, d), 1.0),
        'c_prompt': nrm(ks[2], (BATCH, d), 1.0),
        'c_sample': nrm(ks[3], (DEC_BATCH, d), 1.0),
        'cache_k': nrm(ks[4], (DEPTH, DEC_BATCH, buf, N_HEADS, HEAD_DIM), 1.0),
        'cache_v': nrm(ks[5], (DEPTH, DEC_BATCH, buf, N_HEADS, HEAD_DIM), 1.0),
        'state_conv': nrm(ks[6], (DEPTH, DEC_BATCH, CONV_K - 1, CONV_WIDTH), 1.0),
        'w_ada': nrm(ks[7], (DEPTH, d, 6 * d), 0.5 * d ** -0.5),
        'b_ada': nrm(ks[8], (DEPTH, 6 * d), 0.02),
        'w_in': nrm(ks[9], (DEPTH, d, IN_COLS), d ** -0.5),
        'conv_w': nrm(ks[10], (DEPTH, CONV_K, CONV_WIDTH), CONV_K ** -0.5),
        'g_attn_out': 1.0 + nrm(ks[11], (DEPTH, ATTN_WIDTH), 0.02),
        'g_conv_out': 1.0 + nrm(ks[12], (DEPTH, CONV_WIDTH), 0.02),
        'w_out': nrm(ks[13], (DEPTH, MIX_WIDTH, d), MIX_WIDTH ** -0.5),
        'w_router': nrm(ks[14], (DEPTH, d, N_EXPERTS), d ** -0.5),
        'router_bias': nrm(ks[15], (DEPTH, N_EXPERTS), 0.01),
        'w_exp_gate': nrm(ks[16], (DEPTH, N_EXPERTS, d, D_EXPERT), d ** -0.5),
        'w_exp_up': nrm(ks[17], (DEPTH, N_EXPERTS, d, D_EXPERT), d ** -0.5),
        'w_exp_down': nrm(ks[18], (DEPTH, N_EXPERTS, D_EXPERT, d), D_EXPERT ** -0.5),
        'w_sh_gate': nrm(ks[19], (DEPTH, d, D_SHARED), d ** -0.5),
        'w_sh_up': nrm(ks[20], (DEPTH, d, D_SHARED), d ** -0.5),
        'w_sh_down': nrm(ks[21], (DEPTH, D_SHARED, d), D_SHARED ** -0.5),
        'g_final': 1.0 + nrm(ks[22], (d,), 0.02),
    }

def reference(x_prompt, x_sample, c_prompt, c_sample, cache_k, cache_v, state_conv, w_ada, b_ada,
              w_in, conv_w, g_attn_out, g_conv_out, w_out, w_router, router_bias, w_exp_gate,
              w_exp_up, w_exp_down, w_sh_gate, w_sh_up, w_sh_down, g_final):
    bp, s, _ = x_prompt.shape
    bs = x_sample.shape[0]
    keep_p = min(W_MAX, s)
    xp, xs = x_prompt, x_sample
    kp_l, vp_l, cp_l, ks_l, vs_l, cs_l = [], [], [], [], [], []
    for l in range(DEPTH):
        empty_kv = jnp.zeros((bp, 0, N_HEADS, HEAD_DIM), x_prompt.dtype)
        zero_conv = jnp.zeros((bp, CONV_K - 1, CONV_WIDTH), x_prompt.dtype)
        xp, kp, vp, cp = hybrid_layer(
            xp, c_prompt, empty_kv, empty_kv, zero_conv, 0,
            w_ada[l], b_ada[l], w_in[l], conv_w[l], g_attn_out[l], g_conv_out[l], w_out[l],
            w_router[l], router_bias[l], w_exp_gate[l], w_exp_up[l], w_exp_down[l],
            w_sh_gate[l], w_sh_up[l], w_sh_down[l])
        xs, ksn, vsn, csn = hybrid_layer(
            xs, c_sample, cache_k[l], cache_v[l], state_conv[l], PAST_LEN,
            w_ada[l], b_ada[l], w_in[l], conv_w[l], g_attn_out[l], g_conv_out[l], w_out[l],
            w_router[l], router_bias[l], w_exp_gate[l], w_exp_up[l], w_exp_down[l],
            w_sh_gate[l], w_sh_up[l], w_sh_down[l])
        kp_l.append(kp[:, s - keep_p:])
        vp_l.append(vp[:, s - keep_p:])
        cp_l.append(cp)
        ks_l.append(ksn)
        vs_l.append(vsn)
        cs_l.append(csn)
    y_prompt = rms_norm(xp, g_final)
    y_sample = rms_norm(xs, g_final)
    return (y_prompt, y_sample, jnp.stack(kp_l), jnp.stack(vp_l), jnp.stack(cp_l),
            jnp.stack(ks_l), jnp.stack(vs_l), jnp.stack(cs_l))


_drawn_inputs = setup_inputs


def setup_inputs(seed=0):
    import zlib

    import numpy as np

    out = dict(_drawn_inputs(seed))
    spreads = {}
    factors = {'g_attn_out': 3.823, 'g_conv_out': 4.006, 'g_final': 2.812}
    for name, (base, spread) in spreads.items():
        noise = np.random.default_rng([zlib.crc32(name.encode()), seed]).standard_normal(out[name].shape)
        drawn = base * np.exp(spread * noise) if base else spread * noise
        out[name] = jnp.asarray(drawn.astype(out[name].dtype))
    for name, factor in factors.items():
        out[name] = (out[name] * factor).astype(out[name].dtype)
    return out
```

```python
import numpy as np
from contextlib import ExitStack

import concourse.bass as bass
from concourse import mybir

F32 = mybir.dt.float32
BF16 = mybir.dt.bfloat16
I32 = mybir.dt.int32
U32 = mybir.dt.uint32
ALU = mybir.AluOpType
ACT = mybir.ActivationFunctionType
AX = mybir.AxisListType

P = 128
D = 1024
KC = D // P
SEQ, DEC_B, DEC_T = 512, 8, 4
NS = DEC_B * DEC_T
NTOK = SEQ + NS
NPT = SEQ // P
NT = NPT + 1
HEADS, HD = 8, 64
W = HEADS * HD
WC = W // P
PAST, WIN = 2048, 512
WIN0 = PAST - WIN
SPARSE = WIN0 // 16
SK = WIN + 4 * SPARSE + NS
NE, TOPK, NGRP, GSZ = 64, 8, 8, 8
FE = 256
EPS = 1e-6
NADA, NIN = 12, 6
MAXB = (NTOK * TOPK + NE * (P - 1)) // P
TRIPS = -(-MAXB // 3)
OUTSIDE = 8192
BRANCHES = ((128, 1), (512, 4), (2048, 16))

C_ID, C_IOTA, C_BASE, C_TRI, C_ONE = 0, 128, 256, 384, 512
C_LOW, C_VALID, C_IP, C_TRIP, C_LP = 640, 704, 709, 710, 743
C_POW = C_LP + NT * 5
C_END = C_POW + 1
A_PM, A_PN = 0, 512
A_SM = 1024
A_SN = A_SM + 2 * SK
A_BD = A_SN + 2 * SK
A_SEL = A_BD + W
A_END = A_SEL + 2 * NS


def rows(t):
    return P if t < NPT else NS


def branch_count(dist):
    n = np.zeros(dist.shape, np.float32)
    for w, d in BRANCHES:
        n += (dist >= 0) & (dist <= w) & (dist % d == 0)
    return n


def constants():
    p = np.arange(P)
    c = np.zeros((P, C_END), np.float32)
    c[:, C_ID:C_ID + P] = np.eye(P)
    c[:, C_IOTA:C_IOTA + P] = p[None]
    c[:, C_BASE:C_BASE + P] = P * p[None]
    c[:, C_TRI:C_TRI + P] = p[:, None] < p[None]
    c[:, C_ONE:C_ONE + P] = 1
    g = np.arange(NGRP)
    c[:, C_LOW:C_LOW + 64] = (g[None] < g[:, None]).ravel()[None]
    for t in range(NT):
        c[:, C_VALID + t] = p < rows(t)
        c[:, C_LP + 5 * t + 0] = p
        c[:, C_LP + 5 * t + 1] = P * t - OUTSIDE
        c[:, C_LP + 5 * t + 3] = TOPK * p
        c[:, C_LP + 5 * t + 4] = TOPK * (P * t - OUTSIDE)
    c[:, C_POW] = -0.5
    c[:, C_IP] = p
    c[:, C_TRIP:C_TRIP + TRIPS] = 3 * np.arange(TRIPS)[None]

    a = np.zeros((P, A_END), np.float32)
    for n, diff in enumerate(range(NPT - 1, -1, -1)):
        m = branch_count(P * diff + p[:, None] - p[None])
        a[:, A_PM + n * P:A_PM + (n + 1) * P] = m
    a[:, A_PN:A_PN + 512] = np.where(a[:, A_PM:A_PM + 512] > 0, 0, -1e30)
    pos = np.concatenate([(WIN0 + 4 * p[None] + np.arange(4)[:, None]).ravel(),
                          (16 * np.arange(SPARSE)[None] + np.arange(4)[:, None]).ravel()])
    q = p % DEC_T
    for grp in range(2):
        m = np.zeros((P, SK), np.float32)
        m[:, :len(pos)] = branch_count(PAST + q[:, None] - pos[None])
        batch = 4 * grp + p // 32
        kb, kt = np.arange(NS) // DEC_T, np.arange(NS) % DEC_T
        m[:, len(pos):] = branch_count(q[:, None] - kt[None]) * (kb[None] == batch[:, None])
        a[:, A_SM + grp * SK:A_SM + (grp + 1) * SK] = m
        a[:, A_SN + grp * SK:A_SN + (grp + 1) * SK] = np.where(m > 0, 0, -1e30)
        a[:, A_SEL + grp * NS:A_SEL + (grp + 1) * NS] = (batch * DEC_T + q)[:, None] == np.arange(NS)[None]
    a[:, A_BD:A_BD + W] = (np.arange(W)[None] // HD) == ((p % 32) // DEC_T)[:, None]

    half = HD // 2
    inv = (np.float32(10000.0) ** (-np.arange(half, dtype=np.float32) / np.float32(half))).astype(np.float32)
    where = np.zeros((NT, P), np.float32)
    where[:NPT] = np.arange(SEQ).reshape(NPT, P)
    where[NPT, :NS] = PAST + np.arange(NS) % DEC_T
    ang = (where[:, :, None] * inv[None, None]).astype(np.float32)
    cos, sin = np.cos(ang).astype(np.float32), np.sin(ang).astype(np.float32)
    r = np.concatenate([np.concatenate([cos, cos], -1), np.concatenate([-sin, sin], -1)], 0)
    r = np.ascontiguousarray(r.transpose(1, 0, 2).reshape(P, 2 * NT * HD))
    return c, a, r


def layer(nc, io):
    ctx = ExitStack()

    def sem(name):
        return ctx.enter_context(nc.semaphore(name))

    def keep(name, shape, dt=F32):
        return ctx.enter_context(nc.sbuf_tensor("sb_" + name, shape, dt))

    psum = ctx.enter_context(nc.psum_tensor("psum", [P, 8, 512], F32))

    mod_rows = nc.dram_tensor("mod_rows", (1 + DEC_B, 6 * D), F32, kind="Internal").ap()
    h_rows = nc.dram_tensor("h_rows", (NTOK, D), F32, kind="Internal").ap()
    expert_rows = nc.dram_tensor("expert_rows", (NTOK * TOPK, D), F32, kind="Internal").ap()

    cst = keep("cst", [P, C_END])
    stream = keep("stream", [P, 96 * 256])
    convg = keep("convg", [P, WC, NTOK])
    conv_r = keep("conv_r", [P, NT])
    attn = keep("attn", [P, NT, W])
    gains = keep("gains", [P, 2, WC])
    ident = cst[:, C_ID:C_ID + P]

    stored = sem("stored")
    n_stores = [0]

    def store(eng, dst, src):
        n_stores[0] += 1
        return eng.dma_start(dst, src).then_inc(stored, 16)

    def bc_row(ap_row, n):
        return ap_row.broadcast_to([n, ap_row.shape[1]])

    def mod_sample(j):
        return mod_rows[1:1 + DEC_B, j * D:(j + 1) * D].unsqueeze(1).broadcast_to([DEC_B, DEC_T, D])

    def stage_1():
        st = ExitStack()

        def tmp(name, shape, dt=F32):
            return st.enter_context(nc.sbuf_tensor("sb_" + name, shape, dt))

        k_sb, v_sb = keeps["k"], keeps["v"]
        q_sb = attn
        xh = tmp("xh", [P, NT, D])
        hT = tmp("hT", [P, KC, NTOK])
        bc_shift = tmp("bc_shift", [P, 2, D])
        bc_scale = tmp("bc_scale", [P, 2, D])
        up = tmp("up", [P, WC, 2 + SEQ])
        us = tmp("us", [P, WC, DEC_B, 2 + DEC_T])
        rope = tmp("rope", [P, 2, NT, HD])
        rot = tmp("rot", [P, 2, W])
        c_sb = hT[0:1 + DEC_B, :, :].rearrange("p k n -> p (k n)")[:, 0:3 * D].rearrange("p (a n) -> p a n", a=3)
        cT = tmp("cT", [P, KC, 1 + DEC_B])
        convw = tmp("convw", [P, 3, WC])
        rest = 4 * 4096 + 6 * D
        state = stream[0:2 * DEC_B, rest:rest + W]
        ss = tmp("ss", [P, 2, NT])
        cs = tmp("cs", [P, NT])
        tail = tmp("tail", [P, WC, 2 + 2 * DEC_B])
        tail_rows = stream[0:2 + 2 * DEC_B, rest + W:rest + 2 * W]
        ring = stream[:, 0:4 * 4096].rearrange("p (s k n) -> p s k n", s=4, k=KC)
        mod = stream[0:1 + DEC_B, 4 * 4096:4 * 4096 + 6 * D]
        flat = xh[:, :, :].rearrange("p t n -> p (t n)")
        hcT = flat[:, 0:WC * NTOK].rearrange("p (c n) -> p c n", c=WC)
        convT = flat[:, WC * NTOK:2 * WC * NTOK].rearrange("p (c n) -> p c n", c=WC)

        w_in = [sem(f"s1_w{i}") for i in range(4)]
        w_used = sem("s1_w_used")
        cst_in, c_in, bias_in, x_in, small_in = (sem(f"s1_{n}") for n in
                                                 ("cst_in", "c_in", "bias_in", "x_in", "small_in"))
        c_exp, c_silu, cT_ps, cT_ok = (sem(f"s1_{n}") for n in ("c_exp", "c_silu", "cT_ps", "cT_ok"))
        mod_ok, mod_out, bc_in = (sem(f"s1_{n}") for n in ("mod_ok", "mod_out", "bc_in"))
        h_ok, hT_ps, hT_a, hT_v = (sem(f"s1_{n}") for n in ("h_ok", "hT_ps", "hT_a", "hT_v"))
        proj, qk_ok, v_ok = (sem(f"s1_{n}") for n in ("proj", "qk_ok", "v_ok"))
        cmm, hc_ok, gcb_ok = (sem(f"s1_{n}") for n in ("cmm", "hc_ok", "gcb_ok"))
        st_ps, st_ok, pads = (sem(f"s1_{n}") for n in ("st_ps", "st_ok", "pads"))
        sq_ok, ssq_ps, tail_ok, tail_ps, tail_sb = (sem(f"s1_{n}") for n in
                                                    ("sq_ok", "ssq_ps", "tail_ok", "tail_ps", "tail_sb"))
        ms_ok, cms_ok, rs_ok = (sem(f"s1_{n}") for n in ("ms_ok", "cms_ok", "rs_ok"))
        v_step = sem("s1_v_step")

        order = [0, 1, 2, 3, 5, 4]

        with nc.Block() as block:
            @block.sync
            def _(sp):
                for n in range(NADA + NIN):
                    if n >= 4:
                        if n - 4 < NADA:
                            sp.wait_ge(w_used, n - 3)
                        else:
                            sp.wait_ge(proj, NT * (n - 3 - NADA))
                    src = (io["w_ada"][0][:, n * 512:(n + 1) * 512] if n < NADA else
                           io["w_in"][0][:, order[n - NADA] * W:(order[n - NADA] + 1) * W])
                    sp.dma_start(ring[:, n % 4], src.rearrange("(k p) n -> p k n", p=P)).then_inc(w_in[n % 4], 16)
                sp.wait_ge(qk_ok, 2 * NT)
                sp.wait_ge(v_ok, NT)
                for name, src in (("k", k_sb), ("v", v_sb)):
                    store(sp, io[name + "_prompt"].rearrange("a b (t p) h d -> p (a b t) (h d)", p=P), src[:, 0:NPT, :])
                    store(sp, io[name + "_sample"].rearrange("a b t h d -> (a b t) (h d)"), src[0:NS, NPT, :])
                sp.wait_ge(tail_sb, 1)
                store(sp, io["conv_prompt"].rearrange("a b t n -> (a b t) n"), tail_rows[0:2, :])
                store(sp, io["conv_sample"].rearrange("a b t n -> (a b t) n"), tail_rows[2:, :])

            @block.gpsimd
            def _(pool):
                pool.memset(v_sb[:, NPT, :], 0.0).then_inc(pads, 1)
                pool.memset(up[:, :, 0:2], 0.0).then_inc(pads, 1)
                pool.dma_start(rope[:, :, :, :], io["rope"].rearrange("p (a t n) -> p a t n", a=2, t=NT)).then_inc(small_in, 16)
                pool.dma_start(state[:, :], io["state_conv"].rearrange("a b t n -> (a b t) n")).then_inc(small_in, 16)
                for j in range(3):
                    pool.dma_start(convw[:, j, :], io["conv_w"][0, j].rearrange("(c p) -> p c", p=P),
                                   allow_slow_non_contiguous=True).then_inc(small_in, 16)
                for j, g in enumerate(("g_attn_out", "g_conv_out")):
                    pool.dma_start(gains[:, j, :], io[g][0].rearrange("(c p) -> p c", p=P),
                                   allow_slow_non_contiguous=True).then_inc(small_in, 16)
                for ready, dst, src in ((ms_ok, ss[:, 0], ss[:, 1]), (cms_ok, conv_r, cs)):
                    pool.wait_ge(ready, 1)
                    for r, a, b in ((P, 0, NPT), (NS, NPT, NT)):
                        pool.tensor_tensor(dst[0:r, a:b], src[0:r, a:b], cst[0:r, C_POW:C_POW + 1].broadcast_to([r, b - a]), ALU.pow).then_inc(rs_ok, 1)
                pool.wait_ge(rs_ok, 4)

            @block.scalar
            def _(act):
                act.dma_start(c_sb[0:1, 0, :], io["c_prompt"]).then_inc(c_in, 16)
                act.dma_start(c_sb[1:, 0, :], io["c_sample"]).then_inc(c_in, 16)
                act.dma_start(cst[:, :], io["cst"]).then_inc(cst_in, 16)
                act.dma_start(xh[:, 0:NPT, :], io["x_prompt"][0].rearrange("(t p) n -> p t n", p=P)).then_inc(x_in, 16)
                act.dma_start(xh[0:NS, NPT, :], io["x_sample"].rearrange("b t n -> (b t) n")).then_inc(x_in, 16)
                act.dma_start(mod, bc_row(io["b_ada"], 1 + DEC_B)).then_inc(bias_in, 16)
                act.wait_ge(c_in, 32)
                act.activation(c_sb[:, 1, :], c_sb[:, 0, :], ACT.Exp, scale=-1.0).then_inc(c_exp, 1)
                for n in range(NADA):
                    act.wait_ge(mod_ok, n + 1)
                    act.dma_start(mod_rows[:, n * 512:(n + 1) * 512], mod[:, n * 512:(n + 1) * 512]).then_inc(mod_out, 16)
                    if n == 3:
                        act.wait_ge(mod_out, 64)
                        for j, dst in ((0, bc_shift), (1, bc_scale)):
                            act.dma_start(dst[:, 0, :], bc_row(mod_rows[0:1, j * D:(j + 1) * D], P)).then_inc(bc_in, 16)
                            act.dma_start(dst[0:NS, 1, :], mod_sample(j)).then_inc(bc_in, 16)
                for t in range(NT):
                    act.wait_ge(hT_ps, 2 * t + 1)
                    act.copy(hT[:, 0:4, t * P:t * P + rows(t)],
                             psum[:, 3 + (2 * t) % 4, :].rearrange("p (k n) -> p k n", k=4)[:, :, 0:rows(t)]).then_inc(hT_a, 1)
                act.wait_ge(pads, 1)
                for t in range(NT):
                    act.wait_ge(proj, 2 * NT + t + 1)
                    act.copy(v_sb[0:rows(t), t, :], psum[0:rows(t), (2 * NT + t) % 3, :]).then_inc(v_ok, 1)
                for m in range(WC):
                    act.wait_ge(cmm, m + 1)
                    act.copy(hcT[:, m, 0:SEQ], psum[:, 3 + m % 2, :])
                    act.copy(hcT[:, m, SEQ:], psum[:, 5 + m % 2, 0:NS]).then_inc(hc_ok, 1)
                act.wait_ge(small_in, 7 * 16)
                for m in range(WC):
                    act.wait_ge(gcb_ok, WC + m + 1)
                    act.activation(hcT[:, m, :], convT[:, m, :], ACT.Square).then_inc(sq_ok, 1)
                    act.activation(convg[:, m, :], convT[:, m, :], ACT.Copy, scale=gains[:, 1, m:m + 1]).then_inc(sq_ok, 1)
                act.wait_ge(mod_out, NADA * 16)

            @block.vector
            def _(v):
                n_step = [0]

                def step(ins):
                    n_step[0] += 1
                    ins.then_inc(v_step, 1)

                def settle():
                    v.wait_ge(v_step, n_step[0])

                v.wait_ge(c_exp, 1)
                step(v.tensor_scalar(c_sb[:, 2, :], c_sb[:, 1, :], 1.0, None, ALU.add))
                settle()
                step(v.reciprocal(c_sb[:, 1, :], c_sb[:, 2, :]))
                settle()
                v.tensor_tensor(c_sb[:, 2, :], c_sb[:, 1, :], c_sb[:, 0, :], ALU.mult).then_inc(c_silu, 1)
                v.wait_ge(x_in, 32)
                for t in range(NT):
                    r = rows(t)
                    settle()
                    step(v.tensor_tensor_reduce(rot[0:r, :, :].rearrange("p a n -> p (a n)"), xh[0:r, t, :], xh[0:r, t, :],
                                                1.0, 0.0, ALU.mult, ALU.add, ss[0:r, 0, t:t + 1]))
                v.wait_ge(cT_ps, 1)
                v.tensor_copy(cT[:, :, :], psum[:, 0, 0:KC * 9].rearrange("p (k n) -> p k n", k=KC)).then_inc(cT_ok, 1)
                settle()
                for r, a, b in ((P, 0, NPT), (NS, NPT, NT)):
                    step(v.tensor_scalar(ss[0:r, 1, a:b], ss[0:r, 0, a:b], 1.0 / D, EPS, ALU.mult, ALU.add))
                settle()
                v.sem_inc(ms_ok, 1)
                v.wait_ge(bias_in, 16)
                for n in range(NADA):
                    v.wait_ge(w_used, n + 1)
                    v.tensor_tensor(mod[:, n * 512:(n + 1) * 512], psum[0:9, 1 + n % 2, :],
                                    mod[:, n * 512:(n + 1) * 512], ALU.add).then_inc(mod_ok, 1)
                    if n == 4:
                        v.wait_ge(rs_ok, 2)
                        v.wait_ge(bc_in, 64)
                        step(v.tensor_scalar(bc_scale[:, 0, :], bc_scale[:, 0, :], 1.0, None, ALU.add))
                        step(v.tensor_scalar(bc_scale[0:NS, 1, :], bc_scale[0:NS, 1, :], 1.0, None, ALU.add))
                    if 5 <= n < 5 + NT:
                        t = n - 5
                        r, s = rows(t), t // NPT
                        settle()
                        step(v.scalar_tensor_tensor(xh[0:r, t, :], xh[0:r, t, :], ss[0:r, 0, t:t + 1],
                                                    bc_scale[0:r, s, :], ALU.mult, ALU.mult))
                        settle()
                        v.tensor_tensor(xh[0:r, t, :], xh[0:r, t, :], bc_shift[0:r, s, :], ALU.add).then_inc(h_ok, 1)
                for t in range(NT):
                    v.wait_ge(hT_ps, 2 * t + 2)
                    v.tensor_copy(hT[:, 4:8, t * P:t * P + rows(t)],
                                  psum[:, 3 + (2 * t + 1) % 4, :].rearrange("p (k n) -> p k n", k=4)[:, :, 0:rows(t)]).then_inc(hT_v, 1)
                v.wait_ge(small_in, 7 * 16)
                v.wait_ge(st_ps, 1)
                v.tensor_copy(us[:, :, :, 0:2], psum[:, 7, 0:64].rearrange("p (c b i) -> p c b i", c=WC, b=DEC_B)).then_inc(st_ok, 1)
                for j, dst in ((0, q_sb), (1, k_sb)):
                    for t in range(NT):
                        r, n = rows(t), j * NT + t
                        v.wait_ge(proj, n + 1)
                        src = psum[0:r, n % 3, :].rearrange("p (h d) -> p h d", h=HEADS)
                        ra = rot[0:r, 0, :].rearrange("p (h d) -> p h d", h=HEADS)
                        rb = rot[0:r, 1, :].rearrange("p (h d) -> p h d", h=HEADS)
                        cos = rope[0:r, 0, t, :].unsqueeze(1).broadcast_to([r, HEADS, HD])
                        sin = rope[0:r, 1, t, :].unsqueeze(1).broadcast_to([r, HEADS, HD])
                        h = HD // 2
                        settle()
                        step(v.tensor_tensor(ra, src, cos, ALU.mult))
                        step(v.tensor_tensor(rb[:, :, 0:h], src[:, :, h:], sin[:, :, 0:h], ALU.mult))
                        step(v.tensor_tensor(rb[:, :, h:], src[:, :, 0:h], sin[:, :, h:], ALU.mult))
                        settle()
                        n_step[0] += 1
                        v.tensor_tensor(dst[0:r, t, :], rot[0:r, 0, :], rot[0:r, 1, :], ALU.add).then_inc(v_step, 1)
                        settle()
                        v.sem_inc(qk_ok, 1)
                v.wait_ge(pads, 2)
                v.wait_ge(st_ok, 1)
                for m in range(WC):
                    v.wait_ge(cmm, WC + m + 1)
                    v.wait_ge(hc_ok, m + 1)
                    uss = us[:, m, :, :]
                    b = (WC + m) % 2
                    step(v.tensor_tensor(up[:, m, 2:], psum[:, 3 + b, :], hcT[:, m, 0:SEQ], ALU.mult))
                    step(v.tensor_tensor(uss[:, :, 2:], psum[:, 5 + b, 0:NS].rearrange("p (b t) -> p b t", b=DEC_B),
                                         hcT[:, m, SEQ:].rearrange("p (b t) -> p b t", b=DEC_B), ALU.mult))
                    settle()
                    v.sem_inc(gcb_ok, 1)
                    cp = convT[:, m, 0:SEQ]
                    cq = convT[:, m, SEQ:].rearrange("p (b t) -> p b t", b=DEC_B)
                    for j in range(3):
                        wj = convw[:, j, m:m + 1]
                        if j == 0:
                            step(v.tensor_scalar(cp, up[:, m, 0:SEQ], wj, None, ALU.mult))
                            step(v.tensor_scalar(cq, uss[:, :, 0:DEC_T], wj, None, ALU.mult))
                        else:
                            settle()
                            step(v.scalar_tensor_tensor(cp, up[:, m, j:j + SEQ], wj, cp, ALU.mult, ALU.add))
                            step(v.scalar_tensor_tensor(cq, uss[:, :, j:j + DEC_T], wj, cq, ALU.mult, ALU.add))
                step(v.tensor_copy(tail[:, :, 0:2], up[:, :, SEQ:SEQ + 2]))
                step(v.tensor_copy(tail[:, :, 2:].rearrange("p c (b i) -> p c b i", b=DEC_B), us[:, :, :, DEC_T:]))
                settle()
                v.sem_inc(tail_ok, 1)
                for m in range(WC):
                    v.wait_ge(cmm, 2 * WC + m + 1)
                    b = (2 * WC + m) % 2
                    step(v.tensor_tensor(convT[:, m, 0:SEQ], psum[:, 3 + b, :], convT[:, m, 0:SEQ], ALU.mult))
                    step(v.tensor_tensor(convT[:, m, SEQ:], psum[:, 5 + b, 0:NS], convT[:, m, SEQ:], ALU.mult))
                    settle()
                    v.sem_inc(gcb_ok, 1)
                v.wait_ge(tail_ps, 1)
                v.tensor_copy(tail_rows[:, :], psum[0:18, 0, :]).then_inc(tail_sb, 1)
                v.wait_ge(ssq_ps, 1)
                for r, a, b in ((P, 0, NPT), (NS, NPT, NT)):
                    step(v.tensor_scalar(cs[0:r, a:b], psum[0:r, 7, 64 + a:64 + b], 1.0 / W, EPS, ALU.mult, ALU.add))
                settle()
                v.sem_inc(cms_ok, 1)

            @block.tensor
            def _(pe):
                pe.wait_ge(cst_in, 16)
                pe.wait_ge(c_silu, 1)
                for k in range(KC):
                    last = pe.transpose(psum[:, 0, 9 * k:9 * k + 9], c_sb[:, 2, k * P:(k + 1) * P], ident[0:9, 0:9])
                last.then_inc(cT_ps, 1)
                pe.wait_ge(small_in, 7 * 16)
                for m in range(WC):
                    last = pe.transpose(psum[:, 7, 16 * m:16 * m + 16], state[:, m * P:(m + 1) * P], ident[0:16, 0:16])
                last.then_inc(st_ps, 1)
                pe.wait_ge(cT_ok, 1)
                for n in range(NADA):
                    pe.wait_ge(w_in[n % 4], 16 * (n // 4 + 1))
                    if n >= 2:
                        pe.wait_ge(mod_ok, n - 1)
                    for k in range(KC):
                        last = pe.matmul(psum[0:9, 1 + n % 2, :], cT[:, k, :], ring[:, n % 4, k, :],
                                         start=(k == 0), stop=(k == KC - 1))
                    last.then_inc(w_used, 1)
                for t in range(NT):
                    r = rows(t)
                    pe.wait_ge(h_ok, t + 1)
                    for half in range(2):
                        i = 2 * t + half
                        if i >= 4:
                            pe.wait_ge((hT_a, hT_v)[half], t - 1)
                        for k in range(4):
                            kk = 4 * half + k
                            last = pe.transpose(psum[:, 3 + i % 4, k * P:k * P + r], xh[0:r, t, kk * P:(kk + 1) * P],
                                                ident[0:r, 0:r])
                        last.then_inc(hT_ps, 1)
                pe.wait_ge(mod_ok, NADA)
                for j in range(3):
                    n = NADA + j
                    pe.wait_ge(w_in[n % 4], 16 * (n // 4 + 1))
                    for t in range(NT):
                        i, r = j * NT + t, rows(t)
                        if j == 0:
                            pe.wait_ge(hT_a, t + 1)
                            pe.wait_ge(hT_v, t + 1)
                        if i >= 3:
                            if i - 3 < 2 * NT:
                                pe.wait_ge(qk_ok, i - 2)
                            else:
                                pe.wait_ge(v_ok, i - 2 - 2 * NT)
                        for k in range(KC):
                            last = pe.matmul(psum[0:r, i % 3, :], hT[:, k, t * P:t * P + r], ring[:, n % 4, k, :],
                                             start=(k == 0), stop=(k == KC - 1))
                        last.then_inc(proj, 1)
                for j in range(3):
                    n = NADA + 3 + j
                    pe.wait_ge(w_in[n % 4], 16 * (n // 4 + 1))
                    for m in range(WC):
                        i = j * WC + m
                        if i >= 2:
                            if i - 2 < WC:
                                pe.wait_ge(hc_ok, i - 1)
                            else:
                                pe.wait_ge(gcb_ok, i - 1 - WC)
                        for k in range(KC):
                            pe.matmul(psum[:, 3 + i % 2, :], ring[:, n % 4, k, m * P:(m + 1) * P], hT[:, k, 0:SEQ],
                                      start=(k == 0), stop=(k == KC - 1))
                            last = pe.matmul(psum[:, 5 + i % 2, 0:NS], ring[:, n % 4, k, m * P:(m + 1) * P], hT[:, k, SEQ:],
                                             start=(k == 0), stop=(k == KC - 1))
                        last.then_inc(cmm, 1)
                pe.wait_ge(tail_ok, 1)
                pe.wait_ge(v_ok, NT)
                for m in range(WC):
                    last = pe.transpose(psum[0:18, 0, m * P:(m + 1) * P], tail[:, m, :], ident)
                last.then_inc(tail_ps, 1)
                pe.wait_ge(sq_ok, 2 * WC)
                for t in range(NT):
                    for m in range(WC):
                        last = pe.matmul(psum[0:rows(t), 7, 64 + t:65 + t], hcT[:, m, t * P:t * P + rows(t)],
                                         cst[:, C_ONE:C_ONE + 1], start=(m == 0), stop=(m == WC - 1))
                last.then_inc(ssq_ps, 1)
        st.close()

    wout_in, shared_in = sem("wout_in"), sem("shared_in")

    def load_expert(eng, dst, gate, up_, down, signal):
        gu = dst[:, 0:KC * 2 * FE].rearrange("p (k n) -> p k n", k=KC)
        eng.dma_start(gu[:, :, 0:FE], gate.rearrange("(k p) n -> p k n", p=P)).then_inc(signal, 16)
        eng.dma_start(gu[:, :, FE:], up_.rearrange("(k p) n -> p k n", p=P)).then_inc(signal, 16)
        eng.dma_start(dst[:, KC * 2 * FE:].rearrange("p (k n) -> p k n", k=2),
                      down.rearrange("(k p) n -> p k n", p=P)).then_inc(signal, 16)

    def stage_2():
        st = ExitStack()

        def tmp(name, shape, dt=F32):
            return st.enter_context(nc.sbuf_tensor("sb_" + name, shape, dt))

        k_sb, v_sb = keeps["k"], keeps["v"]
        q_sb = attn
        masks = tmp("masks", [P, A_END])
        qT = tmp("qT", [P, WC, SEQ])
        kT = tmp("kT", [P, WC, SEQ])
        kTn = tmp("kTn", [P, WC, NS])
        qz = tmp("qz", [P, WC, DEC_B, HEADS * DEC_T])
        probs = tmp("probs", [P, 3, SEQ])
        pT = tmp("pT", [P, 2, SEQ])
        nmax = tmp("nmax", [P, NPT * HEADS])
        den = tmp("den", [P, NPT * HEADS])
        rden = tmp("rden", [P, NPT * HEADS])
        KTs = tmp("KTs", [P, 2, WIN + 4 * SPARSE])
        sp_ = tmp("s_probs", [P, SK])
        spT = tmp("s_pT", [P, 9, P])
        snm = tmp("s_nm", [P, 2, 4])
        sden = tmp("s_den", [P, 2, 2])
        om = probs[:, 0:2, :]
        vring = stream[:, 0:4 * 4096].rearrange("p (s t n) -> p s t n", s=4, t=8)
        kring = stream[:, 4 * 4096:6 * 4096].rearrange("p (s t n) -> p s t n", s=2, t=8)
        wout = stream[:, 4 * 4096:6 * 4096].rearrange("p (k n) -> p k n", k=KC)
        shared = stream[:, 0:6144]

        masks_in = sem("s2_masks_in")
        k_in = [sem(f"s2_k{i}") for i in range(2)]
        v_in = [sem(f"s2_v{i}") for i in range(4)]
        zeroed, turn_ps, turn_ok, new_ps, new_ok = (sem(f"s2_{n}") for n in
                                                    ("zeroed", "turn_ps", "turn_ok", "new_ps", "new_ok"))
        sc, sc_read, exp_ok, p_ok = (sem(f"s2_{n}") for n in ("sc", "sc_read", "exp_ok", "p_ok"))
        pT_ps, pT_ok, pv, pv_read = (sem(f"s2_{n}") for n in ("pT_ps", "pT_ok", "pv", "pv_read"))
        kt_ps, kt_a, kt_v, ssc = (sem(f"s2_{n}") for n in ("kt_ps", "kt_a", "kt_v", "ssc"))
        ssc_read, sexp, sp_ok = (sem(f"s2_{n}") for n in ("ssc_read", "sexp", "sp_ok"))
        spt_ps, spt_a, spt_v, spv, om_ok, fold = (sem(f"s2_{n}") for n in
                                                  ("spt_ps", "spt_a", "spt_v", "spv", "om_ok", "fold"))
        v_step = sem("s2_v_step")

        def load_cache(eng, dst, cache, b, signal):
            c = cache[0, b].rearrange("r h d -> r (h d)")
            eng.dma_start(dst[:, 0:4, :], c[WIN0:, :].rearrange("(p t) n -> p t n", t=4)).then_inc(signal, 16)
            eng.dma_start(dst[0:SPARSE, 4:8, :],
                          c[0:WIN0, :].rearrange("(j s) n -> j s n", s=16)[:, 0:4, :]).then_inc(signal, 16)

        with nc.Block() as block:
            @block.sync
            def _(sp):
                sp.dma_start(masks[:, :], io["masks"]).then_inc(masks_in, 16)

                def key(b):
                    if b >= 2:
                        sp.wait_ge(ssc, 4 * (b - 1))
                    load_cache(sp, kring[:, b % 2], io["cache_k"], b, k_in[b % 2])

                def value(b):
                    if b >= 4:
                        sp.wait_ge(spv, b - 3)
                    load_cache(sp, vring[:, b % 4], io["cache_v"], b, v_in[b % 4])

                for b in range(4):
                    if b == 1:
                        sp.wait_ge(stored, 6 * 16)
                    key(b)
                    value(b)
                for b in (4, 6):
                    key(b)
                    key(b + 1)
                    value(b)
                    value(b + 1)
                sp.wait_ge(ssc, 4 * DEC_B)
                sp.dma_start(wout, io["w_out"][0].rearrange("(k p) n -> p k n", p=P)).then_inc(wout_in, 16)
                sp.wait_ge(spv, 6)
                load_expert(sp, shared, io["w_sh_gate"][0], io["w_sh_up"][0], io["w_sh_down"][0], shared_in)

            @block.gpsimd
            def _(pool):
                pool.memset(qz[:, :, :, :], 0.0).then_inc(zeroed, 1)
                pool.memset(spT[:, 8, :], 0.0).then_inc(zeroed, 1)

            @block.scalar
            def _(act):
                for i in range(2 * WC):
                    act.wait_ge(turn_ps, i + 1)
                    act.copy((qT, kT)[i % 2][:, i // 2, :], psum[:, 4 + i % 2, :]).then_inc(turn_ok, 1)
                N = NPT * HEADS
                for n in range(N + 2):
                    if n < N:
                        act.wait_ge(sc_read, n + 1)
                        w = (n // HEADS + 1) * P
                        act.activation(probs[:, n % 3, 0:w], probs[:, n % 3, 0:w], ACT.Exp,
                                       bias=nmax[:, n:n + 1], scale=-1.0).then_inc(exp_ok, 1)
                    m = n - 2
                    if m >= 0:
                        act.wait_ge(pT_ps, m + 1)
                        if m >= 2:
                            act.wait_ge(pv, m - 1)
                        w = (m // HEADS + 1) * P
                        act.copy(pT[:, m % 2, 0:w], psum[:, 4 + m % 2, 0:w]).then_inc(pT_ok, 1)
                for g in range(2):
                    for e in range(16 * g, 16 * g + 16):
                        act.wait_ge(kt_ps, e + 1)
                        if e >= 2:
                            act.wait_ge(ssc, e - 1)
                        act.copy(KTs[:, e % 2, 0:WIN], psum[:, e % 2, :]).then_inc(kt_a, 1)
                    act.wait_ge(ssc_read, g + 1)
                    act.activation(sp_[:, :], sp_[:, :], ACT.Exp, bias=snm[:, g, 2:3], scale=-1.0).then_inc(sexp, 1)
                    act.wait_ge(spt_ps, g + 1)
                    act.copy(spT[:, 0:4, :], psum[:, 0, :].rearrange("p (t n) -> p t n", t=4)).then_inc(spt_a, 1)

            @block.vector
            def _(v):
                n_step = [0]

                def step(ins):
                    n_step[0] += 1
                    ins.then_inc(v_step, 1)

                def settle():
                    v.wait_ge(v_step, n_step[0])

                v.wait_ge(zeroed, 1)
                v.wait_ge(new_ps, 2)
                for h in range(HEADS):
                    lo = (h % 2) * HD
                    step(v.tensor_copy(qz[lo:lo + HD, h // 2, :, h * DEC_T:(h + 1) * DEC_T],
                                       psum[lo:lo + HD, 6, (h // 2) * NS:(h // 2 + 1) * NS].rearrange("p (b t) -> p b t", b=DEC_B)))
                step(v.tensor_copy(kTn[:, :, :], psum[:, 7, 0:WC * NS].rearrange("p (c n) -> p c n", c=WC)))
                settle()
                v.sem_inc(new_ok, 1)
                v.wait_ge(masks_in, 16)
                N = NPT * HEADS

                def finish_tile(i):
                    v.wait_ge(pv, HEADS * (i + 1))
                    step(v.reciprocal(rden[:, i * HEADS:(i + 1) * HEADS], den[:, i * HEADS:(i + 1) * HEADS]))
                    settle()
                    v.tensor_tensor(attn[:, i, :].rearrange("p (h d) -> p h d", h=HEADS),
                                    psum[:, 6 + i % 2, :].rearrange("p (h d) -> p h d", h=HEADS),
                                    rden[:, i * HEADS:(i + 1) * HEADS].unsqueeze(2).broadcast_to([P, HEADS, HD]),
                                    ALU.mult).then_inc(pv_read, 1)

                for n in range(N + 1):
                    if n < N:
                        i = n // HEADS
                        w, a = (i + 1) * P, (NPT - 1 - i) * P
                        v.wait_ge(sc, n + 1)
                        if n >= 3:
                            v.wait_ge(pT_ps, n - 2)
                        v.tensor_tensor_reduce(probs[:, n % 3, 0:w], psum[:, n % 3, 0:w], masks[:, A_PN + a:A_PN + 512],
                                               -HD ** -0.5, 3e38, ALU.add, ALU.min, nmax[:, n:n + 1]).then_inc(sc_read, 1)
                    if n >= 1:
                        m = n - 1
                        i = m // HEADS
                        w, a = (i + 1) * P, (NPT - 1 - i) * P
                        v.wait_ge(exp_ok, m + 1)
                        v.tensor_tensor_reduce(probs[:, m % 3, 0:w], probs[:, m % 3, 0:w], masks[:, A_PM + a:A_PM + 512],
                                               1.0, 0.0, ALU.mult, ALU.add, den[:, m:m + 1]).then_inc(p_ok, 1)
                    if n % HEADS == 5 and n > HEADS:
                        v.wait_ge(p_ok, n)
                        finish_tile(n // HEADS - 1)
                v.wait_ge(p_ok, N)
                finish_tile(NPT - 1)
                for g in range(2):
                    for e in range(16 * g, 16 * g + 16):
                        v.wait_ge(kt_ps, e + 1)
                        if e >= 2:
                            v.wait_ge(ssc, e - 1)
                        v.tensor_copy(KTs[:, e % 2, WIN:], psum[:, 2 + e % 2, 0:4 * SPARSE]).then_inc(kt_v, 1)
                    v.wait_ge(ssc, 16 * (g + 1))
                    if g:
                        v.wait_ge(spt_ps, g)
                    for j, (a, b) in enumerate(((0, WIN), (WIN, SK))):
                        step(v.tensor_tensor_reduce(sp_[:, a:b], psum[:, 4 + j, 0:b - a],
                                                    masks[:, A_SN + g * SK + a:A_SN + g * SK + b],
                                                    -HD ** -0.5, 3e38, ALU.add, ALU.min, snm[:, g, j:j + 1]))
                    settle()
                    v.tensor_tensor(snm[:, g, 2:3], snm[:, g, 0:1], snm[:, g, 1:2], ALU.min).then_inc(ssc_read, 1)
                    v.wait_ge(sexp, g + 1)
                    v.tensor_tensor_reduce(sp_[:, :], sp_[:, :], masks[:, A_SM + g * SK:A_SM + (g + 1) * SK],
                                           1.0, 0.0, ALU.mult, ALU.add, sden[:, g, 0:1]).then_inc(sp_ok, 1)
                    v.wait_ge(zeroed, 2)
                    v.wait_ge(spt_ps, g + 1)
                    v.tensor_copy(spT[0:SPARSE, 4:8, :], psum[0:SPARSE, 1, :].rearrange("p (t n) -> p t n", t=4)).then_inc(spt_v, 1)
                    v.tensor_copy(spT[0:NS, 8, :], psum[0:NS, 2, 0:P]).then_inc(spt_v, 1)
                    v.wait_ge(sp_ok, g + 1)
                    step(v.reciprocal(sden[:, g, 1:2], sden[:, g, 0:1]))
                    settle()
                    v.wait_ge(spv, 4 * (g + 1))
                    v.scalar_tensor_tensor(om[:, g, :], psum[:, 6 + g, :], sden[:, g, 1:2], masks[:, A_BD:A_BD + W],
                                           ALU.mult, ALU.mult).then_inc(om_ok, 1)
                v.wait_ge(fold, 1)
                v.tensor_copy(attn[0:NS, NPT, :], psum[0:NS, 0, :])

            @block.tensor
            def _(pe):
                for j, src in enumerate((q_sb, k_sb)):
                    for c in range(WC):
                        last = pe.transpose(psum[:, 6 + j, c * NS:(c + 1) * NS], src[0:NS, NPT, c * P:(c + 1) * P],
                                            ident[0:NS, 0:NS])
                    last.then_inc(new_ps, 1)
                for i in range(2 * WC):
                    if i >= 2:
                        pe.wait_ge(turn_ok, i - 1)
                    for t in range(NPT):
                        last = pe.transpose(psum[:, 4 + i % 2, t * P:(t + 1) * P],
                                            (q_sb, k_sb)[i % 2][:, t, (i // 2) * P:(i // 2 + 1) * P], ident)
                    last.then_inc(turn_ps, 1)
                pe.wait_ge(turn_ok, 2 * WC)
                N = NPT * HEADS
                for n in range(N + 3):
                    if n < N:
                        i, h = n // HEADS, n % HEADS
                        lo = (h % 2) * HD
                        if n >= 3:
                            pe.wait_ge(sc_read, n - 2)
                        pe.matmul(psum[:, n % 3, 0:(i + 1) * P], qT[lo:lo + HD, h // 2, i * P:(i + 1) * P],
                                  kT[lo:lo + HD, h // 2, 0:(i + 1) * P], start=True, stop=True).then_inc(sc, 1)
                    m = n - 2
                    if 0 <= m < N:
                        pe.wait_ge(p_ok, m + 1)
                        if m >= 2:
                            pe.wait_ge(pT_ok, m - 1)
                        for t in range(m // HEADS + 1):
                            last = pe.transpose(psum[:, 4 + m % 2, t * P:(t + 1) * P], probs[:, m % 3, t * P:(t + 1) * P], ident)
                        last.then_inc(pT_ps, 1)
                    m = n - 3
                    if m >= 0:
                        i, h = m // HEADS, m % HEADS
                        pe.wait_ge(pT_ok, m + 1)
                        if m == 0:
                            pe.wait_ge(new_ok, 1)
                        if h == 0 and i >= 2:
                            pe.wait_ge(pv_read, i - 1)
                        for t in range(i + 1):
                            last = pe.matmul(psum[:, 6 + i % 2, h * HD:(h + 1) * HD], pT[:, m % 2, t * P:(t + 1) * P],
                                             v_sb[:, t, h * HD:(h + 1) * HD], start=(t == 0), stop=(t == i))
                        last.then_inc(pv, 1)
                pe.wait_ge(pv_read, NPT)

                def turn_keys(e):
                    b, c = e // 4, e % 4
                    if c == 0:
                        pe.wait_ge(k_in[b % 2], 32 * (b // 2 + 1))
                    if e >= 2:
                        pe.wait_ge(kt_a, e - 1)
                        pe.wait_ge(kt_v, e - 1)
                    for t in range(4):
                        pe.transpose(psum[:, e % 2, t * P:(t + 1) * P], kring[:, b % 2, t, c * P:(c + 1) * P], ident)
                    for t in range(4):
                        last = pe.transpose(psum[:, 2 + e % 2, t * SPARSE:(t + 1) * SPARSE],
                                            kring[0:SPARSE, b % 2, 4 + t, c * P:(c + 1) * P], ident[0:SPARSE, 0:SPARSE])
                    last.then_inc(kt_ps, 1)

                for g in range(2):
                    if g:
                        pe.wait_ge(ssc_read, g)
                        pe.wait_ge(spt_v, 2 * g)
                        pe.wait_ge(spt_a, g)
                    turn_keys(16 * g)
                    for e in range(16 * g, 16 * g + 16):
                        b, c = e // 4, e % 4
                        lo = 32 * (b % 4)
                        if e + 1 < 16 * g + 16:
                            turn_keys(e + 1)
                        pe.wait_ge(kt_a, e + 1)
                        pe.wait_ge(kt_v, e + 1)
                        w = qz[:, c, b, :]
                        pe.matmul(psum[lo:lo + 32, 4, :], w, KTs[:, e % 2, 0:WIN], start=(c == 0), stop=(c == 3))
                        pe.matmul(psum[lo:lo + 32, 5, 0:4 * SPARSE], w, KTs[:, e % 2, WIN:], start=(c == 0), stop=False,
                                  skip_group_check=True)
                        last = pe.matmul(psum[lo:lo + 32, 5, 4 * SPARSE:4 * SPARSE + NS], w, kTn[:, c, :],
                                         start=False, stop=(c == 3), skip_group_check=True)
                        last.then_inc(ssc, 1)
                    pe.wait_ge(sp_ok, g + 1)
                    for t in range(4):
                        pe.transpose(psum[:, 0, t * P:(t + 1) * P], sp_[:, t * P:(t + 1) * P], ident)
                    for t in range(4):
                        pe.transpose(psum[0:SPARSE, 1, t * P:(t + 1) * P], sp_[:, WIN + t * SPARSE:WIN + (t + 1) * SPARSE], ident)
                    pe.transpose(psum[0:NS, 2, 0:P], sp_[:, WIN + 4 * SPARSE:], ident).then_inc(spt_ps, 1)
                    pe.wait_ge(spt_a, g + 1)
                    pe.wait_ge(spt_v, 2 * (g + 1))
                    for b in range(4 * g, 4 * g + 4):
                        lo = 32 * (b % 4)
                        pe.wait_ge(v_in[b % 4], 32 * (b // 4 + 1))
                        for t in range(9):
                            k = P if t < 4 or t == 8 else SPARSE
                            rhs = vring[0:k, b % 4, t, :] if t < 8 else v_sb[:, NPT, :]
                            last = pe.matmul(psum[lo:lo + 32, 6 + g, :], spT[0:k, t, lo:lo + 32], rhs,
                                             start=(t == 0), stop=(t == 8))
                        last.then_inc(spv, 1)
                pe.wait_ge(om_ok, 2)
                for g in range(2):
                    last = pe.matmul(psum[0:NS, 0, :], masks[:, A_SEL + g * NS:A_SEL + (g + 1) * NS], om[:, g, :],
                                     start=(g == 0), stop=(g == 1))
                last.then_inc(fold, 1)
        st.close()

    def stage_3():
        st = ExitStack()

        def tmp(name, shape, dt=F32):
            return st.enter_context(nc.sbuf_tensor("sb_" + name, shape, dt))

        x2 = tmp("x2", [P, NT, D])
        bc = tmp("bc", [P, 3, 2, D])
        flat = bc[:, :, :, :].rearrange("p a b n -> p (a b n)")
        ysh = flat[:, 0:NT * D].rearrange("p (t n) -> p t n", t=NT)
        h2T = tmp("h2T", [P, KC, NTOK])
        work = tmp("work", [P, 3, D])
        xg = work
        aT = tmp("aT", [P, 2, WC, P])
        wr = tmp("wr", [P, KC, NE])
        sil, hid = (aT[:, :, :, :].rearrange("p s c n -> p (s c n)")[:, 2 * P * a:2 * P * (a + 1)]
                    .rearrange("p (k n) -> p k n", k=2) for a in range(2))
        oh = tmp("oh", [P, 3, NT, P], BF16)
        pick = tmp("pick", [P, 3, NT, 9], BF16)
        table = tmp("table", [P, NT, NE, 9], BF16)
        blk = tmp("blk", [P, 3, NT])
        got = tmp("got", [P, 3, 3])
        token = tmp("token", [P, 3, 1], U32)
        row = tmp("row", [P, 3, 1], U32)
        now_gate = tmp("now_gate", [P, 3])
        tab = tmp("tab", [1, P + 1], I32)
        bias = tmp("bias", [P, NE])
        ss = tmp("ss3", [P, 4, NT])
        small = tmp("small", [P, 80])
        wout = stream[:, 4 * 4096:6 * 4096].rearrange("p (k n) -> p k n", k=KC)
        wslot = [stream[:, 6144 * s:6144 * (s + 1)] for s in range(3)]
        xT = stream[:, 18432:18432 + 3 * D].rearrange("p (s k n) -> p s k n", s=3, k=KC)
        out = stream[:, 18432 + 3 * D:18432 + 6 * D].rearrange("p (s n) -> p s n", s=3)
        af = attn[:, :, :].rearrange("p t n -> p (t n)")
        scores, sel, selm, mask, gate, ra, rb, gpos = (
            af[:, 320 * n:320 * (n + 1)].rearrange("p (t e) -> p t e", t=NT) for n in range(8))
        cf = convg[:, :, :].rearrange("p c n -> p (c n)")
        run = [cf[:, 480 * n:480 * (n + 1)].rearrange("p (t e) -> p t e", t=NT) for n in range(2)]
        erun = [cf[:, 960 + 96 * n:960 + 96 * (n + 1)] for n in range(2)]
        nblk, cnt, first = (cf[:, 1152 + 64 * n:1152 + 64 * (n + 1)] for n in range(3))
        grp = cf[:, 1344:1384].rearrange("p (t g) -> p t g", t=NT)
        gok = cf[:, 1384:1424].rearrange("p (t g) -> p t g", t=NT)
        gneg = cf[:, 1424:1464].rearrange("p (t g) -> p t g", t=NT)
        top = cf[:, 1464:1504].rearrange("p (t g) -> p t g", t=NT)
        gsum, grec = cf[:, 1504:1509], cf[:, 1509:1514]
        blkf, tripf = cf[:, 1514:1515], cf[:, 1515:1516]
        maskb = cf[:, 1520:1520 + 160].bitcast(BF16).rearrange("p (t e) -> p t e", t=NT)
        trib = cf[:, 1680:1680 + 64].bitcast(BF16)
        oneb = cf[:, 1744:1744 + 64].bitcast(BF16)

        DN0 = 2 * NT
        names = ("x_in bc_in small_in ams rs an_ok aT_ps aT_ok prod_c prod_a tc_ok x2_ok ms h2_ok h2_ps h2_a h2_v logit "
                 "ex_ok zeroed mask_ok cnt_ps blk_ok tab_ps tab_ok table_ok consts_ok "
                 "sgu ssil shid "
                 "list_mm list_ok oh_ok token_ok now_ok xt_ps xt_a xt_v gu sil_ok hid_ok dn out_a out_v pick_ok go").split()
        s = {n: sem("s3_" + n) for n in names}
        h_out = [sem(f"s3_h_out{i}") for i in range(2)]
        w_in = [sem(f"s3_w{i}") for i in range(3)]
        moved = [sem(f"s3_moved{i}") for i in range(3)]
        v_step = sem("s3_v_step")

        def trips(eng):
            eng.wait_ge(s["tab_ok"], 1)
            return eng.value_load(tab[0:1, P:P + 1], min_val=0, max_val=TRIPS)

        def expert_of(eng, b):
            return eng.value_load(tab[0:1, bass.ds(b, 1)], min_val=0, max_val=NE - 1)

        def who(v, b, u):
            e = expert_of(v, b)
            v.tensor_tensor(blk[:, u, :].unsqueeze(2), gpos[:, :, bass.ds(e, 1)],
                            cst[:, bass.ds(b + C_BASE, 1)].unsqueeze(1).broadcast_to([P, NT, 1]), ALU.subtract).then_inc(s["blk_ok"], 1)
            v.tensor_copy(pick[:, u, :, :].unsqueeze(2), table[:, :, bass.ds(e, 1), :]).then_inc(s["pick_ok"], 1)
            v.wait_ge(s["blk_ok"], b + 1)
            for t in range(NT):
                last = v.tensor_scalar(oh[:, u, t, :], cst[:, C_IOTA:C_IOTA + P], blk[:, u, t:t + 1], None, ALU.is_equal)
            last.then_inc(s["oh_ok"], 1)

        def fill_list(pe, b, u):
            pe.wait_ge(s["oh_ok"], b + 1)
            pe.wait_ge(s["pick_ok"], b + 1)
            if not isinstance(b, int) or b:
                pe.wait_ge(s["list_ok"], b)
            for t in range(NT):
                last = pe.matmul(psum[:, 6, 0:9], oh[:, u, t, :], pick[:, u, t, :], start=(t == 0), stop=(t == NT - 1))
            last.then_inc(s["list_mm"], 1)

        def read_list(v, b, u):
            v.wait_ge(s["list_mm"], b + 1)
            v.tensor_reduce(got[:, u, :], psum[:, 6, 0:9].rearrange("p (a c) -> p a c", a=3), AX.X, ALU.add).then_inc(s["list_ok"], 1)
            v.wait_ge(s["list_ok"], b + 1)
            v.tensor_scalar(token[:, u, :], got[:, u, 0:1], float(OUTSIDE), None, ALU.add).then_inc(s["token_ok"], 1)

        def gather(pool, b, u, last_row):
            pool.wait_ge(s["token_ok"], b + 1)
            pool.sem_inc(s["go"], 1)
            pool.indirect_dma_start(xg[:, u, :], None, h_rows, bass.IndirectOffsetOnAxis(ap=token[:, u, :], axis=0),
                                    bounds_check=last_row, oob_is_err=False).then_inc(moved[u], 16)

        def turn_rows(pe, u, arrived):
            pe.wait_ge(moved[u], arrived)
            for k in range(KC):
                last = pe.transpose(psum[:, 1 + k // 4, (k % 4) * P:(k % 4 + 1) * P], xg[:, u, k * P:(k + 1) * P], ident)
                if k % 4 == 3:
                    last.then_inc(s["xt_ps"], 1)

        def take_rows_a(act, b, u):
            act.wait_ge(s["xt_ps"], 2 * b + 1)
            act.copy(xT[:, u, 0:4, :], psum[:, 1, :].rearrange("p (k n) -> p k n", k=4)).then_inc(s["xt_a"], 1)

        def take_rows_v(v, b, u):
            v.wait_ge(s["xt_ps"], 2 * b + 2)
            v.tensor_copy(xT[:, u, 4:8, :], psum[:, 2, :].rearrange("p (k n) -> p k n", k=4)).then_inc(s["xt_v"], 1)

        def gate_up(pe, bank, r, rhs, w, done):
            gu = w[:, 0:KC * 2 * FE].rearrange("p (k n) -> p k n", k=KC)
            for m in range(4):
                for k in range(KC):
                    last = pe.matmul(psum[:, bank, m * P:m * P + r], gu[:, k, m * P:(m + 1) * P], rhs(k),
                                     start=(k == 0), stop=(k == KC - 1))
            last.then_inc(done, 1)

        def halves(bank, r):
            gu = psum[:, bank, :].rearrange("p (a k n) -> p a k n", a=2, k=2)
            return gu[:, 0, :, 0:r], gu[:, 1, :, 0:r]

        def down(pe, r, w, done, waits):
            dn = w[:, KC * 2 * FE:].rearrange("p (k n) -> p k n", k=2)
            for n in range(2):
                waits(n)
                for k in range(2):
                    last = pe.matmul(psum[0:r, 4 + n, :], hid[:, k, 0:r], dn[:, k, n * 512:(n + 1) * 512],
                                     start=(k == 0), stop=(k == 1))
                last.then_inc(done, 1)

        with nc.Block() as block:
            @block.sync
            def _(sp):
                sp.dma_start(x2[:, 0:NPT, :], io["x_prompt"][0].rearrange("(t p) n -> p t n", p=P)).then_inc(s["x_in"], 16)
                sp.dma_start(x2[0:NS, NPT, :], io["x_sample"].rearrange("b t n -> (b t) n")).then_inc(s["x_in"], 16)
                for n, j in enumerate((2, 3, 4)):
                    sp.dma_start(bc[:, n, 0, :], bc_row(mod_rows[0:1, j * D:(j + 1) * D], P)).then_inc(s["bc_in"], 16)
                    sp.dma_start(bc[0:NS, n, 1, :], mod_sample(j)).then_inc(s["bc_in"], 16)
                sp.dma_start(wr[:, :, :], io["w_router"][0].rearrange("(k p) n -> p k n", p=P)).then_inc(s["small_in"], 16)
                sp.dma_start(bias[:, :], bc_row(io["router_bias"], P)).then_inc(s["small_in"], 16)
                for t in range(NT):
                    sp.wait_ge(s["h2_ok"], t + 1)
                    sp.dma_start(h_rows[t * P:t * P + rows(t), :], work[0:rows(t), 1 + t % 2, :]).then_inc(h_out[t % 2], 16)
                nb = trips(sp)
                with sp.Fori(0, TRIPS) as i:
                    with sp.If(nb > i):
                        for u in range(3):
                            b = 3 * i + u
                            e = expert_of(sp, b)
                            sp.wait_ge(s["dn"], 2 * (b - 2) + DN0)
                            load_expert(sp, wslot[(u + 1) % 3],
                                        io["w_exp_gate"][0, bass.ds(e, 1)].rearrange("a d f -> (a d) f"),
                                        io["w_exp_up"][0, bass.ds(e, 1)].rearrange("a d f -> (a d) f"),
                                        io["w_exp_down"][0, bass.ds(e, 1)].rearrange("a d f -> (a d) f"), w_in[u])

            @block.gpsimd
            def _(pool):
                pool.memset(table[:, :, :, :].rearrange("p t e c -> p (t e c)"), 0.0).then_inc(s["zeroed"], 1)
                pool.wait_ge(s["zeroed"], 1)
                for t in range(NT):
                    pool.tensor_copy(table[:, t, :, 0:5],
                                     cst[:, C_LP + 5 * t:C_LP + 5 * t + 5].unsqueeze(1).broadcast_to([P, NE, 5])).then_inc(s["consts_ok"], 1)
                minus_half = cst[:, C_POW:C_POW + 1]

                def inverse_root(dst, src):
                    n = dst.shape[1]
                    pool.tensor_tensor(dst, src, minus_half[0:dst.shape[0]].broadcast_to([dst.shape[0], n]), ALU.pow).then_inc(s["rs"], 1)

                pool.wait_ge(s["ams"], 1)
                inverse_root(ss[:, 1, 0:NPT], ss[:, 0, 0:NPT])
                inverse_root(ss[0:NS, 1, NPT:], ss[0:NS, 0, NPT:])
                for t in range(NT):
                    pool.wait_ge(s["ms"], t + 1)
                    inverse_root(ss[0:rows(t), 3, t:t + 1], ss[0:rows(t), 2, t:t + 1])
                pool.wait_ge(s["h2_ps"], 2 * NT)
                pool.wait_ge(s["prod_a"], NT)
                pool.memset(cf[:, 0:1152], 0.0).then_inc(s["zeroed"], 1)
                pool.memset(scores, 1.0).then_inc(s["zeroed"], 1)
                for n in range(2):
                    pool.wait_ge(h_out[n], 16 * (3 - n))
                pool.memset(xg[:, :, :], 0.0).then_inc(s["zeroed"], 1)
                last_row, last_expert_row = pool.to_reg(NTOK - 1), pool.to_reg(NTOK * TOPK - 1)
                pool.wait_ge(s["zeroed"], 4)
                gather(pool, 0, 0, last_row)
                gather(pool, 1, 1, last_row)
                gather(pool, 2, 2, last_row)
                nb = trips(pool)
                with pool.Fori(0, TRIPS) as i:
                    with pool.If(nb > i):
                        for u in range(3):
                            b = 3 * i + u
                            pool.wait_ge(s["xt_ps"], 2 * b + 2)
                            gather(pool, b + 3, u, last_row)
                            pool.wait_ge(s["now_ok"], 2 * b + 2)
                            pool.wait_ge(s["out_a"], b + 1 + NT)
                            pool.wait_ge(s["out_v"], b + 1 + NT)
                            pool.sem_inc(s["go"], 1)
                            pool.indirect_dma_start(expert_rows, bass.IndirectOffsetOnAxis(ap=row[:, u, :], axis=0),
                                                    out[:, u, :], None, bounds_check=last_expert_row,
                                                    oob_is_err=False).then_inc(moved[u], 16)
                for u in range(3):
                    pool.wait_ge(moved[u], 32 * nb + 16)
                pool.wait_ge(s["go"], 6 * nb + 3)

            @block.scalar
            def _(act):
                act.wait_ge(s["rs"], 2)
                for t in range(NT):
                    r = rows(t)
                    act.activation(attn[0:r, t, :], attn[0:r, t, :], ACT.Copy, scale=ss[0:r, 1, t:t + 1]).then_inc(s["an_ok"], 1)

                def take_attn(t):
                    act.wait_ge(s["aT_ps"], t + 1)
                    for c in range(WC):
                        last = act.activation(aT[:, t % 2, c, 0:rows(t)], psum[:, 0, c * P:c * P + rows(t)], ACT.Copy,
                                              scale=gains[:, 0, c:c + 1])
                    last.then_inc(s["aT_ok"], 1)

                def take_norm(t):
                    act.wait_ge(s["h2_ps"], 2 * t + 1)
                    act.copy(h2T[:, 0:4, t * P:t * P + rows(t)],
                             psum[:, 6, :].rearrange("p (k n) -> p k n", k=4)[:, :, 0:rows(t)]).then_inc(s["h2_a"], 1)

                for t in range(NT):
                    r = rows(t)
                    take_attn(t)
                    act.wait_ge(s["prod_c"], t + 1)
                    if t:
                        act.wait_ge(s["x2_ok"], t)
                    act.activation(work[0:r, 0, :], psum[0:r, 4:6, :].rearrange("p a n -> p (a n)"), ACT.Copy,
                                   scale=conv_r[0:r, t:t + 1]).then_inc(s["tc_ok"], 1)
                    if t:
                        take_norm(t - 1)
                take_norm(NT - 1)
                act.wait_ge(s["logit"], NT)
                act.wait_ge(s["zeroed"], 3)
                act.activation(scores[:, 0:NPT, :], psum[:, 1, 0:NPT * NE].rearrange("p (t e) -> p t e", t=NPT), ACT.Exp, scale=-1.0)
                act.activation(scores[0:NS, NPT, :], psum[0:NS, 1, NPT * NE:NT * NE], ACT.Exp, scale=-1.0).then_inc(s["ex_ok"], 1)

                def shared(t):
                    r = rows(t)
                    act.wait_ge(s["sgu"], t + 1)
                    if t:
                        act.wait_ge(s["shid"], t)
                    act.activation(sil[:, :, 0:r], halves(7 * (t % 2), r)[0], ACT.Silu).then_inc(s["ssil"], 1)
                    act.wait_ge(s["dn"], 2 * t + 1)
                    act.copy(ysh[0:r, t, 0:512], psum[0:r, 4, :]).then_inc(s["out_a"], 1)

                for t in range(NT):
                    shared(t)
                take_rows_a(act, 0, 0)
                nb = trips(act)
                with act.Fori(0, TRIPS) as i:
                    with act.If(nb > i):
                        for u in range(3):
                            b = 3 * i + u
                            act.wait_ge(s["gu"], b + 1)
                            act.activation(sil, halves(0, P)[0], ACT.Silu).then_inc(s["sil_ok"], 1)
                            take_rows_a(act, b + 1, (u + 1) % 3)
                            act.wait_ge(s["now_ok"], 2 * b + 2)
                            act.wait_ge(s["dn"], 2 * b + 1 + DN0)
                            act.activation(out[:, u, 0:512], psum[:, 4, :], ACT.Copy, scale=now_gate[:, u:u + 1]).then_inc(s["out_a"], 1)

            @block.vector
            def _(v):
                n_step = [0]

                def step(ins):
                    n_step[0] += 1
                    ins.then_inc(v_step, 1)
                    v.wait_ge(v_step, n_step[0])

                for t in range(NT):
                    r = rows(t)
                    step(v.tensor_tensor_reduce(work[0:r, 1, 0:W], attn[0:r, t, :], attn[0:r, t, :], 1.0, 0.0,
                                                ALU.mult, ALU.add, ss[0:r, 2, t:t + 1]))
                step(v.tensor_scalar(ss[:, 0, 0:NPT], ss[:, 2, 0:NPT], 1.0 / W, EPS, ALU.mult, ALU.add))
                step(v.tensor_scalar(ss[0:NS, 0, NPT:], ss[0:NS, 2, NPT:], 1.0 / W, EPS, ALU.mult, ALU.add))
                v.sem_inc(s["ams"], 1)
                v.wait_ge(s["rs"], 2)
                v.wait_ge(s["bc_in"], 6 * 16)
                for a, r in ((0, P), (1, NS)):
                    step(v.tensor_scalar(bc[0:r, 2, a, :], bc[0:r, 2, a, :], 1.0, None, ALU.add))
                v.wait_ge(s["x_in"], 32)

                def residual(t):
                    r, a = rows(t), t // NPT
                    h = work[0:r, 1 + t % 2, :]
                    v.wait_ge(s["prod_a"], t + 1)
                    v.wait_ge(s["tc_ok"], t + 1)
                    if t >= 2:
                        v.wait_ge(s["h2_ps"], 2 * (t - 1))
                        v.wait_ge(h_out[t % 2], 16 * (t // 2))
                    step(v.tensor_tensor(h, psum[0:r, 2:4, :].rearrange("p a n -> p (a n)"), work[0:r, 0, :], ALU.add))
                    v.sem_inc(s["x2_ok"], 1)
                    step(v.tensor_tensor(h, h, bc[0:r, 0, a, :], ALU.mult))
                    step(v.tensor_tensor(x2[0:r, t, :], x2[0:r, t, :], h, ALU.add))
                    step(v.tensor_tensor_reduce(h, x2[0:r, t, :], x2[0:r, t, :], 1.0, 0.0, ALU.mult, ALU.add, ss[0:r, 0, t:t + 1]))
                    step(v.tensor_scalar(ss[0:r, 2, t:t + 1], ss[0:r, 0, t:t + 1], 1.0 / D, EPS, ALU.mult, ALU.add))
                    v.sem_inc(s["ms"], 1)
                    v.wait_ge(s["rs"], 3 + t)
                    step(v.scalar_tensor_tensor(h, x2[0:r, t, :], ss[0:r, 3, t:t + 1], bc[0:r, 2, a, :], ALU.mult, ALU.mult))
                    step(v.tensor_tensor(h, h, bc[0:r, 1, a, :], ALU.add))
                    v.sem_inc(s["h2_ok"], 1)

                def take_norm(t):
                    v.wait_ge(s["h2_ps"], 2 * t + 2)
                    v.tensor_copy(h2T[:, 4:8, t * P:t * P + rows(t)],
                                  psum[:, 7, :].rearrange("p (k n) -> p k n", k=4)[:, :, 0:rows(t)]).then_inc(s["h2_v"], 1)

                for t in range(NT):
                    residual(t)
                    if t:
                        take_norm(t - 1)
                take_norm(NT - 1)

                def groups():
                    v.wait_ge(s["ex_ok"], 1)
                    v.wait_ge(s["small_in"], 32)
                    step(v.tensor_scalar(ra, scores, 1.0, None, ALU.add))
                    step(v.reciprocal(scores, ra))
                    step(v.tensor_tensor(sel, scores, bias[:, :].unsqueeze(1).broadcast_to([P, NT, NE]), ALU.add))
                    every = sel.rearrange("p t (g e) -> p (t g) e", g=NGRP)
                    raf, rbf = (x.rearrange("p t e -> p (t e)") for x in (ra, rb))
                    hi, lo = every[:, :, 0:8:2], every[:, :, 1:8:2]
                    h1 = raf[:, 0:160].rearrange("p (g e) -> p g e", e=4)
                    l1 = rbf[:, 0:160].rearrange("p (g e) -> p g e", e=4)
                    step(v.tensor_tensor(h1, hi, lo, ALU.max))
                    step(v.tensor_tensor(l1, hi, lo, ALU.min))
                    at = 160
                    for e in (2, 1):
                        n = 40 * e
                        h2_ = raf[:, at:at + n].rearrange("p (g e) -> p g e", e=e)
                        m2 = rbf[:, at:at + n].rearrange("p (g e) -> p g e", e=e)
                        l2 = small[:, 0:n].rearrange("p (g e) -> p g e", e=e)
                        step(v.tensor_tensor(h2_, h1[:, :, 0:2 * e:2], h1[:, :, 1:2 * e:2], ALU.max))
                        step(v.tensor_tensor(m2, h1[:, :, 0:2 * e:2], h1[:, :, 1:2 * e:2], ALU.min))
                        step(v.tensor_tensor(l2, l1[:, :, 0:2 * e:2], l1[:, :, 1:2 * e:2], ALU.max))
                        step(v.tensor_tensor(m2, m2, l2, ALU.max))
                        h1, l1, at = h2_, m2, at + n
                    step(v.tensor_tensor(grp.rearrange("p t g -> p (t g)").unsqueeze(2), h1, l1, ALU.add))

                def choose():
                    other = grp.unsqueeze(2).broadcast_to([P, NT, NGRP, NGRP])
                    own = grp.unsqueeze(3).broadcast_to([P, NT, NGRP, NGRP])
                    a4, b4 = (x.rearrange("p t (g e) -> p t g e", g=NGRP) for x in (ra, rb))
                    low = cst[:, C_LOW:C_LOW + 64].unsqueeze(1).broadcast_to([P, NT, NE])
                    step(v.tensor_tensor(a4, other, own, ALU.is_gt))
                    step(v.tensor_tensor(b4, other, own, ALU.is_equal))
                    step(v.tensor_tensor(rb, rb, low, ALU.mult))
                    step(v.tensor_tensor(ra, ra, rb, ALU.add))
                    step(v.tensor_reduce(gneg, a4, AX.X, ALU.add))
                    step(v.tensor_scalar(gok, gneg, 3.5, None, ALU.is_lt))
                    step(v.tensor_scalar(gneg, gok, 1.0, 1e30, ALU.subtract, ALU.mult))
                    s4 = selm.rearrange("p t (g e) -> p t g e", g=NGRP)
                    step(v.tensor_tensor(s4, sel.rearrange("p t (g e) -> p t g e", g=NGRP),
                                         gok.unsqueeze(3).broadcast_to([P, NT, NGRP, GSZ]), ALU.mult))
                    step(v.tensor_tensor(s4, s4, gneg.unsqueeze(3).broadcast_to([P, NT, NGRP, GSZ]), ALU.add))
                    for t in range(NT):
                        step(v.max(top[:, t, :], selm[:, t, :]))
                        step(v.match_replace(rb[:, t, :], top[:, t, :], selm[:, t, :], -3e38))
                    step(v.tensor_scalar(mask, rb, -2e38, None, ALU.is_lt))
                    step(v.tensor_tensor(ra, scores, mask, ALU.mult))
                    step(v.tensor_reduce(gsum, ra, AX.X, ALU.add))
                    step(v.reciprocal(grec, gsum))
                    step(v.scalar_tensor_tensor(gate, ra, 2.5, grec.unsqueeze(2).broadcast_to([P, NT, NE]), ALU.mult, ALU.mult))
                    step(v.tensor_tensor(mask, mask, cst[:, C_VALID:C_VALID + NT].unsqueeze(2).broadcast_to([P, NT, NE]), ALU.mult))
                    step(v.tensor_copy(maskb, mask))
                    step(v.tensor_copy(trib, cst[:, C_TRI:C_TRI + P]))
                    step(v.tensor_copy(oneb, cst[:, C_ONE:C_ONE + P]))
                    v.sem_inc(s["mask_ok"], 1)

                def running(a, b, width, first):
                    step(v.tensor_copy(a[..., 32:], first))
                    for n in (1, 2, 4, 8, 16, 32):
                        step(v.tensor_tensor(b[..., 32:], a[..., 32:], a[..., 32 - n:width - n], ALU.add))
                        a, b = b, a
                    return a

                def fill_table():
                    total = running(run[0], run[1], 96, mask)
                    v.wait_ge(s["consts_ok"], NT)
                    step(v.tensor_tensor(table[:, :, :, 5], total[..., 32:], mask, ALU.subtract))
                    step(v.tensor_copy(table[:, :, :, 6], gate))
                    step(v.tensor_tensor(ra, gate, table[:, :, :, 6], ALU.subtract))
                    step(v.tensor_copy(table[:, :, :, 7], ra))
                    step(v.tensor_tensor(rb, ra, table[:, :, :, 7], ALU.subtract))
                    step(v.tensor_copy(table[:, :, :, 8], rb))
                    v.sem_inc(s["table_ok"], 1)

                def queues():
                    v.wait_ge(s["cnt_ps"], 1)
                    step(v.tensor_copy(cnt, psum[:, 2, NT * NE:(NT + 1) * NE]))
                    step(v.tensor_scalar(nblk, cnt, 0.0, None, ALU.is_gt))
                    for n in range(1, -(-NTOK // P)):
                        step(v.scalar_tensor_tensor(nblk, cnt, float(n * P), nblk, ALU.is_gt, ALU.add))
                    ends = running(erun[0], erun[1], 96, nblk)[..., 32:]
                    step(v.tensor_tensor(first, ends, nblk, ALU.subtract))
                    step(v.tensor_scalar(first, first, float(P), 1.0, ALU.mult, ALU.add))
                    step(v.tensor_tensor(ra, psum[:, 2, 0:NT * NE].rearrange("p (t e) -> p t e", t=NT),
                                         first.unsqueeze(1).broadcast_to([P, NT, NE]), ALU.add))
                    step(v.tensor_tensor(ra, ra, mask, ALU.mult))
                    step(v.tensor_scalar(gpos, ra, -1.0, None, ALU.add))
                    step(v.tensor_scalar(cnt, ends, cst[:, C_IP:C_IP + 1], None, ALU.is_le))
                    step(v.tensor_reduce(blkf, cnt, AX.X, ALU.add))
                    step(v.tensor_scalar(blkf, blkf, float(NE - 1), None, ALU.min))
                    step(v.tensor_scalar(cnt[:, 0:TRIPS], cst[:, C_TRIP:C_TRIP + TRIPS], ends[:, NE - 1:NE], None, ALU.is_lt))
                    step(v.tensor_reduce(tripf, cnt[:, 0:TRIPS], AX.X, ALU.add))
                    step(v.tensor_copy(tab[0:1, P:P + 1], tripf[0:1, :]))
                    v.sem_inc(s["table_ok"], 1)
                    v.wait_ge(s["tab_ps"], 1)
                    step(v.tensor_copy(tab[0:1, 0:P], psum[0:1, 2, 384:512]))
                    v.sem_inc(s["tab_ok"], 1)

                parts = [groups, choose, fill_table, queues]
                parts[0]()
                for t in range(NT):
                    r = rows(t)
                    v.wait_ge(s["ssil"], t + 1)
                    if t:
                        v.wait_ge(s["dn"], 2 * t)
                    v.tensor_tensor(hid[:, :, 0:r], halves(7 * (t % 2), r)[1], sil[:, :, 0:r], ALU.mult).then_inc(s["shid"], 1)
                    v.wait_ge(s["dn"], 2 * t + 2)
                    v.tensor_copy(ysh[0:r, t, 512:], psum[0:r, 5, :]).then_inc(s["out_v"], 1)
                    if t + 1 < len(parts):
                        parts[t + 1]()
                    if t == 3:
                        for b in range(3):
                            who(v, b, b)
                        for b in range(3):
                            read_list(v, b, b)
                take_rows_v(v, 0, 0)
                nb = trips(v)
                with v.Fori(0, TRIPS) as i:
                    with v.If(nb > i):
                        for u in range(3):
                            b = 3 * i + u
                            v.wait_ge(moved[u], 32 * i + 16)
                            v.tensor_scalar(row[:, u, :], got[:, u, 1:2], float(TOPK * OUTSIDE), None, ALU.add).then_inc(s["now_ok"], 1)
                            v.tensor_copy(now_gate[:, u:u + 1], got[:, u, 2:3]).then_inc(s["now_ok"], 1)
                            v.wait_ge(s["list_mm"], b + 1)
                            who(v, b + 3, u)
                            v.wait_ge(s["sil_ok"], b + 1)
                            v.tensor_tensor(hid, halves(0, P)[1], sil, ALU.mult).then_inc(s["hid_ok"], 1)
                            v.wait_ge(s["now_ok"], 2 * b + 2)
                            read_list(v, b + 3, u)
                            take_rows_v(v, b + 1, (u + 1) % 3)
                            v.wait_ge(s["dn"], 2 * b + 2 + DN0)
                            v.tensor_scalar(out[:, u, 512:], psum[:, 5, :], now_gate[:, u:u + 1], None, ALU.mult).then_inc(s["out_v"], 1)

            @block.tensor
            def _(pe):
                pe.wait_ge(wout_in, 16)
                for t in range(NT + 1):
                    if t < NT:
                        r = rows(t)
                        pe.wait_ge(s["an_ok"], t + 1)
                        if t:
                            pe.wait_ge(s["aT_ok"], t)
                        for c in range(WC):
                            last = pe.transpose(psum[:, 0, c * P:c * P + r], attn[0:r, t, c * P:(c + 1) * P], ident[0:r, 0:r])
                        last.then_inc(s["aT_ps"], 1)
                        if t:
                            pe.wait_ge(s["tc_ok"], t)
                        for n in range(2):
                            for c in range(WC):
                                last = pe.matmul(psum[0:r, 4 + n, :], convg[:, c, t * P:t * P + r],
                                                 wout[:, WC + c, n * 512:(n + 1) * 512], start=(c == 0), stop=(c == WC - 1))
                        last.then_inc(s["prod_c"], 1)
                        if t:
                            pe.wait_ge(s["x2_ok"], t)
                        pe.wait_ge(s["aT_ok"], t + 1)
                        for n in range(2):
                            for c in range(WC):
                                last = pe.matmul(psum[0:r, 2 + n, :], aT[:, t % 2, c, 0:r],
                                                 wout[:, c, n * 512:(n + 1) * 512], start=(c == 0), stop=(c == WC - 1))
                        last.then_inc(s["prod_a"], 1)
                    if t:
                        m = t - 1
                        r = rows(m)
                        pe.wait_ge(s["h2_ok"], m + 1)
                        for half in range(2):
                            if m:
                                pe.wait_ge(s[("h2_a", "h2_v")[half]], m)
                            for k in range(4):
                                kk = 4 * half + k
                                last = pe.transpose(psum[:, 6 + half, k * P:k * P + r],
                                                    work[0:r, 1 + m % 2, kk * P:(kk + 1) * P], ident[0:r, 0:r])
                            last.then_inc(s["h2_ps"], 1)
                        pe.wait_ge(s["h2_a"], m + 1)
                        pe.wait_ge(s["h2_v"], m + 1)
                        if m == 0:
                            pe.wait_ge(s["small_in"], 32)
                        for k in range(KC):
                            last = pe.matmul(psum[0:r, 1, m * NE:(m + 1) * NE], h2T[:, k, m * P:m * P + r], wr[:, k, :],
                                             start=(k == 0), stop=(k == KC - 1))
                        last.then_inc(s["logit"], 1)

                pe.wait_ge(shared_in, 48)
                lhs = lambda t: lambda k: h2T[:, k, t * P:t * P + rows(t)]
                gate_up(pe, 0, P, lhs(0), wslot[0], s["sgu"])
                for t in range(NT):
                    r = rows(t)
                    if t + 1 < NT:
                        if t:
                            pe.wait_ge(s["shid"], t)
                        gate_up(pe, 7 * ((t + 1) % 2), rows(t + 1), lhs(t + 1), wslot[0], s["sgu"])
                    if t == 3:
                        pe.wait_ge(s["table_ok"], 2)
                        pe.transpose(psum[0:1, 2, 384:512], blkf, ident).then_inc(s["tab_ps"], 1)
                    if t == 4:
                        fill_list(pe, 0, 0)
                        fill_list(pe, 1, 1)
                        fill_list(pe, 2, 2)
                    if t == 2:
                        pe.wait_ge(s["mask_ok"], 1)
                        for a in range(NT):
                            for c in range(a + 1):
                                pe.matmul(psum[:, 2, a * NE:(a + 1) * NE], trib if c == a else oneb, maskb[:, c, :],
                                          start=(c == 0), stop=(c == a))
                        for c in range(NT):
                            last = pe.matmul(psum[:, 2, NT * NE:(NT + 1) * NE], oneb, maskb[:, c, :],
                                             start=(c == 0), stop=(c == NT - 1))
                        last.then_inc(s["cnt_ps"], 1)

                    def free(n):
                        if t:
                            pe.wait_ge(s[("out_a", "out_v")[n]], t)

                    pe.wait_ge(s["shid"], t + 1)
                    down(pe, r, wslot[0], s["dn"], free)
                pe.wait_ge(s["tab_ok"], 1)
                turn_rows(pe, 0, 16)
                nb = trips(pe)
                with pe.Fori(0, TRIPS) as i:
                    with pe.If(nb > i):
                        for u in range(3):
                            b = 3 * i + u
                            n1 = (u + 1) % 3
                            w = wslot[n1]
                            pe.wait_ge(w_in[u], 48 * i + 48)
                            pe.wait_ge(s["xt_a"], b + 1)
                            pe.wait_ge(s["xt_v"], b + 1)
                            gate_up(pe, 0, P, lambda k: xT[:, u, k, :], w, s["gu"])
                            fill_list(pe, b + 3, u)
                            turn_rows(pe, n1, 32 * i + (16 if u < 2 else 48))
                            pe.wait_ge(s["hid_ok"], b + 1)
                            down(pe, P, w, s["dn"], lambda n: pe.wait_ge(s[("out_a", "out_v")[n]], b + NT))
        stage_4(x2, ysh, h2T[:, :, :].rearrange("p k n -> p (k n)"), work)
        st.close()

    def stage_4(x2, ysh, room, work):
        gate2 = room[:, 0:2 * D].rearrange("p (a n) -> p a n", a=2)
        gfin = room[:, 2 * D:3 * D]
        ss = room[:, 3 * D:3 * D + 3 * NT].rearrange("p (a t) -> p a t", a=3)
        ring = stream[:, 0:3 * TOPK * D].rearrange("p (s k n) -> p s k n", s=3, k=TOPK)
        H = TOPK // 2
        bc_in, sums, sum_read, y_ok, ms, rs = (sem(f"s4_{n}") for n in ("bc_in", "sums", "sum_read", "y_ok", "ms", "rs"))
        first_in = [sem(f"s4_first{i}") for i in range(3)]
        second_in = [sem(f"s4_second{i}") for i in range(3)]
        y_out = [sem(f"s4_y_out{i}") for i in range(2)]
        v_step = sem("s4_v_step")
        rows_of = expert_rows.rearrange("(n k) d -> n k d", k=TOPK)

        with nc.Block() as block:
            @block.sync
            def _(sp):
                sp.dma_start(gate2[:, 0, :], bc_row(mod_rows[0:1, 5 * D:], P)).then_inc(bc_in, 16)
                sp.dma_start(gate2[0:NS, 1, :], mod_sample(5)).then_inc(bc_in, 16)
                sp.dma_start(gfin, bc_row(io["g_final"].unsqueeze(0), P)).then_inc(bc_in, 16)
                for t in range(NT):
                    r = rows(t)
                    if t >= 3:
                        sp.wait_ge(y_ok, t - 2)
                    for a, signal in ((0, first_in), (H, second_in)):
                        sp.dma_start(ring[0:r, t % 3, a:a + H, :],
                                     rows_of[t * P:t * P + r, a:a + H, :]).then_inc(signal[t % 3], 16)
                sp.wait_ge(stored, 16 * n_stores[0])

            @block.gpsimd
            def _(pool):
                for t in range(NT):
                    r = rows(t)
                    pool.wait_ge(ms, t + 1)
                    pool.tensor_tensor(ss[0:r, 2, t:t + 1], ss[0:r, 1, t:t + 1], cst[0:r, C_POW:C_POW + 1], ALU.pow).then_inc(rs, 1)

            @block.scalar
            def _(act):
                for t in range(NT):
                    act.wait_ge(y_ok, t + 1)
                    dst = (io["y_prompt"][0, t * P:(t + 1) * P, :] if t < NPT else
                           io["y_sample"].rearrange("b t n -> (b t) n"))
                    act.dma_start(dst, work[0:rows(t), t % 2, :]).then_inc(y_out[t % 2], 16)
                act.wait_ge(y_out[0], 3 * 16)
                act.wait_ge(y_out[1], 2 * 16)

            @block.tensor
            def _(pe):
                for t in range(NT):
                    r = rows(t)
                    pe.wait_ge(first_in[t % 3], 16 * (t // 3 + 1))
                    if t >= 2:
                        pe.wait_ge(sum_read, t - 1)
                    for n in range(2):
                        cols = slice(n * 512, (n + 1) * 512)
                        pe.matmul(psum[0:r, 2 * (t % 2) + n, :], ident[0:r, 0:r], ysh[0:r, t, cols], start=True, stop=False)
                        for k in range(H):
                            last = pe.matmul(psum[0:r, 2 * (t % 2) + n, :], ident[0:r, 0:r], ring[0:r, t % 3, k, cols],
                                             start=False, stop=(k == H - 1))
                    last.then_inc(sums, 1)

            @block.vector
            def _(v):
                n_step = [0]

                def step(ins):
                    n_step[0] += 1
                    ins.then_inc(v_step, 1)
                    v.wait_ge(v_step, n_step[0])

                for t in range(NT):
                    r, b = rows(t), 2 * (t % 2)
                    y = work[0:r, t % 2, :]
                    v.wait_ge(second_in[t % 3], 16 * (t // 3 + 1))
                    if t >= 2:
                        v.wait_ge(y_out[t % 2], 16 * (t // 2))
                    step(v.tensor_tensor(y, ring[0:r, t % 3, H, :], ring[0:r, t % 3, H + 1, :], ALU.add))
                    for k in range(H + 2, TOPK):
                        step(v.tensor_tensor(y, y, ring[0:r, t % 3, k, :], ALU.add))
                    v.wait_ge(sums, t + 1)
                    step(v.tensor_tensor(y, psum[0:r, b:b + 2, :].rearrange("p a n -> p (a n)"), y, ALU.add))
                    v.sem_inc(sum_read, 1)
                    if t == 0:
                        v.wait_ge(bc_in, 48)
                    step(v.tensor_tensor(y, y, gate2[0:r, t // NPT, :], ALU.mult))
                    step(v.tensor_tensor(x2[0:r, t, :], x2[0:r, t, :], y, ALU.add))
                    step(v.tensor_tensor_reduce(y, x2[0:r, t, :], x2[0:r, t, :], 1.0, 0.0, ALU.mult, ALU.add, ss[0:r, 0, t:t + 1]))
                    step(v.tensor_scalar(ss[0:r, 1, t:t + 1], ss[0:r, 0, t:t + 1], 1.0 / D, EPS, ALU.mult, ALU.add))
                    v.sem_inc(ms, 1)
                    v.wait_ge(rs, t + 1)
                    v.scalar_tensor_tensor(y, x2[0:r, t, :], ss[0:r, 2, t:t + 1], gfin[0:r], ALU.mult, ALU.mult).then_inc(y_ok, 1)

    kv = ExitStack()
    keeps = {n: kv.enter_context(nc.sbuf_tensor("sb_" + n, [P, NT, W], F32)) for n in "kv"}
    stage_1()
    stage_2()
    kv.close()
    stage_3()
    ctx.close()


_INS = ['x_prompt', 'x_sample', 'c_prompt', 'c_sample', 'cache_k', 'cache_v', 'state_conv', 'w_ada', 'b_ada',
        'w_in', 'conv_w', 'g_attn_out', 'g_conv_out', 'w_out', 'w_router', 'router_bias', 'w_exp_gate',
        'w_exp_up', 'w_exp_down', 'w_sh_gate', 'w_sh_up', 'w_sh_down', 'g_final']
_OUTS = {'y_prompt': (1, SEQ, D), 'y_sample': (DEC_B, DEC_T, D),
         'k_prompt': (1, 1, SEQ, HEADS, HD), 'v_prompt': (1, 1, SEQ, HEADS, HD), 'conv_prompt': (1, 1, 2, W),
         'k_sample': (1, DEC_B, DEC_T, HEADS, HD), 'v_sample': (1, DEC_B, DEC_T, HEADS, HD),
         'conv_sample': (1, DEC_B, 2, W)}


def build(nc, shapes):
    io = {n: nc.dram_tensor(n, s, F32, kind="ExternalInput").ap() for n, s in shapes.items()}
    io |= {n: nc.dram_tensor(n, s, F32, kind="ExternalOutput").ap() for n, s in _OUTS.items()}
    layer(nc, io)


def kernel(**inputs):
    import concourse.bacc as bacc
    from concourse.bass_utils import run_bass_kernel_spmd

    arrays = {n: np.ascontiguousarray(inputs[n]) for n in _INS}
    for n, a in zip(("cst", "masks", "rope"), constants()):
        arrays[n] = a
    nc = bacc.Bacc("TRN2", target_bir_lowering=False, num_devices=1)
    build(nc, {n: a.shape for n, a in arrays.items()})
    r = run_bass_kernel_spmd(nc, [arrays], core_ids=[0])
    return tuple(r.results[0][n] for n in _OUTS)
```

```python
import numpy as np
from contextlib import ExitStack

import concourse.bass as bass
from concourse import mybir

F32 = mybir.dt.float32
BF16 = mybir.dt.bfloat16
I32 = mybir.dt.int32
U32 = mybir.dt.uint32
ALU = mybir.AluOpType
ACT = mybir.ActivationFunctionType
AX = mybir.AxisListType

P = 128
D = 1024
KC = D // P
SEQ, DEC_B, DEC_T = 512, 8, 4
NS = DEC_B * DEC_T
NTOK = SEQ + NS
NPT = SEQ // P
NT = NPT + 1
HEADS, HD = 8, 64
W = HEADS * HD
WC = W // P
PAST, WIN = 2048, 512
WIN0 = PAST - WIN
SPARSE = WIN0 // 16
SK = WIN + 4 * SPARSE + NS
NE, TOPK, NGRP, GSZ = 64, 8, 8, 8
FE = 256
EPS = 1e-6
NADA, NIN = 12, 6
MAXB = (NTOK * TOPK + NE * (P - 1)) // P
TRIPS = -(-MAXB // 3)
OUTSIDE = 8192
BRANCHES = ((128, 1), (512, 4), (2048, 16))

C_ID, C_IOTA, C_BASE, C_TRI, C_ONE = 0, 128, 256, 384, 512
C_LOW, C_VALID, C_IP, C_TRIP, C_LP = 640, 704, 709, 710, 743
C_POW = C_LP + NT * 5
C_END = C_POW + 1
A_PM, A_PN = 0, 512
A_SM = 1024
A_SN = A_SM + 2 * SK
A_BD = A_SN + 2 * SK
A_SEL = A_BD + W
A_END = A_SEL + 2 * NS


def rows(t):
    return P if t < NPT else NS


def branch_count(dist):
    n = np.zeros(dist.shape, np.float32)
    for w, d in BRANCHES:
        n += (dist >= 0) & (dist <= w) & (dist % d == 0)
    return n


def constants():
    p = np.arange(P)
    c = np.zeros((P, C_END), np.float32)
    c[:, C_ID:C_ID + P] = np.eye(P)
    c[:, C_IOTA:C_IOTA + P] = p[None]
    c[:, C_BASE:C_BASE + P] = P * p[None]
    c[:, C_TRI:C_TRI + P] = p[:, None] < p[None]
    c[:, C_ONE:C_ONE + P] = 1
    g = np.arange(NGRP)
    c[:, C_LOW:C_LOW + 64] = (g[None] < g[:, None]).ravel()[None]
    for t in range(NT):
        c[:, C_VALID + t] = p < rows(t)
        c[:, C_LP + 5 * t + 0] = p
        c[:, C_LP + 5 * t + 1] = P * t - OUTSIDE
        c[:, C_LP + 5 * t + 3] = TOPK * p
        c[:, C_LP + 5 * t + 4] = TOPK * (P * t - OUTSIDE)
    c[:, C_POW] = -0.5
    c[:, C_IP] = p
    c[:, C_TRIP:C_TRIP + TRIPS] = 3 * np.arange(TRIPS)[None]

    a = np.zeros((P, A_END), np.float32)
    for n, diff in enumerate(range(NPT - 1, -1, -1)):
        m = branch_count(P * diff + p[:, None] - p[None])
        a[:, A_PM + n * P:A_PM + (n + 1) * P] = m
    a[:, A_PN:A_PN + 512] = np.where(a[:, A_PM:A_PM + 512] > 0, 0, -1e30)
    pos = np.concatenate([(WIN0 + 4 * p[None] + np.arange(4)[:, None]).ravel(),
                          (16 * np.arange(SPARSE)[None] + np.arange(4)[:, None]).ravel()])
    q = p % DEC_T
    for grp in range(2):
        m = np.zeros((P, SK), np.float32)
        m[:, :len(pos)] = branch_count(PAST + q[:, None] - pos[None])
        batch = 4 * grp + p // 32
        kb, kt = np.arange(NS) // DEC_T, np.arange(NS) % DEC_T
        m[:, len(pos):] = branch_count(q[:, None] - kt[None]) * (kb[None] == batch[:, None])
        a[:, A_SM + grp * SK:A_SM + (grp + 1) * SK] = m
        a[:, A_SN + grp * SK:A_SN + (grp + 1) * SK] = np.where(m > 0, 0, -1e30)
        a[:, A_SEL + grp * NS:A_SEL + (grp + 1) * NS] = (batch * DEC_T + q)[:, None] == np.arange(NS)[None]
    a[:, A_BD:A_BD + W] = (np.arange(W)[None] // HD) == ((p % 32) // DEC_T)[:, None]

    half = HD // 2
    inv = (np.float32(10000.0) ** (-np.arange(half, dtype=np.float32) / np.float32(half))).astype(np.float32)
    where = np.zeros((NT, P), np.float32)
    where[:NPT] = np.arange(SEQ).reshape(NPT, P)
    where[NPT, :NS] = PAST + np.arange(NS) % DEC_T
    ang = (where[:, :, None] * inv[None, None]).astype(np.float32)
    cos, sin = np.cos(ang).astype(np.float32), np.sin(ang).astype(np.float32)
    r = np.concatenate([np.concatenate([cos, cos], -1), np.concatenate([-sin, sin], -1)], 0)
    r = np.ascontiguousarray(r.transpose(1, 0, 2).reshape(P, 2 * NT * HD))
    return c, a, r


def layer(nc, io):
    ctx = ExitStack()

    def sem(name):
        return ctx.enter_context(nc.semaphore(name))

    def keep(name, shape, dt=F32):
        return ctx.enter_context(nc.sbuf_tensor("sb_" + name, shape, dt))

    psum = ctx.enter_context(nc.psum_tensor("psum", [P, 8, 512], F32))

    mod_rows = nc.dram_tensor("mod_rows", (1 + DEC_B, 6 * D), F32, kind="Internal").ap()
    h_rows = nc.dram_tensor("h_rows", (NTOK, D), F32, kind="Internal").ap()
    expert_rows = nc.dram_tensor("expert_rows", (NTOK * TOPK, D), F32, kind="Internal").ap()

    cst = keep("cst", [P, C_END])
    stream = keep("stream", [P, 96 * 256])
    convg = keep("convg", [P, WC, NTOK])
    conv_r = keep("conv_r", [P, NT])
    attn = keep("attn", [P, NT, W])
    gains = keep("gains", [P, 2, WC])
    ident = cst[:, C_ID:C_ID + P]

    stored = sem("stored")
    n_stores = [0]

    def store(eng, dst, src):
        n_stores[0] += 1
        return eng.dma_start(dst, src).then_inc(stored, 16)

    def bc_row(ap_row, n):
        return ap_row.broadcast_to([n, ap_row.shape[1]])

    def mod_sample(j):
        return mod_rows[1:1 + DEC_B, j * D:(j + 1) * D].unsqueeze(1).broadcast_to([DEC_B, DEC_T, D])

    last_in = sem("last_in")

    def stage_1():
        st = ExitStack()

        def tmp(name, shape, dt=F32):
            return st.enter_context(nc.sbuf_tensor("sb_" + name, shape, dt))

        k_sb, v_sb = keeps["k"], keeps["v"]
        q_sb = attn
        xh = tmp("xh", [P, NT, D])
        hT = tmp("hT", [P, KC, NTOK])
        bc_shift = tmp("bc_shift", [P, 2, D])
        bc_scale = tmp("bc_scale", [P, 2, D])
        up = tmp("up", [P, WC, 2 + SEQ])
        us = tmp("us", [P, WC, DEC_B, 2 + DEC_T])
        rope = tmp("rope", [P, 2, NT, HD])
        rot = tmp("rot", [P, 2, W])
        c_sb = hT[0:1 + DEC_B, :, :].rearrange("p k n -> p (k n)")[:, 0:D]
        cT = tmp("cT", [P, KC, 1 + DEC_B])
        c_flat = cT[:, :, :].rearrange("p k n -> p (k n)")
        c_tmp = [rot[:, 0, n * 128:n * 128 + KC * 9] for n in range(3)]
        convw = tmp("convw", [P, 3, WC])
        rest = 4 * 4096 + 6 * D
        state = stream[0:2 * DEC_B, rest:rest + W]
        ss = tmp("ss", [P, 2, NT])
        cs = tmp("cs", [P, NT])
        tail = tmp("tail", [P, WC, 2 + 2 * DEC_B])
        tail_rows = stream[0:2 + 2 * DEC_B, rest + W:rest + 2 * W]
        ring = stream[:, 0:4 * 4096].rearrange("p (s k n) -> p s k n", s=4, k=KC)
        mod = stream[0:1 + DEC_B, 4 * 4096:4 * 4096 + 6 * D]
        flat = xh[:, :, :].rearrange("p t n -> p (t n)")
        hcT = flat[:, 0:WC * NTOK].rearrange("p (c n) -> p c n", c=WC)
        convT = flat[:, WC * NTOK:2 * WC * NTOK].rearrange("p (c n) -> p c n", c=WC)

        w_in = [sem(f"s1_w{i}") for i in range(4)]
        w_used = sem("s1_w_used")
        cst_in, c_in, bias_in, x_in, small_in = (sem(f"s1_{n}") for n in
                                                 ("cst_in", "c_in", "bias_in", "x_in", "small_in"))
        c_exp, cT_ps, cT_ok = (sem(f"s1_{n}") for n in ("c_exp", "cT_ps", "cT_ok"))
        mod_ok, mod_out, bc_in = (sem(f"s1_{n}") for n in ("mod_ok", "mod_out", "bc_in"))
        h_ok, hT_ps, hT_a, hT_v = (sem(f"s1_{n}") for n in ("h_ok", "hT_ps", "hT_a", "hT_v"))
        proj, qk_ok, v_ok = (sem(f"s1_{n}") for n in ("proj", "qk_ok", "v_ok"))
        cmm, hc_ok, gcb_ok = (sem(f"s1_{n}") for n in ("cmm", "hc_ok", "gcb_ok"))
        st_ps, st_ok, pads = (sem(f"s1_{n}") for n in ("st_ps", "st_ok", "pads"))
        sq_ok, ssq_ps, tail_ok, tail_ps, tail_sb = (sem(f"s1_{n}") for n in
                                                    ("sq_ok", "ssq_ps", "tail_ok", "tail_ps", "tail_sb"))
        ms_ok, cms_ok, rs_ok = (sem(f"s1_{n}") for n in ("ms_ok", "cms_ok", "rs_ok"))
        v_step = sem("s1_v_step")

        order = [3, 5, 4, 0, 1, 2]

        with nc.Block() as block:
            @block.sync
            def _(sp):
                sp.dma_start(c_sb[0:1, :], io["c_prompt"]).then_inc(c_in, 16)
                sp.dma_start(c_sb[1:, :], io["c_sample"]).then_inc(c_in, 16)
                sp.dma_start(cst[:, :], io["cst"]).then_inc(cst_in, 16)
                for n in range(NADA + NIN):
                    if n >= 4:
                        if n - 4 < NADA:
                            sp.wait_ge(w_used, n - 3)
                        else:
                            sp.wait_ge(cmm, WC * (n - 3 - NADA))
                    src = (io["w_ada"][0][:, n * 512:(n + 1) * 512] if n < NADA else
                           io["w_in"][0][:, order[n - NADA] * W:(order[n - NADA] + 1) * W])
                    sp.dma_start(ring[:, n % 4], src.rearrange("(k p) n -> p k n", p=P)).then_inc(w_in[n % 4], 16)
                sp.wait_ge(qk_ok, 2 * NT)
                sp.wait_ge(v_ok, NT)
                for name, src in (("k", k_sb), ("v", v_sb)):
                    store(sp, io[name + "_prompt"].rearrange("a b (t p) h d -> p (a b t) (h d)", p=P), src[:, 0:NPT, :])
                    store(sp, io[name + "_sample"].rearrange("a b t h d -> (a b t) (h d)"), src[0:NS, NPT, :])
                sp.wait_ge(tail_sb, 1)
                store(sp, io["conv_prompt"].rearrange("a b t n -> (a b t) n"), tail_rows[0:2, :])
                store(sp, io["conv_sample"].rearrange("a b t n -> (a b t) n"), tail_rows[2:, :])

            @block.gpsimd
            def _(pool):
                pool.memset(v_sb[:, NPT, :], 0.0).then_inc(pads, 1)
                pool.memset(up[:, :, 0:2], 0.0).then_inc(pads, 1)
                pool.dma_start(rope[:, :, :, :], io["rope"].rearrange("p (a t n) -> p a t n", a=2, t=NT)).then_inc(small_in, 16)
                pool.dma_start(state[:, :], io["state_conv"].rearrange("a b t n -> (a b t) n")).then_inc(small_in, 16)
                for j in range(3):
                    pool.dma_start(convw[:, j, :], io["conv_w"][0, j].rearrange("(c p) -> p c", p=P),
                                   allow_slow_non_contiguous=True).then_inc(small_in, 16)
                for j, g in enumerate(("g_attn_out", "g_conv_out")):
                    pool.dma_start(gains[:, j, :], io[g][0].rearrange("(c p) -> p c", p=P),
                                   allow_slow_non_contiguous=True).then_inc(small_in, 16)
                pool.wait_ge(cst_in, 16)
                for ready, dst, src in ((ms_ok, ss[:, 0], ss[:, 1]), (cms_ok, conv_r, cs)):
                    pool.wait_ge(ready, 1)
                    for r, a, b in ((P, 0, NPT), (NS, NPT, NT)):
                        pool.tensor_tensor(dst[0:r, a:b], src[0:r, a:b], cst[0:r, C_POW:C_POW + 1].broadcast_to([r, b - a]), ALU.pow).then_inc(rs_ok, 1)
                pool.wait_ge(rs_ok, 4)

            @block.scalar
            def _(act):
                act.dma_start(mod, bc_row(io["b_ada"], 1 + DEC_B)).then_inc(bias_in, 16)
                act.wait_ge(cT_ps, 1)
                act.activation(c_tmp[0], psum[:, 0, 0:KC * 9], ACT.Exp, scale=-1.0).then_inc(c_exp, 1)
                act.dma_start(xh[:, 0:NPT, :], io["x_prompt"][0].rearrange("(t p) n -> p t n", p=P)).then_inc(x_in, 16)
                act.dma_start(xh[0:NS, NPT, :], io["x_sample"].rearrange("b t n -> (b t) n")).then_inc(x_in, 16)
                for n in range(NADA):
                    act.wait_ge(mod_ok, n + 1)
                    act.dma_start(mod_rows[:, n * 512:(n + 1) * 512], mod[:, n * 512:(n + 1) * 512]).then_inc(mod_out, 16)
                    if n == 3:
                        act.wait_ge(mod_out, 64)
                        for j, dst in ((0, bc_shift), (1, bc_scale)):
                            act.dma_start(dst[:, 0, :], bc_row(mod_rows[0:1, j * D:(j + 1) * D], P)).then_inc(bc_in, 16)
                            act.dma_start(dst[0:NS, 1, :], mod_sample(j)).then_inc(bc_in, 16)
                for t in range(NT):
                    act.wait_ge(hT_ps, 2 * t + 1)
                    act.copy(hT[:, 0:4, t * P:t * P + rows(t)],
                             psum[:, 3 + (2 * t) % 4, :].rearrange("p (k n) -> p k n", k=4)[:, :, 0:rows(t)]).then_inc(hT_a, 1)
                for m in range(WC):
                    act.wait_ge(cmm, m + 1)
                    act.copy(hcT[:, m, 0:SEQ], psum[:, 3 + m % 2, :])
                    act.copy(hcT[:, m, SEQ:], psum[:, 5 + m % 2, 0:NS]).then_inc(hc_ok, 1)
                act.wait_ge(small_in, 7 * 16)
                for m in range(WC):
                    act.wait_ge(gcb_ok, WC + m + 1)
                    act.activation(hcT[:, m, :], convT[:, m, :], ACT.Square).then_inc(sq_ok, 1)
                    act.activation(convg[:, m, :], convT[:, m, :], ACT.Copy, scale=gains[:, 1, m:m + 1]).then_inc(sq_ok, 1)
                act.wait_ge(pads, 1)
                for t in range(NT):
                    act.wait_ge(proj, 2 * NT + t + 1)
                    act.copy(v_sb[0:rows(t), t, :], psum[0:rows(t), (2 * NT + t) % 3, :]).then_inc(v_ok, 1)
                act.wait_ge(mod_out, NADA * 16)

            @block.vector
            def _(v):
                n_step = [0]

                def step(ins):
                    n_step[0] += 1
                    ins.then_inc(v_step, 1)

                def settle():
                    v.wait_ge(v_step, n_step[0])

                v.wait_ge(c_exp, 1)
                step(v.tensor_scalar(c_tmp[1], c_tmp[0], 1.0, None, ALU.add))
                settle()
                step(v.reciprocal(c_tmp[2], c_tmp[1]))
                settle()
                step(v.tensor_tensor(c_flat, c_tmp[2], psum[:, 0, 0:KC * 9], ALU.mult))
                settle()
                v.sem_inc(cT_ok, 1)
                v.wait_ge(bias_in, 16)
                for n in range(NADA):
                    v.wait_ge(w_used, n + 1)
                    v.tensor_tensor(mod[:, n * 512:(n + 1) * 512], psum[0:9, 1 + n % 2, :],
                                    mod[:, n * 512:(n + 1) * 512], ALU.add).then_inc(mod_ok, 1)
                    if n == 1:
                        v.wait_ge(x_in, 32)
                        for t in range(NT):
                            r = rows(t)
                            settle()
                            step(v.tensor_tensor_reduce(rot[0:r, :, :].rearrange("p a n -> p (a n)"), xh[0:r, t, :], xh[0:r, t, :],
                                                        1.0, 0.0, ALU.mult, ALU.add, ss[0:r, 0, t:t + 1]))
                    if n == 2:
                        settle()
                        for r, a, b in ((P, 0, NPT), (NS, NPT, NT)):
                            step(v.tensor_scalar(ss[0:r, 1, a:b], ss[0:r, 0, a:b], 1.0 / D, EPS, ALU.mult, ALU.add))
                        settle()
                        v.sem_inc(ms_ok, 1)
                    if n == 6:
                        v.wait_ge(rs_ok, 2)
                        v.wait_ge(bc_in, 64)
                        step(v.tensor_scalar(bc_scale[:, 0, :], bc_scale[:, 0, :], 1.0, None, ALU.add))
                        step(v.tensor_scalar(bc_scale[0:NS, 1, :], bc_scale[0:NS, 1, :], 1.0, None, ALU.add))
                    if n > 6:
                        t = n - 7
                        r, s = rows(t), t // NPT
                        settle()
                        step(v.scalar_tensor_tensor(xh[0:r, t, :], xh[0:r, t, :], ss[0:r, 0, t:t + 1],
                                                    bc_scale[0:r, s, :], ALU.mult, ALU.mult))
                        settle()
                        v.tensor_tensor(xh[0:r, t, :], xh[0:r, t, :], bc_shift[0:r, s, :], ALU.add).then_inc(h_ok, 1)
                for t in range(NT):
                    v.wait_ge(hT_ps, 2 * t + 2)
                    v.tensor_copy(hT[:, 4:8, t * P:t * P + rows(t)],
                                  psum[:, 3 + (2 * t + 1) % 4, :].rearrange("p (k n) -> p k n", k=4)[:, :, 0:rows(t)]).then_inc(hT_v, 1)
                v.wait_ge(small_in, 7 * 16)
                v.wait_ge(st_ps, 1)
                v.tensor_copy(us[:, :, :, 0:2], psum[:, 7, 0:64].rearrange("p (c b i) -> p c b i", c=WC, b=DEC_B)).then_inc(st_ok, 1)
                v.wait_ge(pads, 2)
                v.wait_ge(st_ok, 1)
                for m in range(WC):
                    v.wait_ge(cmm, WC + m + 1)
                    v.wait_ge(hc_ok, m + 1)
                    uss = us[:, m, :, :]
                    b = (WC + m) % 2
                    step(v.tensor_tensor(up[:, m, 2:], psum[:, 3 + b, :], hcT[:, m, 0:SEQ], ALU.mult))
                    step(v.tensor_tensor(uss[:, :, 2:], psum[:, 5 + b, 0:NS].rearrange("p (b t) -> p b t", b=DEC_B),
                                         hcT[:, m, SEQ:].rearrange("p (b t) -> p b t", b=DEC_B), ALU.mult))
                    settle()
                    v.sem_inc(gcb_ok, 1)
                    cp = convT[:, m, 0:SEQ]
                    cq = convT[:, m, SEQ:].rearrange("p (b t) -> p b t", b=DEC_B)
                    for j in range(3):
                        wj = convw[:, j, m:m + 1]
                        if j == 0:
                            step(v.tensor_scalar(cp, up[:, m, 0:SEQ], wj, None, ALU.mult))
                            step(v.tensor_scalar(cq, uss[:, :, 0:DEC_T], wj, None, ALU.mult))
                        else:
                            settle()
                            step(v.scalar_tensor_tensor(cp, up[:, m, j:j + SEQ], wj, cp, ALU.mult, ALU.add))
                            step(v.scalar_tensor_tensor(cq, uss[:, :, j:j + DEC_T], wj, cq, ALU.mult, ALU.add))
                step(v.tensor_copy(tail[:, :, 0:2], up[:, :, SEQ:SEQ + 2]))
                step(v.tensor_copy(tail[:, :, 2:].rearrange("p c (b i) -> p c b i", b=DEC_B), us[:, :, :, DEC_T:]))
                settle()
                v.sem_inc(tail_ok, 1)
                for m in range(WC):
                    v.wait_ge(cmm, 2 * WC + m + 1)
                    b = (2 * WC + m) % 2
                    step(v.tensor_tensor(convT[:, m, 0:SEQ], psum[:, 3 + b, :], convT[:, m, 0:SEQ], ALU.mult))
                    step(v.tensor_tensor(convT[:, m, SEQ:], psum[:, 5 + b, 0:NS], convT[:, m, SEQ:], ALU.mult))
                    settle()
                    v.sem_inc(gcb_ok, 1)
                for j, dst in ((0, q_sb), (1, k_sb)):
                    if j == 1:
                        v.wait_ge(tail_ps, 1)
                        v.tensor_copy(tail_rows[:, :], psum[0:18, 3, :]).then_inc(tail_sb, 1)
                        v.wait_ge(ssq_ps, 1)
                        for r, a, b in ((P, 0, NPT), (NS, NPT, NT)):
                            step(v.tensor_scalar(cs[0:r, a:b], psum[0:r, 7, 64 + a:64 + b], 1.0 / W, EPS, ALU.mult, ALU.add))
                        settle()
                        v.sem_inc(cms_ok, 1)
                    for t in range(NT):
                        r, n = rows(t), j * NT + t
                        v.wait_ge(proj, n + 1)
                        src = psum[0:r, n % 3, :].rearrange("p (h d) -> p h d", h=HEADS)
                        ra = rot[0:r, 0, :].rearrange("p (h d) -> p h d", h=HEADS)
                        rb = rot[0:r, 1, :].rearrange("p (h d) -> p h d", h=HEADS)
                        cos = rope[0:r, 0, t, :].unsqueeze(1).broadcast_to([r, HEADS, HD])
                        sin = rope[0:r, 1, t, :].unsqueeze(1).broadcast_to([r, HEADS, HD])
                        h = HD // 2
                        settle()
                        step(v.tensor_tensor(ra, src, cos, ALU.mult))
                        step(v.tensor_tensor(rb[:, :, 0:h], src[:, :, h:], sin[:, :, 0:h], ALU.mult))
                        step(v.tensor_tensor(rb[:, :, h:], src[:, :, 0:h], sin[:, :, h:], ALU.mult))
                        settle()
                        n_step[0] += 1
                        v.tensor_tensor(dst[0:r, t, :], rot[0:r, 0, :], rot[0:r, 1, :], ALU.add).then_inc(v_step, 1)
                        settle()
                        v.sem_inc(qk_ok, 1)

            @block.tensor
            def _(pe):
                pe.wait_ge(cst_in, 16)
                pe.wait_ge(c_in, 32)
                for k in range(KC):
                    last = pe.transpose(psum[:, 0, 9 * k:9 * k + 9], c_sb[:, k * P:(k + 1) * P], ident[0:9, 0:9])
                last.then_inc(cT_ps, 1)
                pe.wait_ge(cT_ok, 1)
                for n in range(NADA):
                    pe.wait_ge(w_in[n % 4], 16 * (n // 4 + 1))
                    if n >= 2:
                        pe.wait_ge(mod_ok, n - 1)
                    for k in range(KC):
                        last = pe.matmul(psum[0:9, 1 + n % 2, :], cT[:, k, :], ring[:, n % 4, k, :],
                                         start=(k == 0), stop=(k == KC - 1))
                    last.then_inc(w_used, 1)
                pe.wait_ge(small_in, 7 * 16)
                for m in range(WC):
                    last = pe.transpose(psum[:, 7, 16 * m:16 * m + 16], state[:, m * P:(m + 1) * P], ident[0:16, 0:16])
                last.then_inc(st_ps, 1)
                for t in range(NT):
                    r = rows(t)
                    pe.wait_ge(h_ok, t + 1)
                    for half in range(2):
                        i = 2 * t + half
                        if i >= 4:
                            pe.wait_ge((hT_a, hT_v)[half], t - 1)
                        for k in range(4):
                            kk = 4 * half + k
                            last = pe.transpose(psum[:, 3 + i % 4, k * P:k * P + r], xh[0:r, t, kk * P:(kk + 1) * P],
                                                ident[0:r, 0:r])
                        last.then_inc(hT_ps, 1)
                pe.wait_ge(mod_ok, NADA)
                pe.wait_ge(hT_a, NT)
                pe.wait_ge(hT_v, NT)
                for j in range(3):
                    n = NADA + j
                    pe.wait_ge(w_in[n % 4], 16 * (n // 4 + 1))
                    for m in range(WC):
                        i = j * WC + m
                        if i >= 2:
                            if i - 2 < WC:
                                pe.wait_ge(hc_ok, i - 1)
                            else:
                                pe.wait_ge(gcb_ok, i - 1 - WC)
                        for k in range(KC):
                            pe.matmul(psum[:, 3 + i % 2, :], ring[:, n % 4, k, m * P:(m + 1) * P], hT[:, k, 0:SEQ],
                                      start=(k == 0), stop=(k == KC - 1))
                            last = pe.matmul(psum[:, 5 + i % 2, 0:NS], ring[:, n % 4, k, m * P:(m + 1) * P], hT[:, k, SEQ:],
                                             start=(k == 0), stop=(k == KC - 1))
                        last.then_inc(cmm, 1)
                for j in range(3):
                    n = NADA + 3 + j
                    pe.wait_ge(w_in[n % 4], 16 * (n // 4 + 1))
                    if j == 1:
                        pe.wait_ge(tail_ok, 1)
                        pe.wait_ge(gcb_ok, 2 * WC)
                        for m in range(WC):
                            last = pe.transpose(psum[0:18, 3, m * P:(m + 1) * P], tail[:, m, :], ident)
                        last.then_inc(tail_ps, 1)
                        pe.wait_ge(sq_ok, 2 * WC)
                        for t in range(NT):
                            for m in range(WC):
                                last = pe.matmul(psum[0:rows(t), 7, 64 + t:65 + t], hcT[:, m, t * P:t * P + rows(t)],
                                                 cst[:, C_ONE:C_ONE + 1], start=(m == 0), stop=(m == WC - 1))
                        last.then_inc(ssq_ps, 1)
                    for t in range(NT):
                        i, r = j * NT + t, rows(t)
                        if i >= 3:
                            if i - 3 < 2 * NT:
                                pe.wait_ge(qk_ok, i - 2)
                            else:
                                pe.wait_ge(v_ok, i - 2 - 2 * NT)
                        for k in range(KC):
                            last = pe.matmul(psum[0:r, i % 3, :], hT[:, k, t * P:t * P + r], ring[:, n % 4, k, :],
                                             start=(k == 0), stop=(k == KC - 1))
                        last.then_inc(proj, 1)

        st.close()

    wout_in, shared_in = sem("wout_in"), sem("shared_in")

    def load_expert(eng, dst, gate, up_, down, signal):
        gu = dst[:, 0:KC * 2 * FE].rearrange("p (k n) -> p k n", k=KC)
        eng.dma_start(gu[:, :, 0:FE], gate.rearrange("(k p) n -> p k n", p=P)).then_inc(signal, 16)
        eng.dma_start(gu[:, :, FE:], up_.rearrange("(k p) n -> p k n", p=P)).then_inc(signal, 16)
        eng.dma_start(dst[:, KC * 2 * FE:].rearrange("p (k n) -> p k n", k=2),
                      down.rearrange("(k p) n -> p k n", p=P)).then_inc(signal, 16)

    def stage_2():
        st = ExitStack()

        def tmp(name, shape, dt=F32):
            return st.enter_context(nc.sbuf_tensor("sb_" + name, shape, dt))

        k_sb, v_sb = keeps["k"], keeps["v"]
        q_sb = attn
        masks = tmp("masks", [P, A_END])
        qT = tmp("qT", [P, WC, SEQ])
        kT = tmp("kT", [P, WC, SEQ])
        kTn = tmp("kTn", [P, WC, NS])
        qz = tmp("qz", [P, WC, DEC_B, HEADS * DEC_T])
        probs = tmp("probs", [P, 3, SEQ])
        pT = tmp("pT", [P, 2, SEQ])
        nmax = tmp("nmax", [P, NPT * HEADS])
        den = tmp("den", [P, NPT * HEADS])
        rden = tmp("rden", [P, NPT * HEADS])
        KTs = tmp("KTs", [P, 2, WIN + 4 * SPARSE])
        sp_ = tmp("s_probs", [P, SK])
        spT = tmp("s_pT", [P, 9, P])
        snm = tmp("s_nm", [P, 2, 4])
        sden = tmp("s_den", [P, 2, 2])
        om = probs[:, 0:2, :]
        ring = stream[:, :].rearrange("p (s t n) -> p s t n", s=6, t=8)
        items = [(kind, b) for g in range(2) for kind in "kv" for b in range(4 * g, 4 * g + 4)]
        wout = stream[:, 4 * 4096:6 * 4096].rearrange("p (k n) -> p k n", k=KC)
        shared = stream[:, 0:6144]

        masks_in = sem("s2_masks_in")
        row_in = [sem(f"s2_rows{i}") for i in range(6)]
        zeroed, turn_ps, turn_ok, new_ps, new_ok = (sem(f"s2_{n}") for n in
                                                    ("zeroed", "turn_ps", "turn_ok", "new_ps", "new_ok"))
        sc, sc_read, exp_ok, p_ok = (sem(f"s2_{n}") for n in ("sc", "sc_read", "exp_ok", "p_ok"))
        pT_ps, pT_ok, pv, pv_read = (sem(f"s2_{n}") for n in ("pT_ps", "pT_ok", "pv", "pv_read"))
        kt_ps, kt_a, kt_v, ssc = (sem(f"s2_{n}") for n in ("kt_ps", "kt_a", "kt_v", "ssc"))
        ssc_read, sexp, sp_ok = (sem(f"s2_{n}") for n in ("ssc_read", "sexp", "sp_ok"))
        spt_ps, spt_a, spt_v, spv, om_ok, fold = (sem(f"s2_{n}") for n in
                                                  ("spt_ps", "spt_a", "spt_v", "spv", "om_ok", "fold"))
        v_step = sem("s2_v_step")

        def arrived(eng, kind, b):
            j = items.index((kind, b))
            eng.wait_ge(row_in[j % 6], 32 * (j // 6 + 1))
            return ring[:, j % 6]

        def load_cache(eng, dst, cache, b, signal):
            c = cache[0, b].rearrange("r h d -> r (h d)")
            eng.dma_start(dst[:, 0:4, :], c[WIN0:, :].rearrange("(p t) n -> p t n", t=4)).then_inc(signal, 16)
            eng.dma_start(dst[0:SPARSE, 4:8, :],
                          c[0:WIN0, :].rearrange("(j s) n -> j s n", s=16)[:, 0:4, :]).then_inc(signal, 16)

        with nc.Block() as block:
            @block.sync
            def _(sp):
                sp.dma_start(masks[:, :], io["masks"]).then_inc(masks_in, 16)

                for j, (kind, b) in enumerate(items):
                    if j == 5:
                        sp.wait_ge(stored, 6 * 16)
                    if j >= 6:
                        was, n = items[j - 6]
                        if was == "k":
                            sp.wait_ge(kt_ps, 4 * (n + 1))
                        else:
                            sp.wait_ge(spv, n + 1)
                    load_cache(sp, ring[:, j % 6], io["cache_" + kind], b, row_in[j % 6])
                sp.wait_ge(kt_ps, 4 * DEC_B)
                sp.dma_start(wout, io["w_out"][0].rearrange("(k p) n -> p k n", p=P)).then_inc(wout_in, 16)
                sp.wait_ge(spv, 6)
                load_expert(sp, shared, io["w_sh_gate"][0], io["w_sh_up"][0], io["w_sh_down"][0], shared_in)

            @block.gpsimd
            def _(pool):
                pool.memset(qz[:, :, :, :], 0.0).then_inc(zeroed, 1)
                pool.memset(spT[:, 8, :], 0.0).then_inc(zeroed, 1)

            @block.scalar
            def _(act):
                for i in range(2 * WC):
                    act.wait_ge(turn_ps, i + 1)
                    act.copy((qT, kT)[i % 2][:, i // 2, :], psum[:, 4 + i % 2, :]).then_inc(turn_ok, 1)
                N = NPT * HEADS
                for n in range(N + 2):
                    if n < N:
                        act.wait_ge(sc_read, n + 1)
                        w = (n // HEADS + 1) * P
                        act.activation(probs[:, n % 3, 0:w], probs[:, n % 3, 0:w], ACT.Exp,
                                       bias=nmax[:, n:n + 1], scale=-1.0).then_inc(exp_ok, 1)
                    m = n - 2
                    if m >= 0:
                        act.wait_ge(pT_ps, m + 1)
                        if m >= 2:
                            act.wait_ge(pv, m - 1)
                        w = (m // HEADS + 1) * P
                        act.copy(pT[:, m % 2, 0:w], psum[:, 4 + m % 2, 0:w]).then_inc(pT_ok, 1)
                for g in range(2):
                    for e in range(16 * g, 16 * g + 16):
                        act.wait_ge(kt_ps, e + 1)
                        if e >= 2:
                            act.wait_ge(ssc, e - 1)
                        act.copy(KTs[:, e % 2, 0:WIN], psum[:, e % 2, :]).then_inc(kt_a, 1)
                    act.wait_ge(ssc_read, g + 1)
                    act.activation(sp_[:, :], sp_[:, :], ACT.Exp, bias=snm[:, g, 2:3], scale=-1.0).then_inc(sexp, 1)
                    act.wait_ge(spt_ps, g + 1)
                    act.copy(spT[:, 0:4, :], psum[:, 0, :].rearrange("p (t n) -> p t n", t=4)).then_inc(spt_a, 1)

            @block.vector
            def _(v):
                n_step = [0]

                def step(ins):
                    n_step[0] += 1
                    ins.then_inc(v_step, 1)

                def settle():
                    v.wait_ge(v_step, n_step[0])

                v.wait_ge(zeroed, 1)
                v.wait_ge(new_ps, 2)
                for h in range(HEADS):
                    lo = (h % 2) * HD
                    step(v.tensor_copy(qz[lo:lo + HD, h // 2, :, h * DEC_T:(h + 1) * DEC_T],
                                       psum[lo:lo + HD, 6, (h // 2) * NS:(h // 2 + 1) * NS].rearrange("p (b t) -> p b t", b=DEC_B)))
                step(v.tensor_copy(kTn[:, :, :], psum[:, 7, 0:WC * NS].rearrange("p (c n) -> p c n", c=WC)))
                settle()
                v.sem_inc(new_ok, 1)
                v.wait_ge(masks_in, 16)
                N = NPT * HEADS

                def finish_tile(i):
                    v.wait_ge(pv, HEADS * (i + 1))
                    step(v.reciprocal(rden[:, i * HEADS:(i + 1) * HEADS], den[:, i * HEADS:(i + 1) * HEADS]))
                    settle()
                    v.tensor_tensor(attn[:, i, :].rearrange("p (h d) -> p h d", h=HEADS),
                                    psum[:, 6 + i % 2, :].rearrange("p (h d) -> p h d", h=HEADS),
                                    rden[:, i * HEADS:(i + 1) * HEADS].unsqueeze(2).broadcast_to([P, HEADS, HD]),
                                    ALU.mult).then_inc(pv_read, 1)

                for n in range(N + 1):
                    if n < N:
                        i = n // HEADS
                        w, a = (i + 1) * P, (NPT - 1 - i) * P
                        v.wait_ge(sc, n + 1)
                        if n >= 3:
                            v.wait_ge(pT_ps, n - 2)
                        v.tensor_tensor_reduce(probs[:, n % 3, 0:w], psum[:, n % 3, 0:w], masks[:, A_PN + a:A_PN + 512],
                                               -HD ** -0.5, 3e38, ALU.add, ALU.min, nmax[:, n:n + 1]).then_inc(sc_read, 1)
                    if n >= 1:
                        m = n - 1
                        i = m // HEADS
                        w, a = (i + 1) * P, (NPT - 1 - i) * P
                        v.wait_ge(exp_ok, m + 1)
                        v.tensor_tensor_reduce(probs[:, m % 3, 0:w], probs[:, m % 3, 0:w], masks[:, A_PM + a:A_PM + 512],
                                               1.0, 0.0, ALU.mult, ALU.add, den[:, m:m + 1]).then_inc(p_ok, 1)
                    if n % HEADS == 5 and n > HEADS:
                        v.wait_ge(p_ok, n)
                        finish_tile(n // HEADS - 1)
                v.wait_ge(p_ok, N)
                finish_tile(NPT - 1)
                for g in range(2):
                    for e in range(16 * g, 16 * g + 16):
                        v.wait_ge(kt_ps, e + 1)
                        if e >= 2:
                            v.wait_ge(ssc, e - 1)
                        v.tensor_copy(KTs[:, e % 2, WIN:], psum[:, 2 + e % 2, 0:4 * SPARSE]).then_inc(kt_v, 1)
                    v.wait_ge(ssc, 16 * (g + 1))
                    if g:
                        v.wait_ge(spt_ps, g)
                    for j, (a, b) in enumerate(((0, WIN), (WIN, SK))):
                        step(v.tensor_tensor_reduce(sp_[:, a:b], psum[:, 4 + j, 0:b - a],
                                                    masks[:, A_SN + g * SK + a:A_SN + g * SK + b],
                                                    -HD ** -0.5, 3e38, ALU.add, ALU.min, snm[:, g, j:j + 1]))
                    settle()
                    v.tensor_tensor(snm[:, g, 2:3], snm[:, g, 0:1], snm[:, g, 1:2], ALU.min).then_inc(ssc_read, 1)
                    v.wait_ge(sexp, g + 1)
                    v.tensor_tensor_reduce(sp_[:, :], sp_[:, :], masks[:, A_SM + g * SK:A_SM + (g + 1) * SK],
                                           1.0, 0.0, ALU.mult, ALU.add, sden[:, g, 0:1]).then_inc(sp_ok, 1)
                    v.wait_ge(zeroed, 2)
                    v.wait_ge(spt_ps, g + 1)
                    v.tensor_copy(spT[0:SPARSE, 4:8, :], psum[0:SPARSE, 1, :].rearrange("p (t n) -> p t n", t=4)).then_inc(spt_v, 1)
                    v.tensor_copy(spT[0:NS, 8, :], psum[0:NS, 2, 0:P]).then_inc(spt_v, 1)
                    v.wait_ge(sp_ok, g + 1)
                    step(v.reciprocal(sden[:, g, 1:2], sden[:, g, 0:1]))
                    settle()
                    v.wait_ge(spv, 4 * (g + 1))
                    v.scalar_tensor_tensor(om[:, g, :], psum[:, 6 + g, :], sden[:, g, 1:2], masks[:, A_BD:A_BD + W],
                                           ALU.mult, ALU.mult).then_inc(om_ok, 1)
                v.wait_ge(fold, 1)
                v.tensor_copy(attn[0:NS, NPT, :], psum[0:NS, 0, :])

            @block.tensor
            def _(pe):
                for j, src in enumerate((q_sb, k_sb)):
                    for c in range(WC):
                        last = pe.transpose(psum[:, 6 + j, c * NS:(c + 1) * NS], src[0:NS, NPT, c * P:(c + 1) * P],
                                            ident[0:NS, 0:NS])
                    last.then_inc(new_ps, 1)
                for i in range(2 * WC):
                    if i >= 2:
                        pe.wait_ge(turn_ok, i - 1)
                    for t in range(NPT):
                        last = pe.transpose(psum[:, 4 + i % 2, t * P:(t + 1) * P],
                                            (q_sb, k_sb)[i % 2][:, t, (i // 2) * P:(i // 2 + 1) * P], ident)
                    last.then_inc(turn_ps, 1)
                pe.wait_ge(turn_ok, 2 * WC)
                N = NPT * HEADS
                for n in range(N + 3):
                    if n < N:
                        i, h = n // HEADS, n % HEADS
                        lo = (h % 2) * HD
                        if n >= 3:
                            pe.wait_ge(sc_read, n - 2)
                        pe.matmul(psum[:, n % 3, 0:(i + 1) * P], qT[lo:lo + HD, h // 2, i * P:(i + 1) * P],
                                  kT[lo:lo + HD, h // 2, 0:(i + 1) * P], start=True, stop=True).then_inc(sc, 1)
                    m = n - 2
                    if 0 <= m < N:
                        pe.wait_ge(p_ok, m + 1)
                        if m >= 2:
                            pe.wait_ge(pT_ok, m - 1)
                        for t in range(m // HEADS + 1):
                            last = pe.transpose(psum[:, 4 + m % 2, t * P:(t + 1) * P], probs[:, m % 3, t * P:(t + 1) * P], ident)
                        last.then_inc(pT_ps, 1)
                    m = n - 3
                    if m >= 0:
                        i, h = m // HEADS, m % HEADS
                        pe.wait_ge(pT_ok, m + 1)
                        if m == 0:
                            pe.wait_ge(new_ok, 1)
                        if h == 0 and i >= 2:
                            pe.wait_ge(pv_read, i - 1)
                        for t in range(i + 1):
                            last = pe.matmul(psum[:, 6 + i % 2, h * HD:(h + 1) * HD], pT[:, m % 2, t * P:(t + 1) * P],
                                             v_sb[:, t, h * HD:(h + 1) * HD], start=(t == 0), stop=(t == i))
                        last.then_inc(pv, 1)
                pe.wait_ge(pv_read, NPT)

                def turn_keys(e):
                    b, c = e // 4, e % 4
                    keys = arrived(pe, "k", b)
                    if e >= 2:
                        pe.wait_ge(kt_a, e - 1)
                        pe.wait_ge(kt_v, e - 1)
                    for t in range(4):
                        pe.transpose(psum[:, e % 2, t * P:(t + 1) * P], keys[:, t, c * P:(c + 1) * P], ident)
                    for t in range(4):
                        last = pe.transpose(psum[:, 2 + e % 2, t * SPARSE:(t + 1) * SPARSE],
                                            keys[0:SPARSE, 4 + t, c * P:(c + 1) * P], ident[0:SPARSE, 0:SPARSE])
                    last.then_inc(kt_ps, 1)

                for g in range(2):
                    if g:
                        pe.wait_ge(ssc_read, g)
                        pe.wait_ge(spt_v, 2 * g)
                        pe.wait_ge(spt_a, g)
                    turn_keys(16 * g)
                    for e in range(16 * g, 16 * g + 16):
                        b, c = e // 4, e % 4
                        lo = 32 * (b % 4)
                        if e + 1 < 16 * g + 16:
                            turn_keys(e + 1)
                        pe.wait_ge(kt_a, e + 1)
                        pe.wait_ge(kt_v, e + 1)
                        w = qz[:, c, b, :]
                        pe.matmul(psum[lo:lo + 32, 4, :], w, KTs[:, e % 2, 0:WIN], start=(c == 0), stop=(c == 3))
                        pe.matmul(psum[lo:lo + 32, 5, 0:4 * SPARSE], w, KTs[:, e % 2, WIN:], start=(c == 0), stop=False,
                                  skip_group_check=True)
                        last = pe.matmul(psum[lo:lo + 32, 5, 4 * SPARSE:4 * SPARSE + NS], w, kTn[:, c, :],
                                         start=False, stop=(c == 3), skip_group_check=True)
                        last.then_inc(ssc, 1)
                    pe.wait_ge(sp_ok, g + 1)
                    for t in range(4):
                        pe.transpose(psum[:, 0, t * P:(t + 1) * P], sp_[:, t * P:(t + 1) * P], ident)
                    for t in range(4):
                        pe.transpose(psum[0:SPARSE, 1, t * P:(t + 1) * P], sp_[:, WIN + t * SPARSE:WIN + (t + 1) * SPARSE], ident)
                    pe.transpose(psum[0:NS, 2, 0:P], sp_[:, WIN + 4 * SPARSE:], ident).then_inc(spt_ps, 1)
                    pe.wait_ge(spt_a, g + 1)
                    pe.wait_ge(spt_v, 2 * (g + 1))
                    for b in range(4 * g, 4 * g + 4):
                        lo = 32 * (b % 4)
                        values = arrived(pe, "v", b)
                        for t in range(9):
                            k = P if t < 4 or t == 8 else SPARSE
                            rhs = values[0:k, t, :] if t < 8 else v_sb[:, NPT, :]
                            last = pe.matmul(psum[lo:lo + 32, 6 + g, :], spT[0:k, t, lo:lo + 32], rhs,
                                             start=(t == 0), stop=(t == 8))
                        last.then_inc(spv, 1)
                pe.wait_ge(om_ok, 2)
                for g in range(2):
                    last = pe.matmul(psum[0:NS, 0, :], masks[:, A_SEL + g * NS:A_SEL + (g + 1) * NS], om[:, g, :],
                                     start=(g == 0), stop=(g == 1))
                last.then_inc(fold, 1)
        st.close()

    def stage_3():
        st = ExitStack()

        def tmp(name, shape, dt=F32):
            return st.enter_context(nc.sbuf_tensor("sb_" + name, shape, dt))

        x2 = tmp("x2", [P, NT, D])
        bc = tmp("bc", [P, 3, 2, D])
        flat = bc[:, :, :, :].rearrange("p a b n -> p (a b n)")
        ysh = flat[:, 0:NT * D].rearrange("p (t n) -> p t n", t=NT)
        h2T = tmp("h2T", [P, KC, NTOK])
        work = tmp("work", [P, 3, D])
        xg = work
        aT = tmp("aT", [P, 2, WC, P])
        wr = tmp("wr", [P, KC, NE])
        hbuf = aT[:, :, :, :].rearrange("p s c n -> p (s c n)")[:, 0:3 * FE].rearrange("p (a n) -> p a n", a=3)
        sil, hid, hidT = hbuf[:, 0, :], hbuf[:, 1, :], hbuf[:, 2, :].rearrange("p (k n) -> p k n", k=2)
        oh = tmp("oh", [P, 3, NT, P], BF16)
        pick = tmp("pick", [P, 3, NT, 9], BF16)
        table = tmp("table", [P, NT, NE, 9], BF16)
        blk = tmp("blk", [P, 3, NT])
        got = tmp("got", [P, 3, 3])
        token = tmp("token", [P, 3, 1], U32)
        row = tmp("row", [P, 3, 1], U32)
        now_gate = tmp("now_gate", [P, 3])
        tab = tmp("tab", [1, P + 1], I32)
        bias = tmp("bias", [P, NE])
        ss = tmp("ss3", [P, 4, NT])
        small = tmp("small", [P, 80])
        wout = stream[:, 4 * 4096:6 * 4096].rearrange("p (k n) -> p k n", k=KC)
        wslot = [stream[:, 6144 * s:6144 * (s + 1)] for s in range(3)]
        xT = stream[:, 18432:18432 + 3 * D].rearrange("p (s k n) -> p s k n", s=3, k=KC)
        out = stream[:, 18432 + 3 * D:18432 + 6 * D].rearrange("p (s n) -> p s n", s=3)
        af = attn[:, :, :].rearrange("p t n -> p (t n)")
        scores, sel, selm, mask, gate, ra, rb, gpos = (
            af[:, 320 * n:320 * (n + 1)].rearrange("p (t e) -> p t e", t=NT) for n in range(8))
        cf = convg[:, :, :].rearrange("p c n -> p (c n)")
        run = [cf[:, 480 * n:480 * (n + 1)].rearrange("p (t e) -> p t e", t=NT) for n in range(2)]
        erun = [cf[:, 960 + 96 * n:960 + 96 * (n + 1)] for n in range(2)]
        nblk, cnt, first = (cf[:, 1152 + 64 * n:1152 + 64 * (n + 1)] for n in range(3))
        grp = cf[:, 1344:1384].rearrange("p (t g) -> p t g", t=NT)
        gok = cf[:, 1384:1424].rearrange("p (t g) -> p t g", t=NT)
        gneg = cf[:, 1424:1464].rearrange("p (t g) -> p t g", t=NT)
        top = cf[:, 1464:1504].rearrange("p (t g) -> p t g", t=NT)
        gsum, grec = cf[:, 1504:1509], cf[:, 1509:1514]
        blkf, tripf = cf[:, 1514:1515], cf[:, 1515:1516]
        maskb = cf[:, 1520:1520 + 160].bitcast(BF16).rearrange("p (t e) -> p t e", t=NT)
        trib = cf[:, 1680:1680 + 64].bitcast(BF16)
        oneb = cf[:, 1744:1744 + 64].bitcast(BF16)

        DN0 = 2 * NT
        names = ("x_in bc_in small_in ams rs an_ok aT_ps aT_ok prod_c prod_a tc_ok x2_ok ms h2_ok h2_ps h2_sb logit "
                 "ex_ok zeroed mask_ok cnt_ps blk_ok tab_ps tab_ok table_ok consts_ok "
                 "sgu ssil shid sht shT "
                 "list_mm list_ok oh_ok token_ok now_ok xt_ps xt_a xt_v gu sil_ok hid_ok ht_ps ht_ok dn out_lo out_hi pick_ok go").split()
        s = {n: sem("s3_" + n) for n in names}
        h_out = [sem(f"s3_h_out{i}") for i in range(2)]
        w_in = [sem(f"s3_w{i}") for i in range(3)]
        moved = [sem(f"s3_moved{i}") for i in range(3)]
        v_step = sem("s3_v_step")

        room = h2T[:, :, :].rearrange("p k n -> p (k n)")
        gate2 = room[:, 0:2 * D].rearrange("p (a n) -> p a n", a=2)
        gfin = room[:, 2 * D:3 * D]

        def trips(eng):
            eng.wait_ge(s["tab_ok"], 1)
            return eng.value_load(tab[0:1, P:P + 1], min_val=0, max_val=TRIPS)

        def expert_of(eng, b):
            return eng.value_load(tab[0:1, bass.ds(b, 1)], min_val=0, max_val=NE - 1)

        def who(v, b, u):
            e = expert_of(v, b)
            v.tensor_tensor(blk[:, u, :].unsqueeze(2), gpos[:, :, bass.ds(e, 1)],
                            cst[:, bass.ds(b + C_BASE, 1)].unsqueeze(1).broadcast_to([P, NT, 1]), ALU.subtract).then_inc(s["blk_ok"], 1)
            v.tensor_copy(pick[:, u, :, :].unsqueeze(2), table[:, :, bass.ds(e, 1), :]).then_inc(s["pick_ok"], 1)
            v.wait_ge(s["blk_ok"], b + 1)
            for t in range(NT):
                last = v.tensor_scalar(oh[:, u, t, :], cst[:, C_IOTA:C_IOTA + P], blk[:, u, t:t + 1], None, ALU.is_equal)
            last.then_inc(s["oh_ok"], 1)

        def fill_list(pe, b, u):
            pe.wait_ge(s["oh_ok"], b + 1)
            pe.wait_ge(s["pick_ok"], b + 1)
            if not isinstance(b, int) or b:
                pe.wait_ge(s["list_ok"], b)
            for t in range(NT):
                last = pe.matmul(psum[:, 6, 0:9], oh[:, u, t, :], pick[:, u, t, :], start=(t == 0), stop=(t == NT - 1))
            last.then_inc(s["list_mm"], 1)

        def read_list(v, b, u):
            v.wait_ge(s["list_mm"], b + 1)
            v.tensor_reduce(got[:, u, :], psum[:, 6, 0:9].rearrange("p (a c) -> p a c", a=3), AX.X, ALU.add).then_inc(s["list_ok"], 1)
            v.wait_ge(s["list_ok"], b + 1)
            v.tensor_scalar(token[:, u, :], got[:, u, 0:1], float(OUTSIDE), None, ALU.add).then_inc(s["token_ok"], 1)

        def gather(pool, b, u, last_row):
            pool.wait_ge(s["token_ok"], b + 1)
            pool.sem_inc(s["go"], 1)
            pool.indirect_dma_start(xg[:, u, :], None, h_rows, bass.IndirectOffsetOnAxis(ap=token[:, u, :], axis=0),
                                    bounds_check=last_row, oob_is_err=False).then_inc(moved[u], 16)

        def turn_rows(pe, u, chunks):
            for k in chunks:
                last = pe.transpose(psum[:, 1 + k // 4, (k % 4) * P:(k % 4 + 1) * P], xg[:, u, k * P:(k + 1) * P], ident)
                if k % 4 == 3:
                    last.then_inc(s["xt_ps"], 1)

        def take_rows_a(act, b, u):
            act.wait_ge(s["xt_ps"], 2 * b + 1)
            act.copy(xT[:, u, 0:4, :], psum[:, 1, :].rearrange("p (k n) -> p k n", k=4)).then_inc(s["xt_a"], 1)

        def take_rows_v(v, b, u):
            v.wait_ge(s["xt_ps"], 2 * b + 2)
            v.tensor_copy(xT[:, u, 4:8, :], psum[:, 2, :].rearrange("p (k n) -> p k n", k=4)).then_inc(s["xt_v"], 1)

        def gate_up(pe, bank, r, lhs, w, done):
            gu = w[:, 0:KC * 2 * FE].rearrange("p (k n) -> p k n", k=KC)
            for k in range(KC):
                last = pe.matmul(psum[0:r, bank, :], lhs(k), gu[:, k, :], start=(k == 0), stop=(k == KC - 1))
            last.then_inc(done, 1)

        def turn_hidden(pe, r, done):
            for k in range(2):
                last = pe.transpose(psum[:, 3, k * P:k * P + r], hid[0:r, k * P:(k + 1) * P], ident[0:r, 0:r])
            last.then_inc(done, 1)

        def down(pe, r, w, done, waits):
            dn = w[:, KC * 2 * FE:].rearrange("p (k n) -> p k n", k=2)
            for n in range(2):
                waits(n)
                for k in range(2):
                    last = pe.matmul(psum[0:r, 4 + n, :], hidT[:, k, 0:r], dn[:, k, n * 512:(n + 1) * 512],
                                     start=(k == 0), stop=(k == 1))
                last.then_inc(done, 1)

        with nc.Block() as block:
            @block.sync
            def _(sp):
                sp.dma_start(x2[:, 0:NPT, :], io["x_prompt"][0].rearrange("(t p) n -> p t n", p=P)).then_inc(s["x_in"], 16)
                sp.dma_start(x2[0:NS, NPT, :], io["x_sample"].rearrange("b t n -> (b t) n")).then_inc(s["x_in"], 16)
                for n, j in enumerate((2, 3, 4)):
                    sp.dma_start(bc[:, n, 0, :], bc_row(mod_rows[0:1, j * D:(j + 1) * D], P)).then_inc(s["bc_in"], 16)
                    sp.dma_start(bc[0:NS, n, 1, :], mod_sample(j)).then_inc(s["bc_in"], 16)
                sp.dma_start(wr[:, :, :], io["w_router"][0].rearrange("(k p) n -> p k n", p=P)).then_inc(s["small_in"], 16)
                sp.dma_start(bias[:, :], bc_row(io["router_bias"], P)).then_inc(s["small_in"], 16)
                for t in range(NT):
                    sp.wait_ge(s["h2_ok"], t + 1)
                    sp.dma_start(h_rows[t * P:t * P + rows(t), :], work[0:rows(t), 1 + t % 2, :]).then_inc(h_out[t % 2], 16)
                nb = trips(sp)
                with sp.Fori(0, TRIPS) as i:
                    with sp.If(nb > i):
                        for u in range(3):
                            b = 3 * i + u
                            e = expert_of(sp, b)
                            sp.wait_ge(s["dn"], 2 * (b - 2) + DN0)
                            load_expert(sp, wslot[(u + 1) % 3],
                                        io["w_exp_gate"][0, bass.ds(e, 1)].rearrange("a d f -> (a d) f"),
                                        io["w_exp_up"][0, bass.ds(e, 1)].rearrange("a d f -> (a d) f"),
                                        io["w_exp_down"][0, bass.ds(e, 1)].rearrange("a d f -> (a d) f"), w_in[u])

            @block.gpsimd
            def _(pool):
                pool.memset(table[:, :, :, :].rearrange("p t e c -> p (t e c)"), 0.0).then_inc(s["zeroed"], 1)
                pool.wait_ge(s["zeroed"], 1)
                for t in range(NT):
                    pool.tensor_copy(table[:, t, :, 0:5],
                                     cst[:, C_LP + 5 * t:C_LP + 5 * t + 5].unsqueeze(1).broadcast_to([P, NE, 5])).then_inc(s["consts_ok"], 1)
                minus_half = cst[:, C_POW:C_POW + 1]

                def inverse_root(dst, src):
                    n = dst.shape[1]
                    pool.tensor_tensor(dst, src, minus_half[0:dst.shape[0]].broadcast_to([dst.shape[0], n]), ALU.pow).then_inc(s["rs"], 1)

                pool.wait_ge(s["ams"], 1)
                inverse_root(ss[:, 1, 0:NPT], ss[:, 0, 0:NPT])
                inverse_root(ss[0:NS, 1, NPT:], ss[0:NS, 0, NPT:])
                for t in range(NT):
                    pool.wait_ge(s["ms"], t + 1)
                    inverse_root(ss[0:rows(t), 3, t:t + 1], ss[0:rows(t), 2, t:t + 1])
                pool.wait_ge(s["h2_ps"], 2 * NT)
                pool.wait_ge(s["prod_a"], NT)
                pool.memset(cf[:, 0:1152], 0.0).then_inc(s["zeroed"], 1)
                pool.memset(scores, 1.0).then_inc(s["zeroed"], 1)
                for n in range(2):
                    pool.wait_ge(h_out[n], 16 * (3 - n))
                pool.memset(xg[:, :, :], 0.0).then_inc(s["zeroed"], 1)
                last_row, last_expert_row = pool.to_reg(NTOK - 1), pool.to_reg(NTOK * TOPK - 1)
                pool.wait_ge(s["zeroed"], 4)
                gather(pool, 0, 0, last_row)
                gather(pool, 1, 1, last_row)
                gather(pool, 2, 2, last_row)
                nb = trips(pool)
                with pool.Fori(0, TRIPS) as i:
                    with pool.If(nb > i):
                        for u in range(3):
                            b = 3 * i + u
                            pool.wait_ge(s["xt_ps"], 2 * b + 2)
                            gather(pool, b + 3, u, last_row)
                            pool.wait_ge(s["now_ok"], 2 * b + 2)
                            pool.wait_ge(s["out_lo"], b + 1 + NT)
                            pool.wait_ge(s["out_hi"], b + 1 + NT)
                            pool.sem_inc(s["go"], 1)
                            pool.indirect_dma_start(expert_rows, bass.IndirectOffsetOnAxis(ap=row[:, u, :], axis=0),
                                                    out[:, u, :], None, bounds_check=last_expert_row,
                                                    oob_is_err=False).then_inc(moved[u], 16)
                for u in range(3):
                    pool.wait_ge(moved[u], 32 * nb + 16)
                pool.wait_ge(s["go"], 6 * nb + 3)

            @block.scalar
            def _(act):
                act.wait_ge(s["rs"], 2)
                for t in range(NT):
                    r = rows(t)
                    act.activation(attn[0:r, t, :], attn[0:r, t, :], ACT.Copy, scale=ss[0:r, 1, t:t + 1]).then_inc(s["an_ok"], 1)

                def take_attn(t):
                    act.wait_ge(s["aT_ps"], t + 1)
                    for c in range(WC):
                        last = act.activation(aT[:, t % 2, c, 0:rows(t)], psum[:, 0, c * P:c * P + rows(t)], ACT.Copy,
                                              scale=gains[:, 0, c:c + 1])
                    last.then_inc(s["aT_ok"], 1)

                def take_norm(t):
                    for half in range(2):
                        act.wait_ge(s["h2_ps"], 2 * t + half + 1)
                        act.copy(h2T[:, 4 * half:4 * half + 4, t * P:t * P + rows(t)],
                                 psum[:, 6 + half, :].rearrange("p (k n) -> p k n", k=4)[:, :, 0:rows(t)]).then_inc(s["h2_sb"], 1)

                def take_conv(t):
                    r = rows(t)
                    act.wait_ge(s["prod_c"], t + 1)
                    if t:
                        act.wait_ge(s["x2_ok"], t)
                    act.activation(work[0:r, 0, :], psum[0:r, 4:6, :].rearrange("p a n -> p (a n)"), ACT.Copy,
                                   scale=conv_r[0:r, t:t + 1]).then_inc(s["tc_ok"], 1)

                for t in range(NT):
                    if t == 0:
                        take_conv(t)
                    take_attn(t)
                    if t:
                        take_conv(t)
                    if t >= 2:
                        take_norm(t - 2)
                take_norm(NT - 2)
                take_norm(NT - 1)
                act.wait_ge(s["logit"], NT)
                act.wait_ge(s["zeroed"], 3)
                act.activation(scores[:, 0:NPT, :], psum[:, 1, 0:NPT * NE].rearrange("p (t e) -> p t e", t=NPT), ACT.Exp, scale=-1.0)
                act.activation(scores[0:NS, NPT, :], psum[0:NS, 1, NPT * NE:NT * NE], ACT.Exp, scale=-1.0).then_inc(s["ex_ok"], 1)

                def shared(t):
                    r = rows(t)
                    act.wait_ge(s["sgu"], t + 1)
                    if t:
                        act.wait_ge(s["shid"], t)
                    act.activation(sil[0:r], psum[0:r, 7 * (t % 2), 0:FE], ACT.Silu).then_inc(s["ssil"], 1)

                def shared_out(t):
                    r = rows(t)
                    act.wait_ge(s["sht"], t + 1)
                    if t:
                        act.wait_ge(s["dn"], 2 * t)
                    act.copy(hidT[:, :, 0:r], psum[:, 3, 0:2 * P].rearrange("p (k n) -> p k n", k=2)[:, :, 0:r]).then_inc(s["shT"], 1)
                    for n, done in enumerate(("out_lo", "out_hi")):
                        act.wait_ge(s["dn"], 2 * t + n + 1)
                        act.copy(ysh[0:r, t, n * 512:(n + 1) * 512], psum[0:r, 4 + n, :]).then_inc(s[done], 1)

                shared(0)
                for t in range(NT):
                    if t + 1 < NT:
                        shared(t + 1)
                    shared_out(t)
                take_rows_a(act, 0, 0)
                act.wait_ge(s["sgu"], NT)
                act.dma_start(gate2[:, 0, :], bc_row(mod_rows[0:1, 5 * D:], P)).then_inc(last_in, 16)
                act.dma_start(gate2[0:NS, 1, :], mod_sample(5)).then_inc(last_in, 16)
                act.dma_start(gfin, bc_row(io["g_final"].unsqueeze(0), P)).then_inc(last_in, 16)
                nb = trips(act)
                with act.Fori(0, TRIPS) as i:
                    with act.If(nb > i):
                        for u in range(3):
                            b = 3 * i + u
                            act.wait_ge(s["gu"], b + 1)
                            act.activation(sil, psum[:, 0, 0:FE], ACT.Silu).then_inc(s["sil_ok"], 1)
                            take_rows_a(act, b + 1, (u + 1) % 3)
                            act.wait_ge(s["ht_ps"], b + 1)
                            act.copy(hidT, psum[:, 3, 0:2 * P].rearrange("p (k n) -> p k n", k=2)).then_inc(s["ht_ok"], 1)
                            act.wait_ge(s["now_ok"], 2 * b + 2)
                            act.wait_ge(s["dn"], 2 * b + 1 + DN0)
                            act.activation(out[:, u, 0:512], psum[:, 4, :], ACT.Copy, scale=now_gate[:, u:u + 1]).then_inc(s["out_lo"], 1)

            @block.vector
            def _(v):
                n_step = [0]

                def step(ins):
                    n_step[0] += 1
                    ins.then_inc(v_step, 1)
                    v.wait_ge(v_step, n_step[0])

                for t in range(NT):
                    r = rows(t)
                    step(v.tensor_tensor_reduce(work[0:r, 1, 0:W], attn[0:r, t, :], attn[0:r, t, :], 1.0, 0.0,
                                                ALU.mult, ALU.add, ss[0:r, 2, t:t + 1]))
                step(v.tensor_scalar(ss[:, 0, 0:NPT], ss[:, 2, 0:NPT], 1.0 / W, EPS, ALU.mult, ALU.add))
                step(v.tensor_scalar(ss[0:NS, 0, NPT:], ss[0:NS, 2, NPT:], 1.0 / W, EPS, ALU.mult, ALU.add))
                v.sem_inc(s["ams"], 1)
                v.wait_ge(s["rs"], 2)
                v.wait_ge(s["bc_in"], 6 * 16)
                for a, r in ((0, P), (1, NS)):
                    step(v.tensor_scalar(bc[0:r, 2, a, :], bc[0:r, 2, a, :], 1.0, None, ALU.add))
                v.wait_ge(s["x_in"], 32)

                def residual(t):
                    r, a = rows(t), t // NPT
                    h = work[0:r, 1 + t % 2, :]
                    v.wait_ge(s["prod_a"], t + 1)
                    v.wait_ge(s["tc_ok"], t + 1)
                    if t >= 2:
                        v.wait_ge(s["h2_ps"], 2 * (t - 1))
                        v.wait_ge(h_out[t % 2], 16 * (t // 2))
                    step(v.tensor_tensor(h, psum[0:r, 2:4, :].rearrange("p a n -> p (a n)"), work[0:r, 0, :], ALU.add))
                    v.sem_inc(s["x2_ok"], 1)
                    step(v.tensor_tensor(h, h, bc[0:r, 0, a, :], ALU.mult))
                    step(v.tensor_tensor(x2[0:r, t, :], x2[0:r, t, :], h, ALU.add))
                    step(v.tensor_tensor_reduce(h, x2[0:r, t, :], x2[0:r, t, :], 1.0, 0.0, ALU.mult, ALU.add, ss[0:r, 0, t:t + 1]))
                    step(v.tensor_scalar(ss[0:r, 2, t:t + 1], ss[0:r, 0, t:t + 1], 1.0 / D, EPS, ALU.mult, ALU.add))
                    v.sem_inc(s["ms"], 1)
                    v.wait_ge(s["rs"], 3 + t)
                    step(v.scalar_tensor_tensor(h, x2[0:r, t, :], ss[0:r, 3, t:t + 1], bc[0:r, 2, a, :], ALU.mult, ALU.mult))
                    step(v.tensor_tensor(h, h, bc[0:r, 1, a, :], ALU.add))
                    v.sem_inc(s["h2_ok"], 1)

                for t in range(NT):
                    residual(t)

                def groups():
                    v.wait_ge(s["ex_ok"], 1)
                    v.wait_ge(s["small_in"], 32)
                    step(v.tensor_scalar(ra, scores, 1.0, None, ALU.add))
                    step(v.reciprocal(scores, ra))
                    step(v.tensor_tensor(sel, scores, bias[:, :].unsqueeze(1).broadcast_to([P, NT, NE]), ALU.add))
                    every = sel.rearrange("p t (g e) -> p (t g) e", g=NGRP)
                    raf, rbf = (x.rearrange("p t e -> p (t e)") for x in (ra, rb))
                    hi, lo = every[:, :, 0:8:2], every[:, :, 1:8:2]
                    h1 = raf[:, 0:160].rearrange("p (g e) -> p g e", e=4)
                    l1 = rbf[:, 0:160].rearrange("p (g e) -> p g e", e=4)
                    step(v.tensor_tensor(h1, hi, lo, ALU.max))
                    step(v.tensor_tensor(l1, hi, lo, ALU.min))
                    at = 160
                    for e in (2, 1):
                        n = 40 * e
                        h2_ = raf[:, at:at + n].rearrange("p (g e) -> p g e", e=e)
                        m2 = rbf[:, at:at + n].rearrange("p (g e) -> p g e", e=e)
                        l2 = small[:, 0:n].rearrange("p (g e) -> p g e", e=e)
                        step(v.tensor_tensor(h2_, h1[:, :, 0:2 * e:2], h1[:, :, 1:2 * e:2], ALU.max))
                        step(v.tensor_tensor(m2, h1[:, :, 0:2 * e:2], h1[:, :, 1:2 * e:2], ALU.min))
                        step(v.tensor_tensor(l2, l1[:, :, 0:2 * e:2], l1[:, :, 1:2 * e:2], ALU.max))
                        step(v.tensor_tensor(m2, m2, l2, ALU.max))
                        h1, l1, at = h2_, m2, at + n
                    step(v.tensor_tensor(grp.rearrange("p t g -> p (t g)").unsqueeze(2), h1, l1, ALU.add))

                def choose():
                    other = grp.unsqueeze(2).broadcast_to([P, NT, NGRP, NGRP])
                    own = grp.unsqueeze(3).broadcast_to([P, NT, NGRP, NGRP])
                    a4, b4 = (x.rearrange("p t (g e) -> p t g e", g=NGRP) for x in (ra, rb))
                    low = cst[:, C_LOW:C_LOW + 64].unsqueeze(1).broadcast_to([P, NT, NE])
                    step(v.tensor_tensor(a4, other, own, ALU.is_gt))
                    step(v.tensor_tensor(b4, other, own, ALU.is_equal))
                    step(v.tensor_tensor(rb, rb, low, ALU.mult))
                    step(v.tensor_tensor(ra, ra, rb, ALU.add))
                    step(v.tensor_reduce(gneg, a4, AX.X, ALU.add))
                    step(v.tensor_scalar(gok, gneg, 3.5, None, ALU.is_lt))
                    step(v.tensor_scalar(gneg, gok, 1.0, 1e30, ALU.subtract, ALU.mult))
                    s4 = selm.rearrange("p t (g e) -> p t g e", g=NGRP)
                    step(v.tensor_tensor(s4, sel.rearrange("p t (g e) -> p t g e", g=NGRP),
                                         gok.unsqueeze(3).broadcast_to([P, NT, NGRP, GSZ]), ALU.mult))
                    step(v.tensor_tensor(s4, s4, gneg.unsqueeze(3).broadcast_to([P, NT, NGRP, GSZ]), ALU.add))
                    for t in range(NT):
                        step(v.max(top[:, t, :], selm[:, t, :]))
                        step(v.match_replace(rb[:, t, :], top[:, t, :], selm[:, t, :], -3e38))
                    step(v.tensor_scalar(mask, rb, -2e38, None, ALU.is_lt))
                    step(v.tensor_tensor(ra, scores, mask, ALU.mult))
                    step(v.tensor_reduce(gsum, ra, AX.X, ALU.add))
                    step(v.reciprocal(grec, gsum))
                    step(v.scalar_tensor_tensor(gate, ra, 2.5, grec.unsqueeze(2).broadcast_to([P, NT, NE]), ALU.mult, ALU.mult))
                    step(v.tensor_tensor(mask, mask, cst[:, C_VALID:C_VALID + NT].unsqueeze(2).broadcast_to([P, NT, NE]), ALU.mult))
                    step(v.tensor_copy(maskb, mask))
                    step(v.tensor_copy(trib, cst[:, C_TRI:C_TRI + P]))
                    step(v.tensor_copy(oneb, cst[:, C_ONE:C_ONE + P]))
                    v.sem_inc(s["mask_ok"], 1)

                def running(a, b, width, first):
                    step(v.tensor_copy(a[..., 32:], first))
                    for n in (1, 2, 4, 8, 16, 32):
                        step(v.tensor_tensor(b[..., 32:], a[..., 32:], a[..., 32 - n:width - n], ALU.add))
                        a, b = b, a
                    return a

                def fill_table():
                    total = running(run[0], run[1], 96, mask)
                    v.wait_ge(s["consts_ok"], NT)
                    step(v.tensor_tensor(table[:, :, :, 5], total[..., 32:], mask, ALU.subtract))
                    step(v.tensor_copy(table[:, :, :, 6], gate))
                    step(v.tensor_tensor(ra, gate, table[:, :, :, 6], ALU.subtract))
                    step(v.tensor_copy(table[:, :, :, 7], ra))
                    step(v.tensor_tensor(rb, ra, table[:, :, :, 7], ALU.subtract))
                    step(v.tensor_copy(table[:, :, :, 8], rb))
                    v.sem_inc(s["table_ok"], 1)

                def queues():
                    v.wait_ge(s["cnt_ps"], 1)
                    step(v.tensor_copy(cnt, psum[:, 2, NT * NE:(NT + 1) * NE]))
                    step(v.tensor_scalar(nblk, cnt, 0.0, None, ALU.is_gt))
                    for n in range(1, -(-NTOK // P)):
                        step(v.scalar_tensor_tensor(nblk, cnt, float(n * P), nblk, ALU.is_gt, ALU.add))
                    ends = running(erun[0], erun[1], 96, nblk)[..., 32:]
                    step(v.tensor_tensor(first, ends, nblk, ALU.subtract))
                    step(v.tensor_scalar(first, first, float(P), 1.0, ALU.mult, ALU.add))
                    step(v.tensor_tensor(ra, psum[:, 2, 0:NT * NE].rearrange("p (t e) -> p t e", t=NT),
                                         first.unsqueeze(1).broadcast_to([P, NT, NE]), ALU.add))
                    step(v.tensor_tensor(ra, ra, mask, ALU.mult))
                    step(v.tensor_scalar(gpos, ra, -1.0, None, ALU.add))
                    step(v.tensor_scalar(cnt, ends, cst[:, C_IP:C_IP + 1], None, ALU.is_le))
                    step(v.tensor_reduce(blkf, cnt, AX.X, ALU.add))
                    step(v.tensor_scalar(blkf, blkf, float(NE - 1), None, ALU.min))
                    step(v.tensor_scalar(cnt[:, 0:TRIPS], cst[:, C_TRIP:C_TRIP + TRIPS], ends[:, NE - 1:NE], None, ALU.is_lt))
                    step(v.tensor_reduce(tripf, cnt[:, 0:TRIPS], AX.X, ALU.add))
                    step(v.tensor_copy(tab[0:1, P:P + 1], tripf[0:1, :]))
                    v.sem_inc(s["table_ok"], 1)
                    v.wait_ge(s["tab_ps"], 1)
                    step(v.tensor_copy(tab[0:1, 0:P], psum[0:1, 2, 384:512]))
                    v.sem_inc(s["tab_ok"], 1)

                def shared(t):
                    r = rows(t)
                    v.wait_ge(s["ssil"], t + 1)
                    if t:
                        v.wait_ge(s["sht"], t)
                    v.tensor_tensor(hid[0:r], psum[0:r, 7 * (t % 2), FE:], sil[0:r], ALU.mult).then_inc(s["shid"], 1)

                groups()
                shared(0)
                choose()
                shared(1)
                queues()
                shared(2)
                fill_table()
                for b in range(3):
                    who(v, b, b)
                shared(3)
                for b in range(3):
                    read_list(v, b, b)
                shared(4)
                take_rows_v(v, 0, 0)
                nb = trips(v)
                with v.Fori(0, TRIPS) as i:
                    with v.If(nb > i):
                        for u in range(3):
                            b = 3 * i + u
                            v.wait_ge(moved[u], 32 * i + 16)
                            v.tensor_scalar(row[:, u, :], got[:, u, 1:2], float(TOPK * OUTSIDE), None, ALU.add).then_inc(s["now_ok"], 1)
                            v.tensor_copy(now_gate[:, u:u + 1], got[:, u, 2:3]).then_inc(s["now_ok"], 1)
                            v.wait_ge(s["list_mm"], b + 1)
                            who(v, b + 3, u)
                            v.wait_ge(s["sil_ok"], b + 1)
                            v.tensor_tensor(hid, psum[:, 0, FE:], sil, ALU.mult).then_inc(s["hid_ok"], 1)
                            v.wait_ge(s["now_ok"], 2 * b + 2)
                            take_rows_v(v, b + 1, (u + 1) % 3)
                            read_list(v, b + 3, u)
                            v.wait_ge(s["dn"], 2 * b + 2 + DN0)
                            v.tensor_scalar(out[:, u, 512:], psum[:, 5, :], now_gate[:, u:u + 1], None, ALU.mult).then_inc(s["out_hi"], 1)

            @block.tensor
            def _(pe):
                pe.wait_ge(wout_in, 16)

                def turn_attn(t):
                    r = rows(t)
                    pe.wait_ge(s["an_ok"], t + 1)
                    if t:
                        pe.wait_ge(s["aT_ok"], t)
                    for c in range(WC):
                        last = pe.transpose(psum[:, 0, c * P:c * P + r], attn[0:r, t, c * P:(c + 1) * P], ident[0:r, 0:r])
                    last.then_inc(s["aT_ps"], 1)

                def conv_product(t):
                    r = rows(t)
                    if t:
                        pe.wait_ge(s["tc_ok"], t)
                    for n in range(2):
                        for c in range(WC):
                            last = pe.matmul(psum[0:r, 4 + n, :], convg[:, c, t * P:t * P + r],
                                             wout[:, WC + c, n * 512:(n + 1) * 512], start=(c == 0), stop=(c == WC - 1))
                    last.then_inc(s["prod_c"], 1)

                def attn_product(t):
                    r = rows(t)
                    if t:
                        pe.wait_ge(s["x2_ok"], t)
                    pe.wait_ge(s["aT_ok"], t + 1)
                    for n in range(2):
                        for c in range(WC):
                            last = pe.matmul(psum[0:r, 2 + n, :], aT[:, t % 2, c, 0:r],
                                             wout[:, c, n * 512:(n + 1) * 512], start=(c == 0), stop=(c == WC - 1))
                    last.then_inc(s["prod_a"], 1)

                def route(m):
                    r = rows(m)
                    pe.wait_ge(s["h2_ok"], m + 1)
                    for half in range(2):
                        if m:
                            pe.wait_ge(s["h2_sb"], 2 * m - 1 + half)
                        for k in range(4):
                            kk = 4 * half + k
                            last = pe.transpose(psum[:, 6 + half, k * P:k * P + r],
                                                work[0:r, 1 + m % 2, kk * P:(kk + 1) * P], ident[0:r, 0:r])
                        last.then_inc(s["h2_ps"], 1)
                    pe.wait_ge(s["h2_sb"], 2 * m + 2)
                    if m == 0:
                        pe.wait_ge(s["small_in"], 32)
                    for k in range(KC):
                        last = pe.matmul(psum[0:r, 1, m * NE:(m + 1) * NE], h2T[:, k, m * P:m * P + r], wr[:, k, :],
                                         start=(k == 0), stop=(k == KC - 1))
                    last.then_inc(s["logit"], 1)

                for t in range(NT):
                    if t == 0:
                        conv_product(t)
                    turn_attn(t)
                    if t:
                        conv_product(t)
                    attn_product(t)
                    if t >= 2:
                        route(t - 2)
                route(NT - 2)

                lhs = lambda t: lambda k: h2T[:, k, t * P:t * P + rows(t)]
                pe.wait_ge(shared_in, 48)
                pe.wait_ge(s["aT_ok"], NT)
                gate_up(pe, 0, P, lhs(0), wslot[0], s["sgu"])
                route(NT - 1)
                for t in range(NT):
                    r = rows(t)
                    if t + 1 < NT:
                        if t:
                            pe.wait_ge(s["shid"], t)
                        gate_up(pe, 7 * ((t + 1) % 2), rows(t + 1), lhs(t + 1), wslot[0], s["sgu"])
                    if t == 1:
                        pe.wait_ge(s["mask_ok"], 1)
                        for a in range(NT):
                            for c in range(a + 1):
                                pe.matmul(psum[:, 2, a * NE:(a + 1) * NE], trib if c == a else oneb, maskb[:, c, :],
                                          start=(c == 0), stop=(c == a))
                        for c in range(NT):
                            last = pe.matmul(psum[:, 2, NT * NE:(NT + 1) * NE], oneb, maskb[:, c, :],
                                             start=(c == 0), stop=(c == NT - 1))
                        last.then_inc(s["cnt_ps"], 1)
                    if t == 2:
                        pe.wait_ge(s["table_ok"], 1)
                        pe.transpose(psum[0:1, 2, 384:512], blkf, ident).then_inc(s["tab_ps"], 1)
                    if t == 3:
                        for b in range(3):
                            fill_list(pe, b, b)
                    pe.wait_ge(s["shid"], t + 1)
                    turn_hidden(pe, r, s["sht"])
                    pe.wait_ge(s["shT"], t + 1)

                    def free(n):
                        if t:
                            pe.wait_ge(s[("out_lo", "out_hi")[n]], t)

                    down(pe, r, wslot[0], s["dn"], free)
                pe.wait_ge(s["tab_ok"], 1)
                pe.wait_ge(moved[0], 16)
                turn_rows(pe, 0, range(KC))
                nb = trips(pe)
                with pe.Fori(0, TRIPS) as i:
                    with pe.If(nb > i):
                        for u in range(3):
                            b = 3 * i + u
                            n1 = (u + 1) % 3
                            w = wslot[n1]
                            pe.wait_ge(w_in[u], 48 * i + 48)
                            pe.wait_ge(s["xt_a"], b + 1)
                            pe.wait_ge(s["xt_v"], b + 1)
                            gate_up(pe, 0, P, lambda k: xT[:, u, k, :], w, s["gu"])
                            pe.wait_ge(moved[n1], 32 * i + (16 if u < 2 else 48))
                            turn_rows(pe, n1, range(6))
                            pe.wait_ge(s["hid_ok"], b + 1)
                            turn_hidden(pe, P, s["ht_ps"])
                            turn_rows(pe, n1, range(6, KC))
                            fill_list(pe, b + 3, u)
                            pe.wait_ge(s["ht_ok"], b + 1)
                            down(pe, P, w, s["dn"], lambda n: pe.wait_ge(s[("out_lo", "out_hi")[n]], b + NT))
        stage_4(x2, ysh, gate2, gfin, room[:, 3 * D:3 * D + 3 * NT].rearrange("p (a t) -> p a t", a=3), work)
        st.close()

    def stage_4(x2, ysh, gate2, gfin, ss, work):
        ring = stream[:, 0:3 * TOPK * D].rearrange("p (s k n) -> p s k n", s=3, k=TOPK)
        H = TOPK // 2
        sums, sum_read, y_ok, ms, rs = (sem(f"s4_{n}") for n in ("sums", "sum_read", "y_ok", "ms", "rs"))
        first_in = [sem(f"s4_first{i}") for i in range(3)]
        second_in = [sem(f"s4_second{i}") for i in range(3)]
        y_out = [sem(f"s4_y_out{i}") for i in range(2)]
        v_step = sem("s4_v_step")
        rows_of = expert_rows.rearrange("(n k) d -> n k d", k=TOPK)

        with nc.Block() as block:
            @block.sync
            def _(sp):
                for t in range(NT):
                    r = rows(t)
                    if t >= 3:
                        sp.wait_ge(y_ok, t - 2)
                    for a, signal in ((0, first_in), (H, second_in)):
                        sp.dma_start(ring[0:r, t % 3, a:a + H, :],
                                     rows_of[t * P:t * P + r, a:a + H, :]).then_inc(signal[t % 3], 16)
                sp.wait_ge(stored, 16 * n_stores[0])

            @block.gpsimd
            def _(pool):
                for t in range(NT):
                    r = rows(t)
                    pool.wait_ge(ms, t + 1)
                    pool.tensor_tensor(ss[0:r, 2, t:t + 1], ss[0:r, 1, t:t + 1], cst[0:r, C_POW:C_POW + 1], ALU.pow).then_inc(rs, 1)

            @block.scalar
            def _(act):
                for t in range(NT):
                    act.wait_ge(y_ok, t + 1)
                    dst = (io["y_prompt"][0, t * P:(t + 1) * P, :] if t < NPT else
                           io["y_sample"].rearrange("b t n -> (b t) n"))
                    act.dma_start(dst, work[0:rows(t), t % 2, :]).then_inc(y_out[t % 2], 16)
                act.wait_ge(y_out[0], 3 * 16)
                act.wait_ge(y_out[1], 2 * 16)

            @block.tensor
            def _(pe):
                for t in range(NT):
                    r = rows(t)
                    pe.wait_ge(first_in[t % 3], 16 * (t // 3 + 1))
                    if t >= 2:
                        pe.wait_ge(sum_read, t - 1)
                    for n in range(2):
                        cols = slice(n * 512, (n + 1) * 512)
                        pe.matmul(psum[0:r, 2 * (t % 2) + n, :], ident[0:r, 0:r], ysh[0:r, t, cols], start=True, stop=False)
                        for k in range(H):
                            last = pe.matmul(psum[0:r, 2 * (t % 2) + n, :], ident[0:r, 0:r], ring[0:r, t % 3, k, cols],
                                             start=False, stop=(k == H - 1))
                    last.then_inc(sums, 1)

            @block.vector
            def _(v):
                n_step = [0]

                def step(ins):
                    n_step[0] += 1
                    ins.then_inc(v_step, 1)
                    v.wait_ge(v_step, n_step[0])

                for t in range(NT):
                    r, b = rows(t), 2 * (t % 2)
                    y = work[0:r, t % 2, :]
                    v.wait_ge(second_in[t % 3], 16 * (t // 3 + 1))
                    if t >= 2:
                        v.wait_ge(y_out[t % 2], 16 * (t // 2))
                    step(v.tensor_tensor(y, ring[0:r, t % 3, H, :], ring[0:r, t % 3, H + 1, :], ALU.add))
                    for k in range(H + 2, TOPK):
                        step(v.tensor_tensor(y, y, ring[0:r, t % 3, k, :], ALU.add))
                    v.wait_ge(sums, t + 1)
                    step(v.tensor_tensor(y, psum[0:r, b:b + 2, :].rearrange("p a n -> p (a n)"), y, ALU.add))
                    v.sem_inc(sum_read, 1)
                    if t == 0:
                        v.wait_ge(last_in, 48)
                    step(v.tensor_tensor(y, y, gate2[0:r, t // NPT, :], ALU.mult))
                    step(v.tensor_tensor(x2[0:r, t, :], x2[0:r, t, :], y, ALU.add))
                    step(v.tensor_tensor_reduce(y, x2[0:r, t, :], x2[0:r, t, :], 1.0, 0.0, ALU.mult, ALU.add, ss[0:r, 0, t:t + 1]))
                    step(v.tensor_scalar(ss[0:r, 1, t:t + 1], ss[0:r, 0, t:t + 1], 1.0 / D, EPS, ALU.mult, ALU.add))
                    v.sem_inc(ms, 1)
                    v.wait_ge(rs, t + 1)
                    v.scalar_tensor_tensor(y, x2[0:r, t, :], ss[0:r, 2, t:t + 1], gfin[0:r], ALU.mult, ALU.mult).then_inc(y_ok, 1)

    kv = ExitStack()
    keeps = {n: kv.enter_context(nc.sbuf_tensor("sb_" + n, [P, NT, W], F32)) for n in "kv"}
    stage_1()
    stage_2()
    kv.close()
    stage_3()
    ctx.close()


_INS = ['x_prompt', 'x_sample', 'c_prompt', 'c_sample', 'cache_k', 'cache_v', 'state_conv', 'w_ada', 'b_ada',
        'w_in', 'conv_w', 'g_attn_out', 'g_conv_out', 'w_out', 'w_router', 'router_bias', 'w_exp_gate',
        'w_exp_up', 'w_exp_down', 'w_sh_gate', 'w_sh_up', 'w_sh_down', 'g_final']
_OUTS = {'y_prompt': (1, SEQ, D), 'y_sample': (DEC_B, DEC_T, D),
         'k_prompt': (1, 1, SEQ, HEADS, HD), 'v_prompt': (1, 1, SEQ, HEADS, HD), 'conv_prompt': (1, 1, 2, W),
         'k_sample': (1, DEC_B, DEC_T, HEADS, HD), 'v_sample': (1, DEC_B, DEC_T, HEADS, HD),
         'conv_sample': (1, DEC_B, 2, W)}


def build(nc, shapes):
    io = {n: nc.dram_tensor(n, s, F32, kind="ExternalInput").ap() for n, s in shapes.items()}
    io |= {n: nc.dram_tensor(n, s, F32, kind="ExternalOutput").ap() for n, s in _OUTS.items()}
    layer(nc, io)


def kernel(**inputs):
    import concourse.bacc as bacc
    from concourse.bass_utils import run_bass_kernel_spmd

    arrays = {n: np.ascontiguousarray(inputs[n]) for n in _INS}
    for n, a in zip(("cst", "masks", "rope"), constants()):
        arrays[n] = a
    nc = bacc.Bacc("TRN2", target_bir_lowering=False, num_devices=1)
    build(nc, {n: a.shape for n, a in arrays.items()})
    r = run_bass_kernel_spmd(nc, [arrays], core_ids=[0])
    return tuple(r.results[0][n] for n in _OUTS)
```

```python
import numpy as np
from contextlib import ExitStack

import concourse.bass as bass
from concourse import mybir

F32 = mybir.dt.float32
BF16 = mybir.dt.bfloat16
I32 = mybir.dt.int32
U32 = mybir.dt.uint32
ALU = mybir.AluOpType
ACT = mybir.ActivationFunctionType
AX = mybir.AxisListType

P = 128
D = 1024
KC = D // P
SEQ, DEC_B, DEC_T = 512, 8, 4
NS = DEC_B * DEC_T
NTOK = SEQ + NS
NPT = SEQ // P
NT = NPT + 1
HEADS, HD = 8, 64
W = HEADS * HD
WC = W // P
PAST, WIN = 2048, 512
WIN0 = PAST - WIN
SPARSE = WIN0 // 16
SK = WIN + 4 * SPARSE + NS
NE, TOPK, NGRP, GSZ = 64, 8, 8, 8
FE = 256
EPS = 1e-6
NADA, NIN = 12, 6
MAXB = (NTOK * TOPK + NE * (P - 1)) // P
TRIPS = -(-MAXB // 3)
OUTSIDE = 8192
BRANCHES = ((128, 1), (512, 4), (2048, 16))

C_ID, C_IOTA, C_ROUND, C_TRI, C_ONE = 0, 128, 256, 384, 512
C_LOW, C_VALID, C_MOD, C_DIV, C_TRIP, C_LP = 640, 704, 709, 710, 711, 744
C_POW = C_LP + NT * 5
C_END = C_POW + 1
A_PM, A_PN = 0, 512
A_SM = 1024
A_SN = A_SM + 2 * SK
A_BD = A_SN + 2 * SK
A_SEL = A_BD + W
A_END = A_SEL + 2 * NS


def rows(t):
    return P if t < NPT else NS


def branch_count(dist):
    n = np.zeros(dist.shape, np.float32)
    for w, d in BRANCHES:
        n += (dist >= 0) & (dist <= w) & (dist % d == 0)
    return n


def constants():
    p = np.arange(P)
    c = np.zeros((P, C_END), np.float32)
    c[:, C_ID:C_ID + P] = np.eye(P)
    c[:, C_IOTA:C_IOTA + P] = p[None]
    c[:, C_ROUND:C_ROUND + P] = P * (p[None] // 3)
    c[:, C_TRI:C_TRI + P] = p[:, None] < p[None]
    c[:, C_ONE:C_ONE + P] = 1
    g = np.arange(NGRP)
    c[:, C_LOW:C_LOW + 64] = (g[None] < g[:, None]).ravel()[None]
    for t in range(NT):
        c[:, C_VALID + t] = p < rows(t)
        c[:, C_LP + 5 * t + 0] = p
        c[:, C_LP + 5 * t + 1] = P * t - OUTSIDE
        c[:, C_LP + 5 * t + 3] = TOPK * p
        c[:, C_LP + 5 * t + 4] = TOPK * (P * t - OUTSIDE)
    c[:, C_POW] = -0.5
    c[:, C_MOD], c[:, C_DIV] = p % 3, p // 3
    c[:, C_TRIP:C_TRIP + TRIPS] = 3 * np.arange(TRIPS)[None]

    a = np.zeros((P, A_END), np.float32)
    for n, diff in enumerate(range(NPT - 1, -1, -1)):
        m = branch_count(P * diff + p[:, None] - p[None])
        a[:, A_PM + n * P:A_PM + (n + 1) * P] = m
    a[:, A_PN:A_PN + 512] = np.where(a[:, A_PM:A_PM + 512] > 0, 0, -1e30)
    pos = np.concatenate([(WIN0 + 4 * p[None] + np.arange(4)[:, None]).ravel(),
                          (16 * np.arange(SPARSE)[None] + np.arange(4)[:, None]).ravel()])
    q = p % DEC_T
    for grp in range(2):
        m = np.zeros((P, SK), np.float32)
        m[:, :len(pos)] = branch_count(PAST + q[:, None] - pos[None])
        batch = 4 * grp + p // 32
        kb, kt = np.arange(NS) // DEC_T, np.arange(NS) % DEC_T
        m[:, len(pos):] = branch_count(q[:, None] - kt[None]) * (kb[None] == batch[:, None])
        a[:, A_SM + grp * SK:A_SM + (grp + 1) * SK] = m
        a[:, A_SN + grp * SK:A_SN + (grp + 1) * SK] = np.where(m > 0, 0, -1e30)
        a[:, A_SEL + grp * NS:A_SEL + (grp + 1) * NS] = (batch * DEC_T + q)[:, None] == np.arange(NS)[None]
    a[:, A_BD:A_BD + W] = (np.arange(W)[None] // HD) == ((p % 32) // DEC_T)[:, None]

    half = HD // 2
    inv = (10000.0 ** (-np.arange(half) / half)).astype(np.float32)
    where = np.zeros((NT, P), np.float32)
    where[:NPT] = np.arange(SEQ).reshape(NPT, P)
    where[NPT, :NS] = PAST + np.arange(NS) % DEC_T
    ang = (where[:, :, None] * inv[None, None]).astype(np.float32)
    cos, sin = np.cos(ang).astype(np.float32), np.sin(ang).astype(np.float32)
    r = np.concatenate([np.concatenate([cos, cos], -1), np.concatenate([-sin, sin], -1)], 0)
    r = np.ascontiguousarray(r.transpose(1, 0, 2).reshape(P, 2 * NT * HD))
    return c, a, r


def layer(nc, io):
    ctx = ExitStack()

    def sem(name):
        return ctx.enter_context(nc.semaphore(name))

    def keep(name, shape, dt=F32):
        return ctx.enter_context(nc.sbuf_tensor("sb_" + name, shape, dt))

    psum = ctx.enter_context(nc.psum_tensor("psum", [P, 8, 512], F32))

    mod_rows = nc.dram_tensor("mod_rows", (1 + DEC_B, 6 * D), F32, kind="Internal").ap()
    h_rows = nc.dram_tensor("h_rows", (NTOK, D), F32, kind="Internal").ap()
    expert_rows = nc.dram_tensor("expert_rows", (NTOK * TOPK, D), F32, kind="Internal").ap()

    cst = keep("cst", [P, C_END])
    stream = keep("stream", [P, 96 * 256])
    convg = keep("convg", [P, WC, NTOK])
    attn_sq = keep("attn_sq", [P, NT])
    conv_r = keep("conv_r", [P, NT])
    attn = keep("attn", [P, NT, W])
    gains = keep("gains", [P, 2, WC])
    ident = cst[:, C_ID:C_ID + P]

    stored = sem("stored")
    n_stores = [0]

    def store(eng, dst, src):
        n_stores[0] += 1
        return eng.dma_start(dst, src).then_inc(stored, 16)

    def bc_row(ap_row, n):
        return ap_row.broadcast_to([n, ap_row.shape[1]])

    def mod_sample(j):
        return mod_rows[1:1 + DEC_B, j * D:(j + 1) * D].unsqueeze(1).broadcast_to([DEC_B, DEC_T, D])

    last_in = sem("last_in")

    def stage_1():
        st = ExitStack()

        def tmp(name, shape, dt=F32):
            return st.enter_context(nc.sbuf_tensor("sb_" + name, shape, dt))

        k_sb, v_sb = keeps["k"], keeps["v"]
        q_sb = attn
        xh = tmp("xh", [P, NT, D])
        hT = tmp("hT", [P, KC, NTOK])
        bc_shift = tmp("bc_shift", [P, 2, D])
        bc_scale = tmp("bc_scale", [P, 2, D])
        up = tmp("up", [P, WC, 2 + SEQ])
        us = tmp("us", [P, WC, DEC_B, 2 + DEC_T])
        rope = tmp("rope", [P, 2, NT, HD])
        rot = tmp("rot", [P, 2, W])
        c_sb = hT[0:1 + DEC_B, :, :].rearrange("p k n -> p (k n)")[:, 0:D]
        cT = tmp("cT", [P, KC, 1 + DEC_B])
        c_flat = cT[:, :, :].rearrange("p k n -> p (k n)")
        c_tmp = [rot[:, 0, n * 128:n * 128 + KC * 9] for n in range(3)]
        convw = tmp("convw", [P, 3, WC])
        rest = 4 * 4096 + 6 * D
        state = stream[0:2 * DEC_B, rest:rest + W]
        ss = tmp("ss", [P, 2, NT])
        cs = tmp("cs", [P, NT])
        tail = tmp("tail", [P, WC, 2 + 2 * DEC_B])
        tail_rows = stream[0:2 + 2 * DEC_B, rest + W:rest + 2 * W]
        ring = stream[:, 0:4 * 4096].rearrange("p (s k n) -> p s k n", s=4, k=KC)
        mod = stream[0:1 + DEC_B, 4 * 4096:4 * 4096 + 6 * D]
        flat = xh[:, :, :].rearrange("p t n -> p (t n)")
        hcT = flat[:, 0:WC * NTOK].rearrange("p (c n) -> p c n", c=WC)
        convT = flat[:, WC * NTOK:2 * WC * NTOK].rearrange("p (c n) -> p c n", c=WC)

        w_in = [sem(f"s1_w{i}") for i in range(4)]
        w_used = sem("s1_w_used")
        cst_in, c_in, bias_in, x_in, small_in = (sem(f"s1_{n}") for n in
                                                 ("cst_in", "c_in", "bias_in", "x_in", "small_in"))
        c_exp, cT_ps, cT_ok = (sem(f"s1_{n}") for n in ("c_exp", "cT_ps", "cT_ok"))
        mod_ok, mod_out, bc_in = (sem(f"s1_{n}") for n in ("mod_ok", "mod_out", "bc_in"))
        h_ok, hT_ps, hT_a, hT_v = (sem(f"s1_{n}") for n in ("h_ok", "hT_ps", "hT_a", "hT_v"))
        proj, qk_ok, v_ok = (sem(f"s1_{n}") for n in ("proj", "qk_ok", "v_ok"))
        cmm, hc_ok, gcb_ok = (sem(f"s1_{n}") for n in ("cmm", "hc_ok", "gcb_ok"))
        st_ps, st_ok, pads = (sem(f"s1_{n}") for n in ("st_ps", "st_ok", "pads"))
        sq_ok, ssq_ps, tail_ok, tail_ps, tail_sb = (sem(f"s1_{n}") for n in
                                                    ("sq_ok", "ssq_ps", "tail_ok", "tail_ps", "tail_sb"))
        ms_ok, cms_ok, rs_ok = (sem(f"s1_{n}") for n in ("ms_ok", "cms_ok", "rs_ok"))
        v_step = sem("s1_v_step")

        order = [3, 5, 4, 0, 1, 2]

        with nc.Block() as block:
            @block.sync
            def _(sp):
                sp.dma_start(c_sb[0:1, :], io["c_prompt"]).then_inc(c_in, 16)
                sp.dma_start(c_sb[1:, :], io["c_sample"]).then_inc(c_in, 16)
                sp.dma_start(cst[:, :], io["cst"]).then_inc(cst_in, 16)
                for n in range(NADA + NIN):
                    if n >= 4:
                        if n - 4 < NADA:
                            sp.wait_ge(w_used, n - 3)
                        else:
                            sp.wait_ge(cmm, WC * (n - 3 - NADA))
                    src = (io["w_ada"][0][:, n * 512:(n + 1) * 512] if n < NADA else
                           io["w_in"][0][:, order[n - NADA] * W:(order[n - NADA] + 1) * W])
                    sp.dma_start(ring[:, n % 4], src.rearrange("(k p) n -> p k n", p=P)).then_inc(w_in[n % 4], 16)
                sp.wait_ge(qk_ok, 2 * NT)
                sp.wait_ge(v_ok, NT)
                for name, src in (("k", k_sb), ("v", v_sb)):
                    store(sp, io[name + "_prompt"].rearrange("a b (t p) h d -> p (a b t) (h d)", p=P), src[:, 0:NPT, :])
                    store(sp, io[name + "_sample"].rearrange("a b t h d -> (a b t) (h d)"), src[0:NS, NPT, :])
                sp.wait_ge(tail_sb, 1)
                store(sp, io["conv_prompt"].rearrange("a b t n -> (a b t) n"), tail_rows[0:2, :])
                store(sp, io["conv_sample"].rearrange("a b t n -> (a b t) n"), tail_rows[2:, :])

            @block.gpsimd
            def _(pool):
                pool.memset(v_sb[:, NPT, :], 0.0).then_inc(pads, 1)
                pool.memset(up[:, :, 0:2], 0.0).then_inc(pads, 1)
                pool.dma_start(rope[:, :, :, :], io["rope"].rearrange("p (a t n) -> p a t n", a=2,
                        t=NT)).then_inc(small_in, 16)
                pool.dma_start(state[:, :], io["state_conv"].rearrange("a b t n -> (a b t) n")).then_inc(small_in, 16)
                for j in range(3):
                    pool.dma_start(convw[:, j, :], io["conv_w"][0, j].rearrange("(c p) -> p c", p=P),
                                   allow_slow_non_contiguous=True).then_inc(small_in, 16)
                for j, g in enumerate(("g_attn_out", "g_conv_out")):
                    pool.dma_start(gains[:, j, :], io[g][0].rearrange("(c p) -> p c", p=P),
                                   allow_slow_non_contiguous=True).then_inc(small_in, 16)
                pool.wait_ge(cst_in, 16)
                for ready, dst, src in ((ms_ok, ss[:, 0], ss[:, 1]), (cms_ok, conv_r, cs)):
                    pool.wait_ge(ready, 1)
                    for r, a, b in ((P, 0, NPT), (NS, NPT, NT)):
                        pool.tensor_tensor(dst[0:r, a:b], src[0:r, a:b], cst[0:r, C_POW:C_POW + 1].broadcast_to([r,
                                b - a]), ALU.pow).then_inc(rs_ok, 1)
                pool.wait_ge(rs_ok, 4)

            @block.scalar
            def _(act):
                act.dma_start(mod, bc_row(io["b_ada"], 1 + DEC_B)).then_inc(bias_in, 16)
                act.wait_ge(cT_ps, 1)
                act.activation(c_tmp[0], psum[:, 0, 0:KC * 9], ACT.Exp, scale=-1.0).then_inc(c_exp, 1)
                act.dma_start(xh[:, 0:NPT, :], io["x_prompt"][0].rearrange("(t p) n -> p t n", p=P)).then_inc(x_in, 16)
                act.dma_start(xh[0:NS, NPT, :], io["x_sample"].rearrange("b t n -> (b t) n")).then_inc(x_in, 16)
                for n in range(NADA):
                    act.wait_ge(mod_ok, n + 1)
                    act.dma_start(mod_rows[:, n * 512:(n + 1) * 512], mod[:, n * 512:(n + 1) * 512]).then_inc(mod_out, 16)
                    if n == 3:
                        act.wait_ge(mod_out, 64)
                        for j, dst in ((0, bc_shift), (1, bc_scale)):
                            act.dma_start(dst[:, 0, :], bc_row(mod_rows[0:1, j * D:(j + 1) * D], P)).then_inc(bc_in, 16)
                            act.dma_start(dst[0:NS, 1, :], mod_sample(j)).then_inc(bc_in, 16)
                for t in range(NT):
                    act.wait_ge(hT_ps, 2 * t + 1)
                    act.copy(hT[:, 0:4, t * P:t * P + rows(t)],
                             psum[:, 3 + (2 * t) % 4, :].rearrange("p (k n) -> p k n", k=4)[:, :,
                                     0:rows(t)]).then_inc(hT_a, 1)
                for m in range(WC):
                    act.wait_ge(cmm, m + 1)
                    act.copy(hcT[:, m, 0:SEQ], psum[:, 3 + m % 2, :])
                    act.copy(hcT[:, m, SEQ:], psum[:, 5 + m % 2, 0:NS]).then_inc(hc_ok, 1)
                act.wait_ge(small_in, 7 * 16)
                for m in range(WC):
                    act.wait_ge(gcb_ok, WC + m + 1)
                    act.activation(hcT[:, m, :], convT[:, m, :], ACT.Square).then_inc(sq_ok, 1)
                    act.activation(convg[:, m, :], convT[:, m, :], ACT.Copy, scale=gains[:, 1, m:m + 1]).then_inc(sq_ok, 1)
                act.wait_ge(pads, 1)
                for t in range(NT):
                    act.wait_ge(proj, 2 * NT + t + 1)
                    act.copy(v_sb[0:rows(t), t, :], psum[0:rows(t), (2 * NT + t) % 3, :]).then_inc(v_ok, 1)
                act.wait_ge(mod_out, NADA * 16)

            @block.vector
            def _(v):
                n_step = [0]

                def step(ins):
                    n_step[0] += 1
                    ins.then_inc(v_step, 1)

                def settle():
                    v.wait_ge(v_step, n_step[0])

                v.wait_ge(c_exp, 1)
                step(v.tensor_scalar(c_tmp[1], c_tmp[0], 1.0, None, ALU.add))
                settle()
                step(v.reciprocal(c_tmp[2], c_tmp[1]))
                settle()
                step(v.tensor_tensor(c_flat, c_tmp[2], psum[:, 0, 0:KC * 9], ALU.mult))
                settle()
                v.sem_inc(cT_ok, 1)
                v.wait_ge(bias_in, 16)
                for n in range(NADA):
                    v.wait_ge(w_used, n + 1)
                    v.tensor_tensor(mod[:, n * 512:(n + 1) * 512], psum[0:9, 1 + n % 2, :],
                                    mod[:, n * 512:(n + 1) * 512], ALU.add).then_inc(mod_ok, 1)
                    if n == 1:
                        v.wait_ge(x_in, 32)
                        for t in range(NT):
                            r = rows(t)
                            settle()
                            step(v.tensor_tensor_reduce(rot[0:r, :, :].rearrange("p a n -> p (a n)"), xh[0:r, t, :], xh[0:r, t, :],
                                                        1.0, 0.0, ALU.mult, ALU.add, ss[0:r, 0, t:t + 1]))
                    if n == 2:
                        settle()
                        for r, a, b in ((P, 0, NPT), (NS, NPT, NT)):
                            step(v.tensor_scalar(ss[0:r, 1, a:b], ss[0:r, 0, a:b], 1.0 / D, EPS, ALU.mult, ALU.add))
                        settle()
                        v.sem_inc(ms_ok, 1)
                    if n == 6:
                        v.wait_ge(rs_ok, 2)
                        v.wait_ge(bc_in, 64)
                        step(v.tensor_scalar(bc_scale[:, 0, :], bc_scale[:, 0, :], 1.0, None, ALU.add))
                        step(v.tensor_scalar(bc_scale[0:NS, 1, :], bc_scale[0:NS, 1, :], 1.0, None, ALU.add))
                    if n > 6:
                        t = n - 7
                        r, s = rows(t), t // NPT
                        settle()
                        step(v.scalar_tensor_tensor(xh[0:r, t, :], xh[0:r, t, :], ss[0:r, 0, t:t + 1],
                                                    bc_scale[0:r, s, :], ALU.mult, ALU.mult))
                        settle()
                        v.tensor_tensor(xh[0:r, t, :], xh[0:r, t, :], bc_shift[0:r, s, :], ALU.add).then_inc(h_ok, 1)
                for t in range(NT):
                    v.wait_ge(hT_ps, 2 * t + 2)
                    v.tensor_copy(hT[:, 4:8, t * P:t * P + rows(t)],
                                  psum[:, 3 + (2 * t + 1) % 4, :].rearrange("p (k n) -> p k n", k=4)[:, :,
                                          0:rows(t)]).then_inc(hT_v, 1)
                v.wait_ge(small_in, 7 * 16)
                v.wait_ge(st_ps, 1)
                v.tensor_copy(us[:, :, :, 0:2], psum[:, 7, 0:64].rearrange("p (c b i) -> p c b i", c=WC,
                        b=DEC_B)).then_inc(st_ok, 1)
                v.wait_ge(pads, 2)
                v.wait_ge(st_ok, 1)
                for m in range(WC):
                    v.wait_ge(cmm, WC + m + 1)
                    v.wait_ge(hc_ok, m + 1)
                    uss = us[:, m, :, :]
                    b = (WC + m) % 2
                    step(v.tensor_tensor(up[:, m, 2:], psum[:, 3 + b, :], hcT[:, m, 0:SEQ], ALU.mult))
                    step(v.tensor_tensor(uss[:, :, 2:], psum[:, 5 + b, 0:NS].rearrange("p (b t) -> p b t", b=DEC_B),
                                         hcT[:, m, SEQ:].rearrange("p (b t) -> p b t", b=DEC_B), ALU.mult))
                    settle()
                    v.sem_inc(gcb_ok, 1)
                    cp = convT[:, m, 0:SEQ]
                    cq = convT[:, m, SEQ:].rearrange("p (b t) -> p b t", b=DEC_B)
                    for j in range(3):
                        wj = convw[:, j, m:m + 1]
                        if j == 0:
                            step(v.tensor_scalar(cp, up[:, m, 0:SEQ], wj, None, ALU.mult))
                            step(v.tensor_scalar(cq, uss[:, :, 0:DEC_T], wj, None, ALU.mult))
                        else:
                            settle()
                            step(v.scalar_tensor_tensor(cp, up[:, m, j:j + SEQ], wj, cp, ALU.mult, ALU.add))
                            step(v.scalar_tensor_tensor(cq, uss[:, :, j:j + DEC_T], wj, cq, ALU.mult, ALU.add))
                step(v.tensor_copy(tail[:, :, 0:2], up[:, :, SEQ:SEQ + 2]))
                step(v.tensor_copy(tail[:, :, 2:].rearrange("p c (b i) -> p c b i", b=DEC_B), us[:, :, :, DEC_T:]))
                settle()
                v.sem_inc(tail_ok, 1)
                for m in range(WC):
                    v.wait_ge(cmm, 2 * WC + m + 1)
                    b = (2 * WC + m) % 2
                    step(v.tensor_tensor(convT[:, m, 0:SEQ], psum[:, 3 + b, :], convT[:, m, 0:SEQ], ALU.mult))
                    step(v.tensor_tensor(convT[:, m, SEQ:], psum[:, 5 + b, 0:NS], convT[:, m, SEQ:], ALU.mult))
                    settle()
                    v.sem_inc(gcb_ok, 1)
                for j, dst in ((0, q_sb), (1, k_sb)):
                    if j == 1:
                        v.wait_ge(tail_ps, 1)
                        v.tensor_copy(tail_rows[:, :], psum[0:18, 3, :]).then_inc(tail_sb, 1)
                        v.wait_ge(ssq_ps, 1)
                        for r, a, b in ((P, 0, NPT), (NS, NPT, NT)):
                            step(v.tensor_scalar(cs[0:r, a:b], psum[0:r, 7, 64 + a:64 + b], 1.0 / W, EPS, ALU.mult, ALU.add))
                        settle()
                        v.sem_inc(cms_ok, 1)
                    for t in range(NT):
                        r, n = rows(t), j * NT + t
                        v.wait_ge(proj, n + 1)
                        src = psum[0:r, n % 3, :].rearrange("p (h d) -> p h d", h=HEADS)
                        ra = rot[0:r, 0, :].rearrange("p (h d) -> p h d", h=HEADS)
                        rb = rot[0:r, 1, :].rearrange("p (h d) -> p h d", h=HEADS)
                        cos = rope[0:r, 0, t, :].unsqueeze(1).broadcast_to([r, HEADS, HD])
                        sin = rope[0:r, 1, t, :].unsqueeze(1).broadcast_to([r, HEADS, HD])
                        h = HD // 2
                        settle()
                        step(v.tensor_tensor(ra, src, cos, ALU.mult))
                        step(v.tensor_tensor(rb[:, :, 0:h], src[:, :, h:], sin[:, :, 0:h], ALU.mult))
                        step(v.tensor_tensor(rb[:, :, h:], src[:, :, 0:h], sin[:, :, h:], ALU.mult))
                        settle()
                        n_step[0] += 1
                        v.tensor_tensor(dst[0:r, t, :], rot[0:r, 0, :], rot[0:r, 1, :], ALU.add).then_inc(v_step, 1)
                        settle()
                        v.sem_inc(qk_ok, 1)

            @block.tensor
            def _(pe):
                pe.wait_ge(cst_in, 16)
                pe.wait_ge(c_in, 32)
                for k in range(KC):
                    last = pe.transpose(psum[:, 0, 9 * k:9 * k + 9], c_sb[:, k * P:(k + 1) * P], ident[0:9, 0:9])
                last.then_inc(cT_ps, 1)
                pe.wait_ge(cT_ok, 1)
                for n in range(NADA):
                    pe.wait_ge(w_in[n % 4], 16 * (n // 4 + 1))
                    if n >= 2:
                        pe.wait_ge(mod_ok, n - 1)
                    for k in range(KC):
                        last = pe.matmul(psum[0:9, 1 + n % 2, :], cT[:, k, :], ring[:, n % 4, k, :],
                                         start=(k == 0), stop=(k == KC - 1))
                    last.then_inc(w_used, 1)
                pe.wait_ge(small_in, 7 * 16)
                for m in range(WC):
                    last = pe.transpose(psum[:, 7, 16 * m:16 * m + 16], state[:, m * P:(m + 1) * P], ident[0:16, 0:16])
                last.then_inc(st_ps, 1)
                for t in range(NT):
                    r = rows(t)
                    pe.wait_ge(h_ok, t + 1)
                    for half in range(2):
                        i = 2 * t + half
                        if i >= 4:
                            pe.wait_ge((hT_a, hT_v)[half], t - 1)
                        for k in range(4):
                            kk = 4 * half + k
                            last = pe.transpose(psum[:, 3 + i % 4, k * P:k * P + r], xh[0:r, t, kk * P:(kk + 1) * P],
                                                ident[0:r, 0:r])
                        last.then_inc(hT_ps, 1)
                pe.wait_ge(mod_ok, NADA)
                pe.wait_ge(hT_a, NT)
                pe.wait_ge(hT_v, NT)
                for j in range(3):
                    n = NADA + j
                    pe.wait_ge(w_in[n % 4], 16 * (n // 4 + 1))
                    for m in range(WC):
                        i = j * WC + m
                        if i >= 2:
                            if i - 2 < WC:
                                pe.wait_ge(hc_ok, i - 1)
                            else:
                                pe.wait_ge(gcb_ok, i - 1 - WC)
                        for k in range(KC):
                            pe.matmul(psum[:, 3 + i % 2, :], ring[:, n % 4, k, m * P:(m + 1) * P], hT[:, k, 0:SEQ],
                                      start=(k == 0), stop=(k == KC - 1))
                            last = pe.matmul(psum[:, 5 + i % 2, 0:NS], ring[:, n % 4, k, m * P:(m + 1) * P], hT[:, k, SEQ:],
                                             start=(k == 0), stop=(k == KC - 1))
                        last.then_inc(cmm, 1)
                for j in range(3):
                    n = NADA + 3 + j
                    pe.wait_ge(w_in[n % 4], 16 * (n // 4 + 1))
                    if j == 1:
                        pe.wait_ge(tail_ok, 1)
                        pe.wait_ge(gcb_ok, 2 * WC)
                        for m in range(WC):
                            last = pe.transpose(psum[0:18, 3, m * P:(m + 1) * P], tail[:, m, :], ident)
                        last.then_inc(tail_ps, 1)
                        pe.wait_ge(sq_ok, 2 * WC)
                        for t in range(NT):
                            for m in range(WC):
                                last = pe.matmul(psum[0:rows(t), 7, 64 + t:65 + t], hcT[:, m, t * P:t * P + rows(t)],
                                                 cst[:, C_ONE:C_ONE + 1], start=(m == 0), stop=(m == WC - 1))
                        last.then_inc(ssq_ps, 1)
                    for t in range(NT):
                        i, r = j * NT + t, rows(t)
                        if i >= 3:
                            if i - 3 < 2 * NT:
                                pe.wait_ge(qk_ok, i - 2)
                            else:
                                pe.wait_ge(v_ok, i - 2 - 2 * NT)
                        for k in range(KC):
                            last = pe.matmul(psum[0:r, i % 3, :], hT[:, k, t * P:t * P + r], ring[:, n % 4, k, :],
                                             start=(k == 0), stop=(k == KC - 1))
                        last.then_inc(proj, 1)

        st.close()

    wout_conv_in, wout_attn_in, shared_in = sem("wout_conv_in"), sem("wout_attn_in"), sem("shared_in")

    def gate_up_of(w):
        return w[:, 0:KC * 2 * FE].rearrange("p (a k n) -> p k a n", a=2, k=KC)

    def down_of(w):
        return w[:, KC * 2 * FE:].rearrange("p (k n) -> p k n", k=2)

    def load_gate_up(eng, dst, gate, up_, signal):
        for a, src in enumerate((gate, up_)):
            eng.dma_start(dst[:, a * KC * FE:(a + 1) * KC * FE],
                          src.rearrange("(p k) n -> p (k n)", p=P)).then_inc(signal, 16)

    def load_down(eng, dst, down, signal):
        eng.dma_start(dst[:, KC * 2 * FE:], down.rearrange("(p k) n -> p (k n)", p=P)).then_inc(signal, 16)

    def stage_2():
        st = ExitStack()

        def tmp(name, shape, dt=F32):
            return st.enter_context(nc.sbuf_tensor("sb_" + name, shape, dt))

        k_sb, v_sb = keeps["k"], keeps["v"]
        q_sb = attn
        masks = tmp("masks", [P, A_END])
        qT = tmp("qT", [P, WC, SEQ])
        kT = tmp("kT", [P, WC, SEQ])
        kTn = tmp("kTn", [P, WC, NS])
        qz = tmp("qz", [P, WC, DEC_B, HEADS * DEC_T])
        probs = tmp("probs", [P, 3, SEQ])
        pT = tmp("pT", [P, 2, SEQ])
        nmax = tmp("nmax", [P, NPT * HEADS])
        den = tmp("den", [P, NPT * HEADS])
        rden = tmp("rden", [P, NPT * HEADS])
        KTs = tmp("KTs", [P, 2, WIN + 4 * SPARSE])
        sp_ = tmp("s_probs", [P, SK])
        spT = tmp("s_pT", [P, 9, P])
        snm = tmp("s_nm", [P, 2, 4])
        sden = tmp("s_den", [P, 2, 2])
        om = probs[:, 0:2, :]
        ring = stream[:, :].rearrange("p (s t n) -> p s t n", s=6, t=8)
        items = [(kind, b) for g in range(2) for kind in "kv" for b in range(4 * g, 4 * g + 4)]
        wout = stream[:, 4 * 4096:6 * 4096].rearrange("p (k n) -> p k n", k=KC)

        masks_in = sem("s2_masks_in")
        row_in = [sem(f"s2_rows{i}") for i in range(6)]
        zeroed, turn_ps, turn_ok, new_ps, new_ok = (sem(f"s2_{n}") for n in
                                                    ("zeroed", "turn_ps", "turn_ok", "new_ps", "new_ok"))
        sc, sc_read, exp_ok, p_ok = (sem(f"s2_{n}") for n in ("sc", "sc_read", "exp_ok", "p_ok"))
        pT_ps, pT_ok, pv, pv_read = (sem(f"s2_{n}") for n in ("pT_ps", "pT_ok", "pv", "pv_read"))
        kt_ps, kt_a, kt_v, ssc = (sem(f"s2_{n}") for n in ("kt_ps", "kt_a", "kt_v", "ssc"))
        ssc_read, sexp, sp_ok = (sem(f"s2_{n}") for n in ("ssc_read", "sexp", "sp_ok"))
        spt_ps, spt_a, spt_v, spv, om_ok, fold = (sem(f"s2_{n}") for n in
                                                  ("spt_ps", "spt_a", "spt_v", "spv", "om_ok", "fold"))
        v_step = sem("s2_v_step")

        def arrived(eng, kind, b):
            j = items.index((kind, b))
            eng.wait_ge(row_in[j % 6], 32 * (j // 6 + 1))
            return ring[:, j % 6]

        def load_cache(eng, dst, cache, b, signal):
            c = cache[0, b].rearrange("r h d -> r (h d)")
            eng.dma_start(dst[:, 0:4, :], c[WIN0:, :].rearrange("(p t) n -> p t n", t=4)).then_inc(signal, 16)
            eng.dma_start(dst[0:SPARSE, 4:8, :],
                          c[0:WIN0, :].rearrange("(j s) n -> j s n", s=16)[:, 0:4, :]).then_inc(signal, 16)

        with nc.Block() as block:
            @block.sync
            def _(sp):
                sp.dma_start(masks[:, :], io["masks"]).then_inc(masks_in, 16)

                for j, (kind, b) in enumerate(items):
                    if j == 5:
                        sp.wait_ge(stored, 6 * 16)
                    if j >= 6:
                        was, n = items[j - 6]
                        if was == "k":
                            sp.wait_ge(kt_ps, 4 * (n + 1))
                        else:
                            sp.wait_ge(spv, n + 1)
                    load_cache(sp, ring[:, j % 6], io["cache_" + kind], b, row_in[j % 6])
                sp.wait_ge(kt_ps, 4 * DEC_B)
                w_out = io["w_out"][0].rearrange("(k p) n -> p k n", p=P)
                sp.dma_start(wout[:, WC:, :], w_out[:, WC:, :]).then_inc(wout_conv_in, 16)
                sp.dma_start(wout[:, 0:WC, :], w_out[:, 0:WC, :]).then_inc(wout_attn_in, 16)

            @block.gpsimd
            def _(pool):
                pool.memset(qz[:, :, :, :], 0.0).then_inc(zeroed, 1)
                pool.memset(spT[:, 8, :], 0.0).then_inc(zeroed, 1)

            @block.scalar
            def _(act):
                for i in range(2 * WC):
                    act.wait_ge(turn_ps, i + 1)
                    act.copy((qT, kT)[i % 2][:, i // 2, :], psum[:, 4 + i % 2, :]).then_inc(turn_ok, 1)
                N = NPT * HEADS
                for n in range(N + 2):
                    if n < N:
                        act.wait_ge(sc_read, n + 1)
                        w = (n // HEADS + 1) * P
                        act.activation(probs[:, n % 3, 0:w], probs[:, n % 3, 0:w], ACT.Exp,
                                       bias=nmax[:, n:n + 1], scale=-1.0).then_inc(exp_ok, 1)
                    m = n - 2
                    if m >= 0:
                        act.wait_ge(pT_ps, m + 1)
                        if m >= 2:
                            act.wait_ge(pv, m - 1)
                        w = (m // HEADS + 1) * P
                        act.copy(pT[:, m % 2, 0:w], psum[:, 4 + m % 2, 0:w]).then_inc(pT_ok, 1)
                for g in range(2):
                    for e in range(16 * g, 16 * g + 16):
                        act.wait_ge(kt_ps, e + 1)
                        if e >= 2:
                            act.wait_ge(ssc, e - 1)
                        act.copy(KTs[:, e % 2, 0:WIN], psum[:, e % 2, :]).then_inc(kt_a, 1)
                    act.wait_ge(ssc_read, g + 1)
                    act.activation(sp_[:, :], sp_[:, :], ACT.Exp, bias=snm[:, g, 2:3], scale=-1.0).then_inc(sexp, 1)
                    act.wait_ge(spt_ps, g + 1)
                    act.copy(spT[:, 0:4, :], psum[:, 0, :].rearrange("p (t n) -> p t n", t=4)).then_inc(spt_a, 1)

            @block.vector
            def _(v):
                n_step = [0]

                def step(ins):
                    n_step[0] += 1
                    ins.then_inc(v_step, 1)

                def settle():
                    v.wait_ge(v_step, n_step[0])

                v.wait_ge(zeroed, 1)
                v.wait_ge(new_ps, 2)
                for h in range(HEADS):
                    lo = (h % 2) * HD
                    step(v.tensor_copy(qz[lo:lo + HD, h // 2, :, h * DEC_T:(h + 1) * DEC_T],
                                       psum[lo:lo + HD, 6, (h // 2) * NS:(h // 2 + 1) * NS].rearrange("p (b t) -> p b t", b=DEC_B)))
                step(v.tensor_copy(kTn[:, :, :], psum[:, 7, 0:WC * NS].rearrange("p (c n) -> p c n", c=WC)))
                settle()
                v.sem_inc(new_ok, 1)
                v.wait_ge(masks_in, 16)
                N = NPT * HEADS

                def finish_tile(i):
                    v.wait_ge(pv, HEADS * (i + 1))
                    step(v.reciprocal(rden[:, i * HEADS:(i + 1) * HEADS], den[:, i * HEADS:(i + 1) * HEADS]))
                    settle()
                    v.tensor_tensor(attn[:, i, :].rearrange("p (h d) -> p h d", h=HEADS),
                                    psum[:, 6 + i % 2, :].rearrange("p (h d) -> p h d", h=HEADS),
                                    rden[:, i * HEADS:(i + 1) * HEADS].unsqueeze(2).broadcast_to([P, HEADS, HD]),
                                    ALU.mult).then_inc(pv_read, 1)

                for n in range(N + 1):
                    if n < N:
                        i = n // HEADS
                        w, a = (i + 1) * P, (NPT - 1 - i) * P
                        v.wait_ge(sc, n + 1)
                        if n >= 3:
                            v.wait_ge(pT_ps, n - 2)
                        v.tensor_tensor_reduce(probs[:, n % 3, 0:w], psum[:, n % 3, 0:w], masks[:, A_PN + a:A_PN + 512],
                                               -HD ** -0.5, 3e38, ALU.add, ALU.min, nmax[:, n:n + 1]).then_inc(sc_read, 1)
                    if n >= 1:
                        m = n - 1
                        i = m // HEADS
                        w, a = (i + 1) * P, (NPT - 1 - i) * P
                        v.wait_ge(exp_ok, m + 1)
                        v.tensor_tensor_reduce(probs[:, m % 3, 0:w], probs[:, m % 3, 0:w], masks[:, A_PM + a:A_PM + 512],
                                               1.0, 0.0, ALU.mult, ALU.add, den[:, m:m + 1]).then_inc(p_ok, 1)
                    if n % HEADS == 5 and n > HEADS:
                        v.wait_ge(p_ok, n)
                        finish_tile(n // HEADS - 1)
                v.wait_ge(p_ok, N)
                finish_tile(NPT - 1)
                v.wait_ge(pv_read, NPT)
                for t in range(NPT):
                    step(v.tensor_tensor_reduce(probs[:, 2, :], attn[:, t, :], attn[:, t, :], 1.0, 0.0,
                                                ALU.mult, ALU.add, attn_sq[:, t:t + 1]))
                    settle()
                for g in range(2):
                    for e in range(16 * g, 16 * g + 16):
                        v.wait_ge(kt_ps, e + 1)
                        if e >= 2:
                            v.wait_ge(ssc, e - 1)
                        v.tensor_copy(KTs[:, e % 2, WIN:], psum[:, 2 + e % 2, 0:4 * SPARSE]).then_inc(kt_v, 1)
                    v.wait_ge(ssc, 16 * (g + 1))
                    if g:
                        v.wait_ge(spt_ps, g)
                    for j, (a, b) in enumerate(((0, WIN), (WIN, SK))):
                        step(v.tensor_tensor_reduce(sp_[:, a:b], psum[:, 4 + j, 0:b - a],
                                                    masks[:, A_SN + g * SK + a:A_SN + g * SK + b],
                                                    -HD ** -0.5, 3e38, ALU.add, ALU.min, snm[:, g, j:j + 1]))
                    settle()
                    v.tensor_tensor(snm[:, g, 2:3], snm[:, g, 0:1], snm[:, g, 1:2], ALU.min).then_inc(ssc_read, 1)
                    v.wait_ge(sexp, g + 1)
                    v.tensor_tensor_reduce(sp_[:, :], sp_[:, :], masks[:, A_SM + g * SK:A_SM + (g + 1) * SK],
                                           1.0, 0.0, ALU.mult, ALU.add, sden[:, g, 0:1]).then_inc(sp_ok, 1)
                    v.wait_ge(zeroed, 2)
                    v.wait_ge(spt_ps, g + 1)
                    v.tensor_copy(spT[0:SPARSE, 4:8, :], psum[0:SPARSE, 1, :].rearrange("p (t n) -> p t n",
                            t=4)).then_inc(spt_v, 1)
                    v.tensor_copy(spT[0:NS, 8, :], psum[0:NS, 2, 0:P]).then_inc(spt_v, 1)
                    v.wait_ge(sp_ok, g + 1)
                    step(v.reciprocal(sden[:, g, 1:2], sden[:, g, 0:1]))
                    settle()
                    v.wait_ge(spv, 4 * (g + 1))
                    v.scalar_tensor_tensor(om[:, g, :], psum[:, 6 + g, :], sden[:, g, 1:2], masks[:, A_BD:A_BD + W],
                                           ALU.mult, ALU.mult).then_inc(om_ok, 1)
                v.wait_ge(fold, 1)
                v.tensor_copy(attn[0:NS, NPT, :], psum[0:NS, 0, :])

            @block.tensor
            def _(pe):
                for j, src in enumerate((q_sb, k_sb)):
                    for c in range(WC):
                        last = pe.transpose(psum[:, 6 + j, c * NS:(c + 1) * NS], src[0:NS, NPT, c * P:(c + 1) * P],
                                            ident[0:NS, 0:NS])
                    last.then_inc(new_ps, 1)
                for i in range(2 * WC):
                    if i >= 2:
                        pe.wait_ge(turn_ok, i - 1)
                    for t in range(NPT):
                        last = pe.transpose(psum[:, 4 + i % 2, t * P:(t + 1) * P],
                                            (q_sb, k_sb)[i % 2][:, t, (i // 2) * P:(i // 2 + 1) * P], ident)
                    last.then_inc(turn_ps, 1)
                pe.wait_ge(turn_ok, 2 * WC)
                N = NPT * HEADS
                for n in range(N + 3):
                    if n < N:
                        i, h = n // HEADS, n % HEADS
                        lo = (h % 2) * HD
                        if n >= 3:
                            pe.wait_ge(sc_read, n - 2)
                        pe.matmul(psum[:, n % 3, 0:(i + 1) * P], qT[lo:lo + HD, h // 2, i * P:(i + 1) * P],
                                  kT[lo:lo + HD, h // 2, 0:(i + 1) * P], start=True, stop=True).then_inc(sc, 1)
                    m = n - 2
                    if 0 <= m < N:
                        pe.wait_ge(p_ok, m + 1)
                        if m >= 2:
                            pe.wait_ge(pT_ok, m - 1)
                        for t in range(m // HEADS + 1):
                            last = pe.transpose(psum[:, 4 + m % 2, t * P:(t + 1) * P], probs[:, m % 3, t * P:(t + 1) * P], ident)
                        last.then_inc(pT_ps, 1)
                    m = n - 3
                    if m >= 0:
                        i, h = m // HEADS, m % HEADS
                        pe.wait_ge(pT_ok, m + 1)
                        if m == 0:
                            pe.wait_ge(new_ok, 1)
                        if h == 0 and i >= 2:
                            pe.wait_ge(pv_read, i - 1)
                        for t in range(i + 1):
                            last = pe.matmul(psum[:, 6 + i % 2, h * HD:(h + 1) * HD], pT[:, m % 2, t * P:(t + 1) * P],
                                             v_sb[:, t, h * HD:(h + 1) * HD], start=(t == 0), stop=(t == i))
                        last.then_inc(pv, 1)
                pe.wait_ge(pv_read, NPT)

                def turn_keys(e):
                    b, c = e // 4, e % 4
                    keys = arrived(pe, "k", b)
                    if e >= 2:
                        pe.wait_ge(kt_a, e - 1)
                        pe.wait_ge(kt_v, e - 1)
                    for t in range(4):
                        pe.transpose(psum[:, e % 2, t * P:(t + 1) * P], keys[:, t, c * P:(c + 1) * P], ident)
                    for t in range(4):
                        last = pe.transpose(psum[:, 2 + e % 2, t * SPARSE:(t + 1) * SPARSE],
                                            keys[0:SPARSE, 4 + t, c * P:(c + 1) * P], ident[0:SPARSE, 0:SPARSE])
                    last.then_inc(kt_ps, 1)

                for g in range(2):
                    if g:
                        pe.wait_ge(ssc_read, g)
                        pe.wait_ge(spt_v, 2 * g)
                        pe.wait_ge(spt_a, g)
                    turn_keys(16 * g)
                    for e in range(16 * g, 16 * g + 16):
                        b, c = e // 4, e % 4
                        lo = 32 * (b % 4)
                        if e + 1 < 16 * g + 16:
                            turn_keys(e + 1)
                        pe.wait_ge(kt_a, e + 1)
                        pe.wait_ge(kt_v, e + 1)
                        w = qz[:, c, b, :]
                        pe.matmul(psum[lo:lo + 32, 4, :], w, KTs[:, e % 2, 0:WIN], start=(c == 0), stop=(c == 3))
                        pe.matmul(psum[lo:lo + 32, 5, 0:4 * SPARSE], w, KTs[:, e % 2, WIN:], start=(c == 0), stop=False,
                                  skip_group_check=True)
                        last = pe.matmul(psum[lo:lo + 32, 5, 4 * SPARSE:4 * SPARSE + NS], w, kTn[:, c, :],
                                         start=False, stop=(c == 3), skip_group_check=True)
                        last.then_inc(ssc, 1)
                    pe.wait_ge(sp_ok, g + 1)
                    for t in range(4):
                        pe.transpose(psum[:, 0, t * P:(t + 1) * P], sp_[:, t * P:(t + 1) * P], ident)
                    for t in range(4):
                        pe.transpose(psum[0:SPARSE, 1, t * P:(t + 1) * P], sp_[:, WIN + t * SPARSE:WIN + (t + 1) * SPARSE], ident)
                    pe.transpose(psum[0:NS, 2, 0:P], sp_[:, WIN + 4 * SPARSE:], ident).then_inc(spt_ps, 1)
                    pe.wait_ge(spt_a, g + 1)
                    pe.wait_ge(spt_v, 2 * (g + 1))
                    for b in range(4 * g, 4 * g + 4):
                        lo = 32 * (b % 4)
                        values = arrived(pe, "v", b)
                        for t in range(9):
                            k = P if t < 4 or t == 8 else SPARSE
                            rhs = values[0:k, t, :] if t < 8 else v_sb[:, NPT, :]
                            last = pe.matmul(psum[lo:lo + 32, 6 + g, :], spT[0:k, t, lo:lo + 32], rhs,
                                             start=(t == 0), stop=(t == 8))
                        last.then_inc(spv, 1)
                pe.wait_ge(om_ok, 2)
                for g in range(2):
                    last = pe.matmul(psum[0:NS, 0, :], masks[:, A_SEL + g * NS:A_SEL + (g + 1) * NS], om[:, g, :],
                                     start=(g == 0), stop=(g == 1))
                last.then_inc(fold, 1)
        st.close()

    def stage_3():
        st = ExitStack()

        def tmp(name, shape, dt=F32):
            return st.enter_context(nc.sbuf_tensor("sb_" + name, shape, dt))

        x2 = tmp("x2", [P, NT, D])
        bc = tmp("bc", [P, 3, 2, D])
        flat = bc[:, :, :, :].rearrange("p a b n -> p (a b n)")
        ysh = flat[:, 0:NT * D].rearrange("p (t n) -> p t n", t=NT)
        h2T = tmp("h2T", [P, KC, NTOK])
        work = tmp("work", [P, 3, D])
        xg = work
        aT = tmp("aT", [P, 2, WC, P])
        wr = tmp("wr", [P, KC, NE])
        hbuf = aT[:, :, :, :].rearrange("p s c n -> p (s c n)")[:, 0:3 * FE].rearrange("p (a n) -> p a n", a=3)
        sil, hid, hidT = hbuf[:, 0, :], hbuf[:, 1, :], hbuf[:, 2, :].rearrange("p (k n) -> p k n", k=2)
        oh = tmp("oh", [P, 3, NT, P], BF16)
        pick = tmp("pick", [P, 3, NT, 9], BF16)
        table = tmp("table", [P, NT, NE, 9], BF16)
        blk = tmp("blk", [P, 3, NT])
        got = tmp("got", [P, 3, 3])
        token = tmp("token", [P, 3, 1], U32)
        row = tmp("row", [P, 3, 1], U32)
        now_gate = tmp("now_gate", [P, 3])
        bias = tmp("bias", [P, NE])
        ss = tmp("ss3", [P, 4, NT])
        merged = tmp("merged", [P, 80])
        wout = stream[:, 4 * 4096:6 * 4096].rearrange("p (k n) -> p k n", k=KC)
        WEXP = 3 * KC * FE
        wslot = [stream[:, WEXP * n:WEXP * (n + 1)] for n in range(3)]
        xT = stream[:, 3 * WEXP:3 * WEXP + 3 * D].rearrange("p (s k n) -> p s k n", s=3, k=KC)
        out = stream[:, 3 * WEXP + 3 * D:3 * WEXP + 6 * D].rearrange("p (s n) -> p s n", s=3)
        af = attn[:, :, :].rearrange("p t n -> p (t n)")
        scores, sel, selm, mask, gate, ra, rb, gpos = (
            af[:, 320 * n:320 * (n + 1)].rearrange("p (t e) -> p t e", t=NT) for n in range(8))
        cf = convg[:, :, :].rearrange("p c n -> p (c n)")
        run = [cf[:, 480 * n:480 * (n + 1)].rearrange("p (t e) -> p t e", t=NT) for n in range(2)]
        erun = [cf[:, 960 + 96 * n:960 + 96 * (n + 1)] for n in range(2)]
        nblk, cnt, first = (cf[:, 1152 + 64 * n:1152 + 64 * (n + 1)] for n in range(3))
        grp = cf[:, 1344:1384].rearrange("p (t g) -> p t g", t=NT)
        gok = cf[:, 1384:1424].rearrange("p (t g) -> p t g", t=NT)
        gneg = cf[:, 1424:1464].rearrange("p (t g) -> p t g", t=NT)
        top = cf[:, 1464:1504].rearrange("p (t g) -> p t g", t=NT)
        gsum, grec = cf[:, 1504:1509], cf[:, 1509:1514]
        blkf, tripf, lane = cf[:, 1514:1515], cf[:, 1515:1516], cf[:, 1516:1519]
        maskb = cf[:, 1520:1520 + 160].bitcast(BF16).rearrange("p (t e) -> p t e", t=NT)
        trib = cf[:, 1680:1680 + 64].bitcast(BF16)
        oneb = cf[:, 1744:1744 + 64].bitcast(BF16)
        tab = cf[0:1, 1808:1808 + 2 * P + 1].bitcast(I32)
        experts, fresh, n_trips = tab[:, 0:P], tab[:, P:2 * P], tab[:, 2 * P:2 * P + 1]
        expert_row = af[0:1, 0:P]

        DN0 = 2 * NT
        names = ("x_in bc_in small_in ams rs an_ok aT_ps aT_ok prod_c prod_a tc_ok x2_ok ms h2_ok h2_ps h2_sb logit "
                 "ex_ok zeroed mask_ok cnt_ps blk_ok tab_ps tab_ok table_ok consts_ok "
                 "ssil shid sht "
                 "list_mm list_ok oh_ok token_ok now_ok xt_ps xt_a xt_v gu sil_ok hid_ok ht_ps ht_ok dn out_lo out_hi pick_ok go").split()
        s = {n: sem("s3_" + n) for n in names}
        h_out = [sem(f"s3_h_out{i}") for i in range(2)]
        w_in = [sem(f"s3_w{i}") for i in range(3)]
        gath = [sem(f"s3_gath{i}") for i in range(3)]
        scat = [sem(f"s3_scat{i}") for i in range(3)]
        v_step = sem("s3_v_step")

        room = h2T[:, :, :].rearrange("p k n -> p (k n)")
        gate2 = room[:, 0:2 * D].rearrange("p (a n) -> p a n", a=2)
        gfin = room[:, 2 * D:3 * D]

        def trips(eng):
            eng.wait_ge(s["tab_ok"], 1)
            return eng.value_load(n_trips, min_val=0, max_val=TRIPS)

        def expert_of(eng, b):
            return eng.value_load(experts[:, bass.ds(b, 1)], min_val=0, max_val=NE - 1)

        def who(v, b, u):
            e = expert_of(v, b)
            v.tensor_tensor(blk[:, u, :].unsqueeze(2), gpos[:, :, bass.ds(e, 1)],
                            cst[:, bass.ds(b + C_ROUND, 1)].unsqueeze(1).broadcast_to([P, NT, 1]),
                                    ALU.subtract).then_inc(s["blk_ok"], 1)
            v.tensor_copy(pick[:, u, :, :].unsqueeze(2), table[:, :, bass.ds(e, 1), :]).then_inc(s["pick_ok"], 1)
            v.wait_ge(s["blk_ok"], b + 1)
            for t in range(NT):
                last = v.tensor_scalar(oh[:, u, t, :], cst[:, C_IOTA:C_IOTA + P], lane[:, u:u + 1], blk[:, u, t:t + 1],
                                       ALU.add, ALU.is_equal)
            last.then_inc(s["oh_ok"], 1)

        def fill_list(pe, b, u, first=False):
            pe.wait_ge(s["oh_ok"], b + 1)
            pe.wait_ge(s["pick_ok"], b + 1)
            if not first:
                pe.wait_ge(s["list_ok"], b)
            for t in range(NT):
                last = pe.matmul(psum[:, 6, 0:9], oh[:, u, t, :], pick[:, u, t, :], start=(t == 0), stop=(t == NT - 1))
            last.then_inc(s["list_mm"], 1)

        def read_list(v, b, u):
            v.wait_ge(s["list_mm"], b + 1)
            v.tensor_reduce(got[:, u, :], psum[:, 6, 0:9].rearrange("p (a c) -> p a c", a=3), AX.X,
                    ALU.add).then_inc(s["list_ok"], 1)
            v.wait_ge(s["list_ok"], b + 1)
            v.tensor_scalar(token[:, u, :], got[:, u, 0:1], float(OUTSIDE), None, ALU.add).then_inc(s["token_ok"], 1)

        def gather(pool, b, u, last_row):
            pool.wait_ge(s["token_ok"], b + 1)
            pool.sem_inc(s["go"], 1)
            pool.indirect_dma_start(xg[:, u, :], None, h_rows, bass.IndirectOffsetOnAxis(ap=token[:, u, :], axis=0),
                                    bounds_check=last_row, oob_is_err=False).then_inc(gath[u], 16)

        def turn_rows(pe, u):
            for k in range(KC):
                last = pe.transpose(psum[:, 1 + k // 4, (k % 4) * P:(k % 4 + 1) * P], xg[:, u, k::KC], ident)
                if k % 4 == 3:
                    last.then_inc(s["xt_ps"], 1)

        def take_rows_a(act, b, u):
            act.wait_ge(s["xt_ps"], 2 * b + 1)
            act.copy(xT[:, u, 0:4, :], psum[:, 1, :].rearrange("p (k n) -> p k n", k=4)).then_inc(s["xt_a"], 1)

        def take_rows_v(v, b, u):
            v.wait_ge(s["xt_ps"], 2 * b + 2)
            v.tensor_copy(xT[:, u, 4:8, :], psum[:, 2, :].rearrange("p (k n) -> p k n", k=4)).then_inc(s["xt_v"], 1)

        def gate_up(pe, bank, r, lhs, w, done):
            gu = gate_up_of(w)
            for k in range(KC):
                last = pe.matmul(psum[0:r, bank, :].rearrange("p (a n) -> p a n", a=2), lhs(k), gu[:, k, :, :],
                                 start=(k == 0), stop=(k == KC - 1))
            last.then_inc(done, 1)

        def turn_hidden(pe, r, done):
            for k in range(2):
                last = pe.transpose(psum[:, 3, k * P:k * P + r], hid[0:r, k::2], ident[0:r, 0:r])
            last.then_inc(done, 1)

        def out_read(pe, tiles):
            return lambda n: pe.wait_ge(s[("out_lo", "out_hi")[n]], tiles)

        def down(pe, r, w, done, waits):
            dn = down_of(w)
            for n in range(2):
                if waits:
                    waits(n)
                for k in range(2):
                    last = pe.matmul(psum[0:r, 4 + n, :], hidT[:, k, 0:r], dn[:, k, n * 512:(n + 1) * 512],
                                     start=(k == 0), stop=(k == 1))
                last.then_inc(done, 1)

        with nc.Block() as block:
            @block.sync
            def _(sp):
                sp.dma_start(x2[:, 0:NPT, :], io["x_prompt"][0].rearrange("(t p) n -> p t n", p=P)).then_inc(s["x_in"], 16)
                sp.dma_start(x2[0:NS, NPT, :], io["x_sample"].rearrange("b t n -> (b t) n")).then_inc(s["x_in"], 16)
                for n, j in enumerate((2, 3, 4)):
                    sp.dma_start(bc[:, n, 0, :], bc_row(mod_rows[0:1, j * D:(j + 1) * D], P)).then_inc(s["bc_in"], 16)
                    sp.dma_start(bc[0:NS, n, 1, :], mod_sample(j)).then_inc(s["bc_in"], 16)
                sp.dma_start(wr[:, :, :], io["w_router"][0].rearrange("(p k) n -> p k n", p=P)).then_inc(s["small_in"], 16)
                sp.dma_start(bias[:, :], bc_row(io["router_bias"], P)).then_inc(s["small_in"], 16)
                load_gate_up(sp, wslot[0], io["w_sh_gate"][0], io["w_sh_up"][0], shared_in)
                load_down(sp, wslot[0], io["w_sh_down"][0], shared_in)
                for t in range(NT):
                    sp.wait_ge(s["h2_ok"], t + 1)
                    sp.dma_start(h_rows[t * P:t * P + rows(t), :], work[0:rows(t), 1 + t % 2, :]).then_inc(h_out[t % 2], 16)

                def weights_of(name, e):
                    return io[name][0, bass.ds(e, 1)].rearrange("a d f -> (a d) f")

                def is_new(b):
                    return sp.value_load(fresh[:, bass.ds(b, 1)], min_val=0, max_val=1)

                def gate_up_weights(b, u):
                    used = b - 2 + NT
                    e, new = expert_of(sp, b), is_new(b)
                    with sp.If(new > 0):
                        sp.wait_ge(s["gu"], used)
                        load_gate_up(sp, wslot[(u + 1) % 3], weights_of("w_exp_gate", e), weights_of("w_exp_up", e), w_in[u])
                    with sp.If(new < 1):
                        sp.wait_ge(s["gu"], used)
                        sp.sem_inc(w_in[u], 32)

                def down_weights(b, u):
                    used = 2 * (b - 2) + DN0
                    e, new = expert_of(sp, b), is_new(b)
                    with sp.If(new > 0):
                        sp.wait_ge(s["dn"], used)
                        load_down(sp, wslot[(u + 1) % 3], weights_of("w_exp_down", e), w_in[u])
                    with sp.If(new < 1):
                        sp.wait_ge(s["dn"], used)
                        sp.sem_inc(w_in[u], 16)

                nb = trips(sp)
                gate_up_weights(0, 0)
                with sp.Fori(0, TRIPS) as i:
                    with sp.If(nb > i):
                        for u in range(3):
                            b = 3 * i + u
                            if u < 2:
                                gate_up_weights(b + 1, u + 1)
                            else:
                                with sp.If(nb > i + 1):
                                    gate_up_weights(b + 1, 0)
                            sp.wait_ge(s["go"], 3)
                            down_weights(b, u)

            @block.gpsimd
            def _(pool):
                minus_half = cst[:, C_POW:C_POW + 1]

                def inverse_root(dst, src):
                    n = dst.shape[1]
                    pool.tensor_tensor(dst, src, minus_half[0:dst.shape[0]].broadcast_to([dst.shape[0], n]),
                            ALU.pow).then_inc(s["rs"], 1)

                pool.wait_ge(s["ams"], 1)
                inverse_root(ss[:, 1, 0:NPT], ss[:, 0, 0:NPT])
                inverse_root(ss[0:NS, 1, NPT:], ss[0:NS, 0, NPT:])
                pool.memset(table[:, :, :, :].rearrange("p t e c -> p (t e c)"), 0.0).then_inc(s["zeroed"], 1)
                pool.wait_ge(s["zeroed"], 1)
                for t in range(NT):
                    pool.tensor_copy(table[:, t, :, 0:5],
                                     cst[:, C_LP + 5 * t:C_LP + 5 * t + 5].unsqueeze(1).broadcast_to([P, NE,
                                             5])).then_inc(s["consts_ok"], 1)
                for t in range(NT):
                    pool.wait_ge(s["ms"], t + 1)
                    inverse_root(ss[0:rows(t), 3, t:t + 1], ss[0:rows(t), 2, t:t + 1])
                pool.wait_ge(s["h2_ps"], 2 * NT)
                pool.wait_ge(s["prod_a"], NT)
                pool.memset(cf[:, 0:1152], 0.0).then_inc(s["zeroed"], 1)
                pool.memset(scores, 1.0).then_inc(s["zeroed"], 1)
                for n in range(2):
                    pool.wait_ge(h_out[n], 16 * (3 - n))
                pool.memset(xg[:, :, :], 0.0).then_inc(s["zeroed"], 1)
                last_row, last_expert_row = pool.to_reg(NTOK - 1), pool.to_reg(NTOK * TOPK - 1)
                pool.wait_ge(s["zeroed"], 4)
                gather(pool, 0, 0, last_row)
                gather(pool, 1, 1, last_row)
                gather(pool, 2, 2, last_row)
                nb = trips(pool)
                with pool.Fori(0, TRIPS) as i:
                    with pool.If(nb > i):
                        for u in range(3):
                            b = 3 * i + u
                            pool.wait_ge(s["xt_ps"], 2 * b + 2)
                            gather(pool, b + 3, u, last_row)
                            pool.wait_ge(s["now_ok"], 2 * b + 2)
                            pool.wait_ge(s["out_lo"], b + 1 + NT)
                            pool.wait_ge(s["out_hi"], b + 1 + NT)
                            pool.sem_inc(s["go"], 1)
                            pool.indirect_dma_start(expert_rows, bass.IndirectOffsetOnAxis(ap=row[:, u, :], axis=0),
                                                    out[:, u, :], None, bounds_check=last_expert_row,
                                                    oob_is_err=False).then_inc(scat[u], 16)
                for u in range(3):
                    pool.wait_ge(scat[u], 16 * nb)
                    pool.wait_ge(gath[u], 16 * nb + 16)
                pool.wait_ge(s["go"], 6 * nb + 3)

            @block.scalar
            def _(act):
                act.wait_ge(s["rs"], 2)
                def scale_attn(t):
                    r = rows(t)
                    act.activation(attn[0:r, t, :], attn[0:r, t, :], ACT.Copy, scale=ss[0:r, 1,
                            t:t + 1]).then_inc(s["an_ok"], 1)

                def take_attn(t):
                    act.wait_ge(s["aT_ps"], t + 1)
                    for c in range(WC):
                        last = act.activation(aT[:, t % 2, c, 0:rows(t)], psum[:, 0, c * P:c * P + rows(t)], ACT.Copy,
                                              scale=gains[:, 0, c:c + 1])
                    last.then_inc(s["aT_ok"], 1)

                def take_norm(t):
                    for half in range(2):
                        act.wait_ge(s["h2_ps"], 2 * t + half + 1)
                        act.copy(h2T[:, 4 * half:4 * half + 4, t * P:t * P + rows(t)],
                                 psum[:, 6 + half, :].rearrange("p (k n) -> p k n", k=4)[:, :,
                                         0:rows(t)]).then_inc(s["h2_sb"], 1)

                def take_conv(t):
                    r = rows(t)
                    act.wait_ge(s["prod_c"], t + 1)
                    if t:
                        act.wait_ge(s["x2_ok"], t)
                    act.activation(work[0:r, 0, :], psum[0:r, 4:6, :].rearrange("p a n -> p (a n)"), ACT.Copy,
                                   scale=conv_r[0:r, t:t + 1]).then_inc(s["tc_ok"], 1)

                scale_attn(0)
                for t in range(NT):
                    if t + 1 < NT:
                        scale_attn(t + 1)
                    take_attn(t)
                    take_conv(t)
                    if t >= 2:
                        take_norm(t - 2)
                take_norm(NT - 2)
                take_norm(NT - 1)
                act.wait_ge(s["logit"], NT)
                act.wait_ge(s["zeroed"], 3)
                act.activation(scores[:, 0:NPT, :], psum[:, 1, 0:NPT * NE].rearrange("p (t e) -> p t e", t=NPT), ACT.Exp, scale=-1.0)
                act.activation(scores[0:NS, NPT, :], psum[0:NS, 1, NPT * NE:NT * NE], ACT.Exp,
                        scale=-1.0).then_inc(s["ex_ok"], 1)

                def shared(t):
                    r = rows(t)
                    act.wait_ge(s["gu"], t + 1)
                    if t:
                        act.wait_ge(s["shid"], t)
                    act.activation(sil[0:r], psum[0:r, 7 * (t % 2), 0:FE], ACT.Silu).then_inc(s["ssil"], 1)

                def shared_turned(t):
                    r = rows(t)
                    act.wait_ge(s["sht"], t + 1)
                    if t:
                        act.wait_ge(s["dn"], 2 * t)
                    act.copy(hidT[:, :, 0:r], psum[:, 3, 0:2 * P].rearrange("p (k n) -> p k n", k=2)[:, :,
                            0:r]).then_inc(s["ht_ok"], 1)

                def shared_out(t):
                    r = rows(t)
                    for n, done in enumerate(("out_lo", "out_hi")):
                        act.wait_ge(s["dn"], 2 * t + n + 1)
                        act.copy(ysh[0:r, t, n * 512:(n + 1) * 512], psum[0:r, 4 + n, :]).then_inc(s[done], 1)

                def silu(b):
                    act.wait_ge(s["gu"], b + 1 + NT)
                    act.activation(sil, psum[:, 0, 0:FE], ACT.Silu).then_inc(s["sil_ok"], 1)

                shared(0)
                for t in range(NT):
                    if t + 1 < NT:
                        shared(t + 1)
                    shared_turned(t)
                    if t + 1 < NT:
                        shared_out(t)
                take_rows_a(act, 0, 0)
                silu(0)
                take_rows_a(act, 1, 1)
                shared_out(NT - 1)
                act.wait_ge(s["gu"], NT)
                act.dma_start(gate2[:, 0, :], bc_row(mod_rows[0:1, 5 * D:], P)).then_inc(last_in, 16)
                act.dma_start(gate2[0:NS, 1, :], mod_sample(5)).then_inc(last_in, 16)
                act.dma_start(gfin, bc_row(io["g_final"].unsqueeze(0), P)).then_inc(last_in, 16)
                nb = trips(act)
                with act.Fori(0, TRIPS) as i:
                    with act.If(nb > i):
                        for u in range(3):
                            b = 3 * i + u
                            act.wait_ge(s["ht_ps"], b + 1)
                            act.copy(hidT, psum[:, 3, 0:2 * P].rearrange("p (k n) -> p k n", k=2)).then_inc(s["ht_ok"], 1)
                            silu(b + 1)
                            take_rows_a(act, b + 2, (u + 2) % 3)
                            act.wait_ge(s["now_ok"], 2 * b + 2)
                            act.wait_ge(s["dn"], 2 * b + 1 + DN0)
                            act.activation(out[:, u, 0:512], psum[:, 4, :], ACT.Copy, scale=now_gate[:,
                                    u:u + 1]).then_inc(s["out_lo"], 1)

            @block.vector
            def _(v):
                n_step = [0]

                def step(ins):
                    n_step[0] += 1
                    ins.then_inc(v_step, 1)
                    v.wait_ge(v_step, n_step[0])

                step(v.tensor_tensor_reduce(work[0:NS, 1, 0:W], attn[0:NS, NPT, :], attn[0:NS, NPT, :], 1.0, 0.0,
                                            ALU.mult, ALU.add, attn_sq[0:NS, NPT:]))
                step(v.tensor_scalar(ss[:, 0, 0:NPT], attn_sq[:, 0:NPT], 1.0 / W, EPS, ALU.mult, ALU.add))
                step(v.tensor_scalar(ss[0:NS, 0, NPT:], attn_sq[0:NS, NPT:], 1.0 / W, EPS, ALU.mult, ALU.add))
                v.sem_inc(s["ams"], 1)
                v.wait_ge(s["rs"], 2)
                v.wait_ge(s["bc_in"], 6 * 16)
                for a, r in ((0, P), (1, NS)):
                    step(v.tensor_scalar(bc[0:r, 2, a, :], bc[0:r, 2, a, :], 1.0, None, ALU.add))
                v.wait_ge(s["x_in"], 32)

                def residual(t):
                    r, a = rows(t), t // NPT
                    h = work[0:r, 1 + t % 2, :]
                    v.wait_ge(s["prod_a"], t + 1)
                    v.wait_ge(s["tc_ok"], t + 1)
                    if t >= 2:
                        v.wait_ge(s["h2_ps"], 2 * (t - 1))
                        v.wait_ge(h_out[t % 2], 16 * (t // 2))
                    step(v.tensor_tensor(h, psum[0:r, 2:4, :].rearrange("p a n -> p (a n)"), work[0:r, 0, :], ALU.add))
                    v.sem_inc(s["x2_ok"], 1)
                    step(v.tensor_tensor(h, h, bc[0:r, 0, a, :], ALU.mult))
                    step(v.tensor_tensor(x2[0:r, t, :], x2[0:r, t, :], h, ALU.add))
                    step(v.tensor_tensor_reduce(h, x2[0:r, t, :], x2[0:r, t, :], 1.0, 0.0, ALU.mult, ALU.add, ss[0:r, 0, t:t + 1]))
                    step(v.tensor_scalar(ss[0:r, 2, t:t + 1], ss[0:r, 0, t:t + 1], 1.0 / D, EPS, ALU.mult, ALU.add))
                    v.sem_inc(s["ms"], 1)
                    v.wait_ge(s["rs"], 3 + t)
                    step(v.scalar_tensor_tensor(h, x2[0:r, t, :], ss[0:r, 3, t:t + 1], bc[0:r, 2, a, :], ALU.mult, ALU.mult))
                    step(v.tensor_tensor(h, h, bc[0:r, 1, a, :], ALU.add))
                    v.sem_inc(s["h2_ok"], 1)

                for t in range(NT):
                    residual(t)

                def groups():
                    v.wait_ge(s["ex_ok"], 1)
                    v.wait_ge(s["small_in"], 32)
                    step(v.tensor_scalar(ra, scores, 1.0, None, ALU.add))
                    step(v.reciprocal(scores, ra))
                    step(v.tensor_tensor(sel, scores, bias[:, :].unsqueeze(1).broadcast_to([P, NT, NE]), ALU.add))
                    every = sel.rearrange("p t (g e) -> p (t g) e", g=NGRP)
                    raf, rbf = (x.rearrange("p t e -> p (t e)") for x in (ra, rb))
                    hi, lo = every[:, :, 0:8:2], every[:, :, 1:8:2]
                    h1 = raf[:, 0:160].rearrange("p (g e) -> p g e", e=4)
                    l1 = rbf[:, 0:160].rearrange("p (g e) -> p g e", e=4)
                    step(v.tensor_tensor(h1, hi, lo, ALU.max))
                    step(v.tensor_tensor(l1, hi, lo, ALU.min))
                    at = 160
                    for e in (2, 1):
                        n = 40 * e
                        h2_ = raf[:, at:at + n].rearrange("p (g e) -> p g e", e=e)
                        m2 = rbf[:, at:at + n].rearrange("p (g e) -> p g e", e=e)
                        l2 = merged[:, 0:n].rearrange("p (g e) -> p g e", e=e)
                        step(v.tensor_tensor(h2_, h1[:, :, 0:2 * e:2], h1[:, :, 1:2 * e:2], ALU.max))
                        step(v.tensor_tensor(m2, h1[:, :, 0:2 * e:2], h1[:, :, 1:2 * e:2], ALU.min))
                        step(v.tensor_tensor(l2, l1[:, :, 0:2 * e:2], l1[:, :, 1:2 * e:2], ALU.max))
                        step(v.tensor_tensor(m2, m2, l2, ALU.max))
                        h1, l1, at = h2_, m2, at + n
                    step(v.tensor_tensor(grp.rearrange("p t g -> p (t g)").unsqueeze(2), h1, l1, ALU.add))

                def choose():
                    other = grp.unsqueeze(2).broadcast_to([P, NT, NGRP, NGRP])
                    own = grp.unsqueeze(3).broadcast_to([P, NT, NGRP, NGRP])
                    a4, b4 = (x.rearrange("p t (g e) -> p t g e", g=NGRP) for x in (ra, rb))
                    low = cst[:, C_LOW:C_LOW + 64].unsqueeze(1).broadcast_to([P, NT, NE])
                    step(v.tensor_tensor(a4, other, own, ALU.is_gt))
                    step(v.tensor_tensor(b4, other, own, ALU.is_equal))
                    step(v.tensor_tensor(rb, rb, low, ALU.mult))
                    step(v.tensor_tensor(ra, ra, rb, ALU.add))
                    step(v.tensor_reduce(gneg, a4, AX.X, ALU.add))
                    step(v.tensor_scalar(gok, gneg, 3.5, None, ALU.is_lt))
                    step(v.tensor_scalar(gneg, gok, 1.0, 1e30, ALU.subtract, ALU.mult))
                    s4 = selm.rearrange("p t (g e) -> p t g e", g=NGRP)
                    step(v.tensor_tensor(s4, sel.rearrange("p t (g e) -> p t g e", g=NGRP),
                                         gok.unsqueeze(3).broadcast_to([P, NT, NGRP, GSZ]), ALU.mult))
                    step(v.tensor_tensor(s4, s4, gneg.unsqueeze(3).broadcast_to([P, NT, NGRP, GSZ]), ALU.add))
                    for t in range(NT):
                        step(v.max(top[:, t, :], selm[:, t, :]))
                        step(v.match_replace(rb[:, t, :], top[:, t, :], selm[:, t, :], -3e38))
                    step(v.tensor_scalar(mask, rb, -2e38, None, ALU.is_lt))
                    step(v.tensor_tensor(ra, scores, mask, ALU.mult))
                    step(v.tensor_reduce(gsum, ra, AX.X, ALU.add))
                    step(v.reciprocal(grec, gsum))
                    step(v.scalar_tensor_tensor(gate, ra, 2.5, grec.unsqueeze(2).broadcast_to([P, NT, NE]), ALU.mult, ALU.mult))
                    step(v.tensor_tensor(mask, mask, cst[:, C_VALID:C_VALID + NT].unsqueeze(2).broadcast_to([P, NT, NE]), ALU.mult))
                    step(v.tensor_copy(maskb, mask))
                    step(v.tensor_copy(trib, cst[:, C_TRI:C_TRI + P]))
                    step(v.tensor_copy(oneb, cst[:, C_ONE:C_ONE + P]))
                    v.sem_inc(s["mask_ok"], 1)

                def running(a, b, width, first):
                    step(v.tensor_copy(a[..., 32:], first))
                    for n in (1, 2, 4, 8, 16, 32):
                        step(v.tensor_tensor(b[..., 32:], a[..., 32:], a[..., 32 - n:width - n], ALU.add))
                        a, b = b, a
                    return a

                def fill_table():
                    total = running(run[0], run[1], 96, mask)
                    v.wait_ge(s["consts_ok"], NT)
                    step(v.tensor_tensor(table[:, :, :, 5], total[..., 32:], mask, ALU.subtract))
                    step(v.tensor_copy(table[:, :, :, 6], gate))
                    step(v.tensor_tensor(ra, gate, table[:, :, :, 6], ALU.subtract))
                    step(v.tensor_copy(table[:, :, :, 7], ra))
                    step(v.tensor_tensor(rb, ra, table[:, :, :, 7], ALU.subtract))
                    step(v.tensor_copy(table[:, :, :, 8], rb))
                    v.sem_inc(s["table_ok"], 1)

                def queues():
                    v.wait_ge(s["cnt_ps"], 1)
                    step(v.tensor_copy(cnt, psum[:, 2, NT * NE:(NT + 1) * NE]))
                    step(v.tensor_scalar(nblk, cnt, 0.0, None, ALU.is_gt))
                    for n in range(1, -(-NTOK // P)):
                        step(v.scalar_tensor_tensor(nblk, cnt, float(n * P), nblk, ALU.is_gt, ALU.add))
                    ends = running(erun[0], erun[1], 96, nblk)[..., 32:]
                    step(v.tensor_tensor(first, ends, nblk, ALU.subtract))
                    step(v.tensor_scalar(first, first, float(P), 1.0, ALU.mult, ALU.add))
                    step(v.tensor_tensor(ra, psum[:, 2, 0:NT * NE].rearrange("p (t e) -> p t e", t=NT),
                                         first.unsqueeze(1).broadcast_to([P, NT, NE]), ALU.add))
                    step(v.tensor_tensor(ra, ra, mask, ALU.mult))
                    step(v.tensor_scalar(gpos, ra, -1.0, None, ALU.add))
                    step(v.tensor_scalar(cnt[:, 0:TRIPS], cst[:, C_TRIP:C_TRIP + TRIPS], ends[:, NE - 1:NE], None, ALU.is_lt))
                    step(v.tensor_reduce(tripf, cnt[:, 0:TRIPS], AX.X, ALU.add))
                    step(v.tensor_scalar(lane, cst[:, C_IOTA:C_IOTA + 3], tripf, float(P), ALU.mult, ALU.mult))
                    step(v.tensor_scalar(blkf, cst[:, C_MOD:C_MOD + 1], tripf, cst[:, C_DIV:C_DIV + 1], ALU.mult, ALU.add))
                    step(v.tensor_scalar(cnt, ends, blkf, None, ALU.is_le))
                    step(v.tensor_reduce(blkf, cnt, AX.X, ALU.add))
                    step(v.tensor_scalar(blkf, blkf, float(NE - 1), None, ALU.min))
                    v.sem_inc(s["table_ok"], 1)
                    step(v.tensor_copy(n_trips, tripf[0:1, :]))
                    step(v.memset(fresh[:, 0:3], 1))
                    v.wait_ge(s["tab_ps"], 1)
                    step(v.tensor_copy(experts, psum[0:1, 2, 384:512]))
                    step(v.tensor_copy(expert_row, psum[0:1, 2, 384:512]))
                    step(v.tensor_tensor(fresh[:, 3:], expert_row[:, 3:], expert_row[:, 0:P - 3], ALU.not_equal))
                    v.sem_inc(s["tab_ok"], 1)

                def shared(t):
                    r = rows(t)
                    v.wait_ge(s["ssil"], t + 1)
                    if t:
                        v.wait_ge(s["sht"], t)
                    v.tensor_tensor(hid[0:r], psum[0:r, 7 * (t % 2), FE:], sil[0:r], ALU.mult).then_inc(s["shid"], 1)

                groups()
                shared(0)
                choose()
                shared(1)
                queues()
                shared(2)
                fill_table()
                for b in range(3):
                    who(v, b, b)
                shared(3)
                for b in range(3):
                    read_list(v, b, b)
                shared(4)
                v.wait_ge(s["list_mm"], 1)
                who(v, 3, 0)

                def place(u):
                    v.tensor_scalar(row[:, u, :], got[:, u, 1:2], float(TOPK * OUTSIDE), None,
                            ALU.add).then_inc(s["now_ok"], 1)

                def multiply(b):
                    v.wait_ge(s["sil_ok"], b + 1)
                    v.tensor_tensor(hid, psum[:, 0, FE:], sil, ALU.mult).then_inc(s["hid_ok"], 1)

                take_rows_v(v, 0, 0)
                multiply(0)
                take_rows_v(v, 1, 1)
                nb = trips(v)
                with v.Fori(0, TRIPS) as i:
                    with v.If(nb > i):
                        for u in range(3):
                            b = 3 * i + u
                            with v.If(i > 0):
                                v.wait_ge(scat[u], 16 * i)
                                place(u)
                            with v.If(i < 1):
                                place(u)
                            v.tensor_copy(now_gate[:, u:u + 1], got[:, u, 2:3]).then_inc(s["now_ok"], 1)
                            v.wait_ge(s["now_ok"], 2 * b + 2)
                            read_list(v, b + 3, u)
                            v.wait_ge(s["list_mm"], b + 2)
                            who(v, b + 4, (u + 1) % 3)
                            multiply(b + 1)
                            take_rows_v(v, b + 2, (u + 2) % 3)
                            v.wait_ge(s["dn"], 2 * b + 2 + DN0)
                            v.tensor_scalar(out[:, u, 512:], psum[:, 5, :], now_gate[:, u:u + 1], None,
                                    ALU.mult).then_inc(s["out_hi"], 1)

            @block.tensor
            def _(pe):

                def turn_attn(t):
                    r = rows(t)
                    pe.wait_ge(s["an_ok"], t + 1)
                    if t:
                        pe.wait_ge(s["aT_ok"], t)
                    for c in range(WC):
                        last = pe.transpose(psum[:, 0, c * P:c * P + r], attn[0:r, t, c * P:(c + 1) * P], ident[0:r, 0:r])
                    last.then_inc(s["aT_ps"], 1)

                def conv_product(t, halves=(0, 1)):
                    r = rows(t)
                    if t:
                        pe.wait_ge(s["tc_ok"], t)
                    else:
                        pe.wait_ge(wout_conv_in, 16)
                    for n in halves:
                        for c in range(WC):
                            last = pe.matmul(psum[0:r, 4 + n, :], convg[:, c, t * P:t * P + r],
                                             wout[:, WC + c, n * 512:(n + 1) * 512], start=(c == 0), stop=(c == WC - 1))
                    if halves[-1] == 1:
                        last.then_inc(s["prod_c"], 1)

                def attn_product(t):
                    r = rows(t)
                    if t:
                        pe.wait_ge(s["x2_ok"], t)
                    pe.wait_ge(s["aT_ok"], t + 1)
                    if t == 0:
                        pe.wait_ge(wout_attn_in, 16)
                    for n in range(2):
                        for c in range(WC):
                            last = pe.matmul(psum[0:r, 2 + n, :], aT[:, t % 2, c, 0:r],
                                             wout[:, c, n * 512:(n + 1) * 512], start=(c == 0), stop=(c == WC - 1))
                    last.then_inc(s["prod_a"], 1)

                def route(m):
                    r = rows(m)
                    pe.wait_ge(s["h2_ok"], m + 1)
                    for half in range(2):
                        if m:
                            pe.wait_ge(s["h2_sb"], 2 * m - 1 + half)
                        for k in range(4):
                            kk = 4 * half + k
                            last = pe.transpose(psum[:, 6 + half, k * P:k * P + r],
                                                work[0:r, 1 + m % 2, kk::KC], ident[0:r, 0:r])
                        last.then_inc(s["h2_ps"], 1)
                    pe.wait_ge(s["h2_sb"], 2 * m + 2)
                    if m == 0:
                        pe.wait_ge(s["small_in"], 32)
                    for k in range(KC):
                        last = pe.matmul(psum[0:r, 1, m * NE:(m + 1) * NE], h2T[:, k, m * P:m * P + r], wr[:, k, :],
                                         start=(k == 0), stop=(k == KC - 1))
                    last.then_inc(s["logit"], 1)

                for t in range(NT):
                    if t == 0:
                        conv_product(t, (0,))
                    turn_attn(t)
                    conv_product(t, (0, 1) if t else (1,))
                    attn_product(t)
                    if t >= 2:
                        route(t - 2)
                route(NT - 2)

                lhs = lambda t: lambda k: h2T[:, k, t * P:t * P + rows(t)]
                pe.wait_ge(shared_in, 48)
                pe.wait_ge(s["aT_ok"], NT)
                gate_up(pe, 0, P, lhs(0), wslot[0], s["gu"])
                route(NT - 1)
                for t in range(NT):
                    r = rows(t)
                    if t + 1 < NT:
                        if t:
                            pe.wait_ge(s["shid"], t)
                        gate_up(pe, 7 * ((t + 1) % 2), rows(t + 1), lhs(t + 1), wslot[0], s["gu"])
                    if t == 1:
                        pe.wait_ge(s["mask_ok"], 1)
                        for a in range(NT):
                            for c in range(a + 1):
                                pe.matmul(psum[:, 2, a * NE:(a + 1) * NE], trib if c == a else oneb, maskb[:, c, :],
                                          start=(c == 0), stop=(c == a))
                        for c in range(NT):
                            last = pe.matmul(psum[:, 2, NT * NE:(NT + 1) * NE], oneb, maskb[:, c, :],
                                             start=(c == 0), stop=(c == NT - 1))
                        last.then_inc(s["cnt_ps"], 1)
                    if t == 2:
                        pe.wait_ge(s["table_ok"], 1)
                        pe.transpose(psum[0:1, 2, 384:512], blkf, ident).then_inc(s["tab_ps"], 1)
                    if t == 3:
                        for b in range(3):
                            fill_list(pe, b, b, first=(b == 0))
                    pe.wait_ge(s["shid"], t + 1)
                    turn_hidden(pe, r, s["sht"])
                    if t + 1 < NT:
                        pe.wait_ge(s["ht_ok"], t + 1)
                        down(pe, r, wslot[0], s["dn"], out_read(pe, t) if t else None)
                pe.wait_ge(s["tab_ok"], 1)
                pe.wait_ge(gath[0], 16)
                turn_rows(pe, 0)
                nb = trips(pe)
                with pe.Fori(0, TRIPS) as i:
                    with pe.If(nb > i):
                        for u in range(3):
                            b = 3 * i + u
                            n1 = (u + 1) % 3
                            pe.wait_ge(w_in[u], 48 * i + 48)
                            pe.wait_ge(s["xt_a"], b + 1)
                            pe.wait_ge(s["xt_v"], b + 1)
                            gate_up(pe, 0, P, lambda k: xT[:, u, k, :], wslot[n1], s["gu"])
                            pe.wait_ge(gath[n1], 16 * i + (16 if u < 2 else 32))
                            turn_rows(pe, n1)
                            pe.wait_ge(s["ht_ok"], b + NT)
                            down(pe, P, wslot[u], s["dn"], out_read(pe, b - 1 + NT))
                            pe.wait_ge(s["hid_ok"], b + 1)
                            turn_hidden(pe, P, s["ht_ps"])
                            fill_list(pe, b + 3, u)
                blocks = 3 * nb
                pe.wait_ge(s["ht_ok"], blocks + NT)
                pe.transpose(psum[:, 3, 0:P], ident, ident).then_inc(s["gu"], 1)
                pe.wait_ge(s["xt_a"], blocks + 1)
                pe.wait_ge(s["xt_v"], blocks + 1)
                pe.wait_ge(gath[1], 16 * nb + 16)
                turn_rows(pe, 1)
                down(pe, P, wslot[0], s["dn"], out_read(pe, blocks - 1 + NT))
        stage_4(x2, ysh, gate2, gfin, room[:, 3 * D:3 * D + 3 * NT].rearrange("p (a t) -> p a t", a=3), work)
        st.close()

    def stage_4(x2, ysh, gate2, gfin, ss, work):
        ring = stream[:, 0:3 * TOPK * D].rearrange("p (s k n) -> p s k n", s=3, k=TOPK)
        H = TOPK // 2
        order = [NPT, *range(NPT)]
        two_ok, sums, sum_read, y_ok, ms, rs = (sem(f"s4_{n}") for n in ("two_ok", "sums", "sum_read", "y_ok", "ms", "rs"))
        first_in = [sem(f"s4_first{i}") for i in range(3)]
        second_in = [sem(f"s4_second{i}") for i in range(3)]
        y_out = [sem(f"s4_y_out{i}") for i in range(2)]
        v_step = sem("s4_v_step")
        rows_of = expert_rows.rearrange("(n k) d -> n k d", k=TOPK)

        with nc.Block() as block:
            @block.sync
            def _(sp):
                for j, t in enumerate(order):
                    r = rows(t)
                    if j >= 3:
                        sp.wait_ge(y_ok, j - 2)
                    for a, signal in ((0, first_in), (H, second_in)):
                        sp.dma_start(ring[0:r, j % 3, a:a + H, :],
                                     rows_of[t * P:t * P + r, a:a + H, :]).then_inc(signal[j % 3], 16)
                sp.wait_ge(stored, 16 * n_stores[0])

            @block.gpsimd
            def _(pool):
                def last_two(j):
                    r = rows(order[j])
                    pool.wait_ge(second_in[j % 3], 16 * (j // 3 + 1))
                    a, b = ring[0:r, j % 3, TOPK - 2, :], ring[0:r, j % 3, TOPK - 1, :]
                    pool.tensor_tensor(a, a, b, ALU.add).then_inc(two_ok, 1)

                last_two(0)
                for j, t in enumerate(order):
                    r = rows(t)
                    if j + 1 < NT:
                        last_two(j + 1)
                    pool.wait_ge(ms, j + 1)
                    pool.tensor_tensor(ss[0:r, 2, t:t + 1], ss[0:r, 1, t:t + 1], cst[0:r, C_POW:C_POW + 1],
                            ALU.pow).then_inc(rs, 1)

            @block.scalar
            def _(act):
                for j, t in enumerate(order):
                    act.wait_ge(y_ok, j + 1)
                    dst = (io["y_prompt"][0, t * P:(t + 1) * P, :] if t < NPT else
                           io["y_sample"].rearrange("b t n -> (b t) n"))
                    act.dma_start(dst, work[0:rows(t), j % 2, :]).then_inc(y_out[j % 2], 16)
                act.wait_ge(y_out[0], 3 * 16)
                act.wait_ge(y_out[1], 2 * 16)

            @block.tensor
            def _(pe):
                for j, t in enumerate(order):
                    r = rows(t)
                    pe.wait_ge(first_in[j % 3], 16 * (j // 3 + 1))
                    if j >= 2:
                        pe.wait_ge(sum_read, j - 1)
                    for n in range(2):
                        cols = slice(n * 512, (n + 1) * 512)
                        pe.matmul(psum[0:r, 2 * (j % 2) + n, :], ident[0:r, 0:r], ysh[0:r, t, cols], start=True, stop=False)
                        for k in range(H):
                            last = pe.matmul(psum[0:r, 2 * (j % 2) + n, :], ident[0:r, 0:r], ring[0:r, j % 3, k, cols],
                                             start=False, stop=(k == H - 1))
                    last.then_inc(sums, 1)

            @block.vector
            def _(v):
                n_step = [0]

                def step(ins):
                    n_step[0] += 1
                    ins.then_inc(v_step, 1)
                    v.wait_ge(v_step, n_step[0])

                for j, t in enumerate(order):
                    r, b = rows(t), 2 * (j % 2)
                    y = work[0:r, j % 2, :]
                    v.wait_ge(second_in[j % 3], 16 * (j // 3 + 1))
                    if j >= 2:
                        v.wait_ge(y_out[j % 2], 16 * (j // 2))
                    step(v.tensor_tensor(y, ring[0:r, j % 3, H, :], ring[0:r, j % 3, H + 1, :], ALU.add))
                    for k in range(H + 2, TOPK - 1):
                        if k == TOPK - 2:
                            v.wait_ge(two_ok, j + 1)
                        step(v.tensor_tensor(y, y, ring[0:r, j % 3, k, :], ALU.add))
                    v.wait_ge(sums, j + 1)
                    step(v.tensor_tensor(y, psum[0:r, b:b + 2, :].rearrange("p a n -> p (a n)"), y, ALU.add))
                    v.sem_inc(sum_read, 1)
                    if j == 0:
                        v.wait_ge(last_in, 48)
                    step(v.tensor_tensor(y, y, gate2[0:r, t // NPT, :], ALU.mult))
                    step(v.tensor_tensor(x2[0:r, t, :], x2[0:r, t, :], y, ALU.add))
                    step(v.tensor_tensor_reduce(y, x2[0:r, t, :], x2[0:r, t, :], 1.0, 0.0, ALU.mult, ALU.add, ss[0:r, 0, t:t + 1]))
                    step(v.tensor_scalar(ss[0:r, 1, t:t + 1], ss[0:r, 0, t:t + 1], 1.0 / D, EPS, ALU.mult, ALU.add))
                    v.sem_inc(ms, 1)
                    v.wait_ge(rs, j + 1)
                    v.scalar_tensor_tensor(y, x2[0:r, t, :], ss[0:r, 2, t:t + 1], gfin[0:r], ALU.mult,
                            ALU.mult).then_inc(y_ok, 1)

    kv = ExitStack()
    keeps = {n: kv.enter_context(nc.sbuf_tensor("sb_" + n, [P, NT, W], F32)) for n in "kv"}
    stage_1()
    stage_2()
    kv.close()
    stage_3()
    ctx.close()


_INS = ['x_prompt', 'x_sample', 'c_prompt', 'c_sample', 'cache_k', 'cache_v', 'state_conv', 'w_ada', 'b_ada',
        'w_in', 'conv_w', 'g_attn_out', 'g_conv_out', 'w_out', 'w_router', 'router_bias', 'w_exp_gate',
        'w_exp_up', 'w_exp_down', 'w_sh_gate', 'w_sh_up', 'w_sh_down', 'g_final']
_OUTS = {'y_prompt': (1, SEQ, D), 'y_sample': (DEC_B, DEC_T, D),
         'k_prompt': (1, 1, SEQ, HEADS, HD), 'v_prompt': (1, 1, SEQ, HEADS, HD), 'conv_prompt': (1, 1, 2, W),
         'k_sample': (1, DEC_B, DEC_T, HEADS, HD), 'v_sample': (1, DEC_B, DEC_T, HEADS, HD),
         'conv_sample': (1, DEC_B, 2, W)}


def build(nc, shapes):
    io = {n: nc.dram_tensor(n, s, F32, kind="ExternalInput").ap() for n, s in shapes.items()}
    io |= {n: nc.dram_tensor(n, s, F32, kind="ExternalOutput").ap() for n, s in _OUTS.items()}
    layer(nc, io)


def kernel(**inputs):
    import concourse.bacc as bacc
    from concourse.bass_utils import run_bass_kernel_spmd

    arrays = {n: np.ascontiguousarray(inputs[n]) for n in _INS}
    for n, a in zip(("cst", "masks", "rope"), constants()):
        arrays[n] = a
    nc = bacc.Bacc("TRN2", target_bir_lowering=False, num_devices=1)
    build(nc, {n: a.shape for n, a in arrays.items()})
    r = run_bass_kernel_spmd(nc, [arrays], core_ids=[0])
    return tuple(r.results[0][n] for n in _OUTS)
```
